# Optimizing a Trainium2 kernel written in Bass

```python
import math
import jax, jax.numpy as jnp
from jax import lax
import numpy as np

D_MODEL = 1024
BATCH = 1
SEQ = 512
DEPTH = 2

CTX_LEN = 256
GRID_W = 64
N_EVEN = (DEPTH + 1) // 2
N_ODD = DEPTH // 2
N_MOD = 9
D_FF = 2816
FFN_RES = 0.5
EPS = 1e-6
Q_BLOCK = 128
ROPE_THETA = 10000.0

CONV_CH = 512
CONV_K = 31
MLA_HEADS = 8
MLA_NOPE = 64
MLA_ROPE = 32
MLA_V = 64
Q_LORA = 384
KV_LORA = 256
MLA_SCALE = (MLA_NOPE + MLA_ROPE) ** -0.5
GQA_HEADS = 8
GQA_KV_HEADS = 2
GQA_GROUP = GQA_HEADS // GQA_KV_HEADS
GQA_HD = 64
GQA_SCALE = GQA_HD ** -0.5
FNET_GROUPS = 4
FNET_CH = 128

EVEN_IN = 2 * CONV_CH + Q_LORA + KV_LORA + MLA_ROPE
EVEN_MIX = CONV_CH + MLA_HEADS * MLA_V
ODD_Q = GQA_HEADS * GQA_HD
ODD_KV = GQA_KV_HEADS * GQA_HD
ODD_F = FNET_GROUPS * FNET_CH
ODD_IN = ODD_Q + 2 * ODD_KV + ODD_F
ODD_MIX = ODD_Q + ODD_F

kernel_name = 'hybrid_conv_mla_gqa_fnet_diffusion_trunk'

def rmsnorm(x, g):
    xf = x.astype(jnp.float32)
    y = xf * lax.rsqrt(jnp.mean(xf * xf, axis=-1, keepdims=True) + EPS)
    return (y * g.astype(jnp.float32)).astype(x.dtype)

def layernorm(x, g, b):
    xf = x.astype(jnp.float32)
    mu = jnp.mean(xf, axis=-1, keepdims=True)
    var = jnp.mean(jnp.square(xf - mu), axis=-1, keepdims=True)
    y = (xf - mu) * lax.rsqrt(var + EPS)
    return (y * g.astype(jnp.float32) + b.astype(jnp.float32)).astype(x.dtype)

def adaln(x, g, shift, scale):
    return rmsnorm(x, g) * (1.0 + scale) + shift

def swiglu(h, w_gate, w_up, w_down):
    return (jax.nn.silu(h @ w_gate) * (h @ w_up)) @ w_down

def ffn_sublayer(x, mod, k, g_pre, g_post, w_gate, w_up, w_down):
    h = adaln(x, g_pre, mod[:, :, 3 * k], mod[:, :, 3 * k + 1])
    y = swiglu(h, w_gate, w_up, w_down)
    return x + FFN_RES * mod[:, :, 3 * k + 2] * rmsnorm(y, g_post)

def rope_tables(row, col, rot_dim, dtype):
    nf = rot_dim // 4
    inv = ROPE_THETA ** (-jnp.arange(nf, dtype=jnp.float32) / nf)
    ang = jnp.concatenate([row[:, None].astype(jnp.float32) * inv,
                           col[:, None].astype(jnp.float32) * inv], axis=-1)
    return jnp.cos(ang).astype(dtype), jnp.sin(ang).astype(dtype)

def rope_2d(x, cos, sin):
    nf = x.shape[-1] // 4
    xp = x.reshape(x.shape[:-1] + (2, 2, nf))
    x1, x2 = xp[..., 0, :], xp[..., 1, :]
    c = cos.reshape(cos.shape[0], 1, 2, nf)
    s = sin.reshape(sin.shape[0], 1, 2, nf)
    return jnp.stack([x1 * c - x2 * s, x1 * s + x2 * c], axis=-2).reshape(x.shape)

def block_attention(q, k, v, scale):
    B, Lq, Hk, G, dk = q.shape
    nblk = Lq // Q_BLOCK
    qb = jnp.moveaxis(q.reshape(B, nblk, Q_BLOCK, Hk, G, dk), 1, 0)

    def one_block(qi):
        s = jnp.einsum('bqhgd,bkhd->bhgqk', qi, k, preferred_element_type=jnp.float32) * scale
        p = jax.nn.softmax(s, axis=-1).astype(v.dtype)
        return jnp.einsum('bhgqk,bkhe->bqhge', p, v)

    o = lax.map(one_block, qb)
    return jnp.moveaxis(o, 0, 1).reshape(B, Lq, Hk, G, v.shape[-1])

def depthwise_conv(u, w, b):
    y = lax.conv_general_dilated(u, w[:, None, :].astype(u.dtype), window_strides=(1,),
                                 padding=[(CONV_K // 2, CONV_K // 2)],
                                 dimension_numbers=('NWC', 'WIO', 'NWC'),
                                 feature_group_count=u.shape[-1])
    return y + b

def conformer_conv(val, gate, conv_w, conv_b, ln_g, ln_b):
    u = val * jax.nn.sigmoid(gate)
    u = depthwise_conv(u, conv_w, conv_b)
    u = layernorm(u, ln_g, ln_b)
    return jax.nn.silu(u)

def fourier_mix(f):
    B, L, _ = f.shape
    fg = f.reshape(B, L, FNET_GROUPS, FNET_CH).astype(jnp.float32)
    out = jnp.real(jnp.fft.fft2(fg, axes=(1, 3), norm='ortho'))
    return out.reshape(B, L, ODD_F).astype(f.dtype)

def mla_queries(cq, g_cq, w_uq, rot):
    B, L, _ = cq.shape
    q = (rmsnorm(cq, g_cq) @ w_uq).reshape(B, L, MLA_HEADS, MLA_NOPE + MLA_ROPE)
    if rot is not None:
        q = jnp.concatenate([q[..., :MLA_NOPE], rope_2d(q[..., MLA_NOPE:], *rot)], axis=-1)
    return q[:, :, :, None, :]

def mla_keys_values(ckv, kpe, g_ckv, w_ukv, rot):
    B, L, _ = ckv.shape
    kv = (rmsnorm(ckv, g_ckv) @ w_ukv).reshape(B, L, MLA_HEADS, MLA_NOPE + MLA_V)
    kpe = kpe[:, :, None, :]
    if rot is not None:
        kpe = rope_2d(kpe, *rot)
    k = jnp.concatenate([kv[..., :MLA_NOPE],
                         jnp.broadcast_to(kpe, (B, L, MLA_HEADS, MLA_ROPE))], axis=-1)
    return k, kv[..., MLA_NOPE:]

def even_mixer(h, hc, w_in, conv_w, conv_b, ln_g, ln_b, g_cq, w_uq, g_ckv, w_ukv, w_out,
               rot, need_ctx):
    B, L, _ = h.shape
    Lc = hc.shape[1]
    a_cols = 2 * CONV_CH
    splits = [CONV_CH, a_cols, a_cols + Q_LORA, a_cols + Q_LORA + KV_LORA]
    a_val, a_gate, cq, ckv, kpe = jnp.split(h @ w_in, splits, axis=-1)
    cq_c, ckv_c, kpe_c = jnp.split(hc @ w_in[:, a_cols:], [Q_LORA, Q_LORA + KV_LORA], axis=-1)
    k_c, v_c = mla_keys_values(ckv_c, kpe_c, g_ckv, w_ukv, None)
    k, v = mla_keys_values(ckv, kpe, g_ckv, w_ukv, rot)
    q = mla_queries(cq, g_cq, w_uq, rot)
    o_b = block_attention(q, jnp.concatenate([k_c, k], axis=1), jnp.concatenate([v_c, v], axis=1),
                          MLA_SCALE).reshape(B, L, MLA_HEADS * MLA_V)
    o_a = conformer_conv(a_val, a_gate, conv_w, conv_b, ln_g, ln_b)
    y = jnp.concatenate([o_a, o_b], axis=-1) @ w_out
    if not need_ctx:
        return y, None
    a_val_c, a_gate_c = jnp.split(hc @ w_in[:, :a_cols], 2, axis=-1)
    q_c = mla_queries(cq_c, g_cq, w_uq, None)
    o_bc = block_attention(q_c, k_c, v_c, MLA_SCALE).reshape(B, Lc, MLA_HEADS * MLA_V)
    o_ac = conformer_conv(a_val_c, a_gate_c, conv_w, conv_b, ln_g, ln_b)
    y_c = jnp.concatenate([o_ac, o_bc], axis=-1) @ w_out
    return y, y_c

def odd_mixer(h, hc, w_in, g_qn, g_kn, w_out, rot, need_ctx):
    B, L, _ = h.shape
    Lc = hc.shape[1]
    kv_lo, kv_hi = ODD_Q, ODD_Q + 2 * ODD_KV
    q, k, v, f = jnp.split(h @ w_in, [ODD_Q, ODD_Q + ODD_KV, kv_hi], axis=-1)
    q = rope_2d(rmsnorm(q.reshape(B, L, GQA_HEADS, GQA_HD), g_qn), *rot)
    k = rope_2d(rmsnorm(k.reshape(B, L, GQA_KV_HEADS, GQA_HD), g_kn), *rot)
    v = v.reshape(B, L, GQA_KV_HEADS, GQA_HD)
    k_c, v_c = jnp.split(hc @ w_in[:, kv_lo:kv_hi], 2, axis=-1)
    k_c = rmsnorm(k_c.reshape(B, Lc, GQA_KV_HEADS, GQA_HD), g_kn)
    v_c = v_c.reshape(B, Lc, GQA_KV_HEADS, GQA_HD)
    o_c = block_attention(q.reshape(B, L, GQA_KV_HEADS, GQA_GROUP, GQA_HD),
                          jnp.concatenate([k_c, k], axis=1), jnp.concatenate([v_c, v], axis=1),
                          GQA_SCALE).reshape(B, L, ODD_Q)
    o_d = fourier_mix(f)
    y = jnp.concatenate([o_c, o_d], axis=-1) @ w_out
    if not need_ctx:
        return y, None
    q_c = rmsnorm((hc @ w_in[:, :ODD_Q]).reshape(B, Lc, GQA_HEADS, GQA_HD), g_qn)
    o_cc = block_attention(q_c.reshape(B, Lc, GQA_KV_HEADS, GQA_GROUP, GQA_HD), k_c, v_c,
                           GQA_SCALE).reshape(B, Lc, ODD_Q)
    o_dc = fourier_mix(hc @ w_in[:, kv_hi:])
    y_c = jnp.concatenate([o_cc, o_dc], axis=-1) @ w_out
    return y, y_c

def setup_inputs(seed: int = 0) -> dict:
    key = jax.random.key(seed)
    keys = jax.random.split(key, 32)
    ks = iter([keys[i] for i in range(32)])
    D = D_MODEL

    def nrm(shape, scale):
        return jax.random.normal(next(ks), shape, jnp.float32) * scale

    def gain(shape):
        return 1.0 + nrm(shape, 0.02)

    return {
        'x': nrm((BATCH, SEQ, D), 1.0),
        'c': nrm((BATCH, D), 1.0),
        'ctx': nrm((BATCH, CTX_LEN, D), 1.0),
        'c_ctx': nrm((D,), 1.0),
        'w_mod': nrm((DEPTH, D, N_MOD * D), 0.5 * D ** -0.5),
        'b_mod': nrm((DEPTH, N_MOD * D), 0.02),
        'g_pre': gain((DEPTH, 3, D)),
        'g_post': gain((DEPTH, 3, D)),
        'ffn_w_gate': nrm((DEPTH, 2, D, D_FF), D ** -0.5),
        'ffn_w_up': nrm((DEPTH, 2, D, D_FF), D ** -0.5),
        'ffn_w_down': nrm((DEPTH, 2, D_FF, D), D_FF ** -0.5),
        'ev_w_in': nrm((N_EVEN, D, EVEN_IN), D ** -0.5),
        'ev_conv_w': nrm((N_EVEN, CONV_K, CONV_CH), CONV_K ** -0.5),
        'ev_conv_b': nrm((N_EVEN, CONV_CH), 0.02),
        'ev_ln_g': gain((N_EVEN, CONV_CH)),
        'ev_ln_b': nrm((N_EVEN, CONV_CH), 0.02),
        'ev_g_cq': gain((N_EVEN, Q_LORA)),
        'ev_w_uq': nrm((N_EVEN, Q_LORA, MLA_HEADS * (MLA_NOPE + MLA_ROPE)), Q_LORA ** -0.5),
        'ev_g_ckv': gain((N_EVEN, KV_LORA)),
        'ev_w_ukv': nrm((N_EVEN, KV_LORA, MLA_HEADS * (MLA_NOPE + MLA_V)), KV_LORA ** -0.5),
        'ev_w_out': nrm((N_EVEN, EVEN_MIX, D), EVEN_MIX ** -0.5),
        'od_w_in': nrm((N_ODD, D, ODD_IN), D ** -0.5),
        'od_g_qn': gain((N_ODD, GQA_HD)),
        'od_g_kn': gain((N_ODD, GQA_HD)),
        'od_w_out': nrm((N_ODD, ODD_MIX, D), ODD_MIX ** -0.5),
    }

def reference(x, c, ctx, c_ctx, w_mod, b_mod, g_pre, g_post, ffn_w_gate, ffn_w_up, ffn_w_down,
              ev_w_in, ev_conv_w, ev_conv_b, ev_ln_g, ev_ln_b, ev_g_cq, ev_w_uq, ev_g_ckv,
              ev_w_ukv, ev_w_out, od_w_in, od_g_qn, od_g_kn, od_w_out):
    B, L, D = x.shape
    ROWS = L // GRID_W
    row = jnp.repeat(jnp.arange(ROWS), GRID_W)
    col = jnp.tile(jnp.arange(GRID_W), ROWS)
    rot_mla = rope_tables(row, col, MLA_ROPE, x.dtype)
    rot_gqa = rope_tables(row, col, GQA_HD, x.dtype)
    sc = jax.nn.silu(c)
    scc = jax.nn.silu(c_ctx)
    xc = ctx
    for i in range(DEPTH):
        need_ctx = i < DEPTH - 1
        mod = (sc @ w_mod[i] + b_mod[i]).reshape(B, 1, N_MOD, D)
        modc = (scc @ w_mod[i] + b_mod[i]).reshape(1, 1, N_MOD, D)
        x = ffn_sublayer(x, mod, 0, g_pre[i, 0], g_post[i, 0],
                         ffn_w_gate[i, 0], ffn_w_up[i, 0], ffn_w_down[i, 0])
        xc = ffn_sublayer(xc, modc, 0, g_pre[i, 0], g_post[i, 0],
                          ffn_w_gate[i, 0], ffn_w_up[i, 0], ffn_w_down[i, 0])
        h = adaln(x, g_pre[i, 1], mod[:, :, 3], mod[:, :, 4])
        hc = adaln(xc, g_pre[i, 1], modc[:, :, 3], modc[:, :, 4])
        j = i // 2
        if i % 2 == 0:
            y, y_c = even_mixer(h, hc, ev_w_in[j], ev_conv_w[j], ev_conv_b[j], ev_ln_g[j], ev_ln_b[j],
                                ev_g_cq[j], ev_w_uq[j], ev_g_ckv[j], ev_w_ukv[j], ev_w_out[j],
                                rot_mla, need_ctx)
        else:
            y, y_c = odd_mixer(h, hc, od_w_in[j], od_g_qn[j], od_g_kn[j], od_w_out[j],
                               rot_gqa, need_ctx)
        x = x + mod[:, :, 5] * rmsnorm(y, g_post[i, 1])
        x = ffn_sublayer(x, mod, 2, g_pre[i, 2], g_post[i, 2],
                         ffn_w_gate[i, 1], ffn_w_up[i, 1], ffn_w_down[i, 1])
        if need_ctx:
            xc = xc + modc[:, :, 5] * rmsnorm(y_c, g_post[i, 1])
            xc = ffn_sublayer(xc, modc, 2, g_pre[i, 2], g_post[i, 2],
                              ffn_w_gate[i, 1], ffn_w_up[i, 1], ffn_w_down[i, 1])
    return x


_drawn_inputs = setup_inputs


def setup_inputs(seed=0):
    import zlib

    import numpy as np

    out = dict(_drawn_inputs(seed))
    spreads = {}
    factors = {'g_pre': 4.832,
     'g_post': 5.656,
     'ev_conv_b': 5.846,
     'ev_ln_g': 8.0,
     'ev_ln_b': 8.0,
     'ev_g_cq': 8.0,
     'ev_g_ckv': 8.0,
     'od_g_qn': 8.0,
     'od_g_kn': 8.0}
    for name, (base, spread) in spreads.items():
        noise = np.random.default_rng([zlib.crc32(name.encode()), seed]).standard_normal(out[name].shape)
        drawn = base * np.exp(spread * noise) if base else spread * noise
        out[name] = __import__('jax').numpy.asarray(drawn.astype(out[name].dtype))
    for name, factor in factors.items():
        out[name] = (out[name] * factor).astype(out[name].dtype)
    return out
```

```python
from contextlib import ExitStack

import numpy as np

import concourse.bass as bass
from concourse import mybir

F32 = mybir.dt.float32
F32R = mybir.dt.float32r
ACT = mybir.ActivationFunctionType
ALU = mybir.AluOpType
AX_X = mybir.AxisListType.X

P = 128
D = 1024
KD = D // P
CTX, SEQ = 256, 512
TOK = CTX + SEQ
EPS = 1e-6
D_FF = 2816
FT = D_FF // P
STEPS = FT // 2
CHUNK = 1024
RAWS, SLOTS = 2, 4
MOD_SLOTS = 2
UNITS = 18
SEG_C, SEG_X = (0, CTX, 1), (CTX, SEQ, 0)
ALL, XONLY = (SEG_C, SEG_X), (SEG_X,)

CONV_CH, CONV_K = 512, 31
KC = CONV_CH // P
HALO = CONV_K // 2
GAPPED = CTX + HALO + SEQ
PADDED = GAPPED + 2 * HALO
HEADS, NOPE, ROPE, VD = 8, 64, 32, 64
QK = NOPE + ROPE
Q_LORA, KV_LORA = 384, 256
KQ, KKV = Q_LORA // P, KV_LORA // P
MLA_SCALE = QK ** -0.5
GQA_HEADS, GQA_KV, HD = 8, 2, 64
GQA_SCALE = HD ** -0.5
GRID_W = 64
ROPE_THETA = 10000.0

FFN_CHUNKS = 3 * FT
E_IN, E_V, E_PAIR, E_OUT = 0, 14, 16, 24
E_CHUNKS = 32
O_IN, O_DFT, O_OUT = 0, 10, 14
O_CHUNKS = 22
BASE = {0: 0, 1: FFN_CHUNKS, 2: FFN_CHUNKS + E_CHUNKS, 3: 2 * FFN_CHUNKS + E_CHUNKS,
        4: 3 * FFN_CHUNKS + E_CHUNKS, 5: 3 * FFN_CHUNKS + E_CHUNKS + O_CHUNKS}

V_GPRE, V_GPOST, V_C, V_CCTX, V_CONVB, V_LNG, V_LNB, V_GCQ = 0, 48, 96, 104, 112, 116, 120, 124
V_CONVW, V_GCKV, V_GQN, V_GKN = 128, 252, 254, 255

C_ID, C_N1024, C_N384, C_N256, C_M512, C_N512, C_P96, C_B64, C_P128, C_DFT = (P * i for i in range(10))
C_MROPE = C_DFT + 2 * P
C_GROPE = C_MROPE + 2 * SEQ
C_END = C_GROPE + 2 * SEQ


def rope_rows(rot_dim):
    nf = rot_dim // 4
    inv = ROPE_THETA ** (-np.arange(nf, dtype=np.float32) / np.float32(nf))
    row = np.repeat(np.arange(SEQ // GRID_W), GRID_W).astype(np.float32)
    col = np.tile(np.arange(GRID_W), SEQ // GRID_W).astype(np.float32)
    cos, sin, swap = [], [], []
    for axis, place in enumerate((row, col)):
        for half in range(2):
            for f in range(nf):
                ang = place * inv[f]
                cos.append(np.cos(ang))
                sin.append(np.sin(ang))
                d = (axis * 2 + half) * nf + f
                swap.append((d, (axis * 2 + 1 - half) * nf + f, 1.0 if half else -1.0))
    return np.array(cos, np.float32), np.array(sin, np.float32), swap


def constant_array():
    k = np.zeros((P, C_END), np.float32)
    k[:, C_ID:C_ID + P] = np.eye(P)
    for at, v in ((C_N1024, -0.5 / D), (C_N384, -0.5 / Q_LORA), (C_N256, -0.5 / KV_LORA),
                  (C_M512, 1.0 / CONV_CH), (C_N512, -0.5 / CONV_CH)):
        k[:, at:at + P] = v
    cos, sin, swap = rope_rows(ROPE)
    for d, s, sign in swap:
        k[NOPE + s, C_P96 + NOPE + d] = sign
    k[NOPE:QK, C_MROPE:C_MROPE + SEQ] = cos
    k[NOPE:QK, C_MROPE + SEQ:C_MROPE + 2 * SEQ] = sin
    cos, sin, swap = rope_rows(HD)
    for h in range(2):
        k[h * HD:(h + 1) * HD, C_B64 + h * HD:C_B64 + (h + 1) * HD] = -0.5 / HD
        for d, s, sign in swap:
            k[h * HD + s, C_P128 + h * HD + d] = sign
        k[h * HD:(h + 1) * HD, C_GROPE:C_GROPE + SEQ] = cos
        k[h * HD:(h + 1) * HD, C_GROPE + SEQ:C_GROPE + 2 * SEQ] = sin
    a = 2 * np.pi * (np.outer(np.arange(P), np.arange(P)) % P) / P
    k[:, C_DFT:C_DFT + P] = np.cos(a) / np.sqrt(P)
    k[:, C_DFT + P:C_DFT + 2 * P] = np.sin(a) / np.sqrt(P)
    return k


def dft_array():
    a = 2 * np.pi * (np.outer(np.arange(SEQ), np.arange(SEQ)) % SEQ) / SEQ
    return np.concatenate([np.cos(a), -np.sin(a)], axis=1).astype(np.float32) / np.float32(np.sqrt(SEQ))


def trunk(nc, x_in, c_in, ctx_in, c_ctx_in, w_mod, b_mod, g_pre, g_post, w_gate, w_up, w_down,
          ev_w_in, conv_w, conv_b, ln_g, ln_b, g_cq, w_uq, g_ckv, w_ukv, ev_w_out,
          od_w_in, g_qn, g_kn, od_w_out, consts, dft, out):
    mod_scratch = nc.dram_tensor("mod_scratch", (UNITS * 8, 4, P), F32).ap()
    x_scratch = nc.dram_tensor("x_scratch", (P, KD, TOK), F32).ap()
    ctx = ExitStack()
    names = {}

    def sb(stack, name, shape, dt=F32):
        return stack.enter_context(nc.sbuf_tensor(name, shape, dt))

    def sem(name):
        if name not in names:
            names[name] = ctx.enter_context(nc.semaphore(name))
        return names[name]

    with ctx:
        h = sb(ctx, "h", [P, KD, 2, TOK], F32R)
        raw = sb(ctx, "raw", [P, RAWS, CHUNK])
        w_half = [sb(ctx, "w_hi", [P, SLOTS, CHUNK], F32R), sb(ctx, "w_lo", [P, SLOTS, CHUNK], F32R)]
        sq = sb(ctx, "sq", [P, 2, TOK])
        sum_sq = sb(ctx, "sum_sq", [P, GAPPED])
        ident = sb(ctx, "ident", [P, 2 * P])
        vecs = sb(ctx, "vecs", [P, 2 * P])
        cond = sb(ctx, "cond", [P, KD, 2, 2], F32R)
        mod = sb(ctx, "mod", [P, 6, 3, KD, 2])
        coef_pre = sb(ctx, "coef_pre", [P, 6, KD, 2])
        coef_post = sb(ctx, "coef_post", [P, 6, KD, 2])
        small = sb(ctx, "small", [P, 10])
        taps = sb(ctx, "taps", [P, 32])
        n1024 = ident[:, P:2 * P]
        idm = ident[:, 0:P]
        with ExitStack() as s:
            x = sb(s, "x", [P, KD, TOK])
            y = sb(s, "y", [P, KD, TOK])
            hid = sb(s, "hid", [P, 2, 2, 2, TOK], F32R)
            mod_raw = sb(s, "mod_raw", [P, MOD_SLOTS, CHUNK])
            m_half = [sb(s, "m_hi", [P, MOD_SLOTS, CHUNK], F32R), sb(s, "m_lo", [P, MOD_SLOTS, CHUNK], F32R)]
            mod_row = sb(s, "mod_row", [4, CHUNK])
        with ExitStack() as s:
            sb(s, "x_", [P, KD, TOK])
            sb(s, "y_", [P, KD, TOK])
            t = sb(s, "t", [P, 2, TOK])
            rstd = sb(s, "rstd", [P, TOK])
            sb(s, "pad_", [P, TOK])
            fin = sb(s, "fin", [P, 14, P])
        m_rows = fin[:, 0:8, :].rearrange("r (l s) c -> r l s c", l=2)
        m_sum = fin[:, 8:12, :].rearrange("r (l j) c -> r l j c", l=2)
        m_bias = fin[:, 12:14, :]
        with ExitStack() as s:
            sb(s, "x__", [P, KD, TOK])
            tok_in = sb(s, "tok_in", [P, TOK // P, D])
            sb(s, "t__", [P, 3, TOK])
            vec_in = sb(s, "vec_in", [P, 2, P])
            cond_f = sb(s, "cond_f", [P, 2, KD])
        with ExitStack() as s:
            u = sb(s, "u", [P, KC, PADDED])
            cn = sb(s, "cn", [P, KQ + KKV, 2, TOK], F32R)
            v_all = sb(s, "v_all", [P, TOK // P, HEADS * VD])
            e_vz = sb(s, "e_vz", [P, TOK // P, 2, 3 * VD], F32R)
            prob = sb(s, "prob", [P, 2, TOK])
            q_f = sb(s, "q_f", [P, 2, TOK])
            e_mats = sb(s, "e_mats", [P, C_B64 - C_N384])
            e_rope = sb(s, "e_rope", [P, 2, SEQ])
            with ExitStack() as s2:
                q_h = sb(s2, "q_h", [P, 2, 2, TOK], F32R)
                k_h = sb(s2, "k_h", [P, 2, 2, TOK], F32R)
            with ExitStack() as s2:
                cqkv = sb(s2, "cqkv", [P, KQ + KKV, TOK])
                rstd_e = sb(s2, "rstd_e", [P, TOK])
        pt = h[:, 0:4, :, :].rearrange("p a b c -> p (a b c)").rearrange("p (k g q) -> p k g q", k=6, g=2)
        with ExitStack() as s:
            q4 = sb(s, "q4", [P, 4, SEQ])
            kv_f = sb(s, "kv_f", [P, 2, TOK])
            o_rope = sb(s, "o_rope", [P, 2, SEQ])
            o_mats = sb(s, "o_mats", [P, 4, P])
            dft_c = sb(s, "dft_c", [P, 2, 2 * P], F32R)
            k_dup = sb(s, "k_dup", [P, GQA_KV, 2, TOK], F32R)
            v_t = sb(s, "v_t", [P, TOK // P, P])
            o_vz = sb(s, "o_vz", [P, TOK // P, 2, 3 * VD], F32R)
            o_prob = sb(s, "o_prob", [P, 2, TOK])
            rstd_o = sb(s, "rstd_o", [P, TOK])
            qz = sb(s, "qz", [P, 2, 2, SEQ], F32R)
            with ExitStack() as s2:
                f4 = sb(s2, "f4", [P, 4, SEQ])
                f_h = sb(s2, "f_h", [P, 2, SEQ], F32R)
                ab = sb(s2, "ab", [P, 4, 2, 2 * P], F32R)
            with ExitStack() as s2:
                o_pt = sb(s2, "o_pt", [P, TOK // P, 2, SEQ], F32R)

        ps = ctx.enter_context(nc.psum_tensor("ps", [P, 8 * 512], F32))

        def tile(bank, c0=0, n=TOK, r0=0, r1=P):
            return ps[r0:r1, bank * 512 + 256 + c0:bank * 512 + 256 + c0 + n]

        def bank_(b, n=512, r0=0, r1=P):
            return ps[r0:r1, b * 512:b * 512 + n]

        w_loaded = [sem(f"w_loaded{j}") for j in range(RAWS)]
        w_hi, w_lo, w_done = sem("w_hi"), sem("w_lo"), sem("w_done")
        m_loaded = [sem(f"m_loaded{j}") for j in range(MOD_SLOTS)]
        m_hi, m_lo, m_done = sem("m_hi"), sem("m_lo"), sem("m_done")
        row_ready, row_stored = sem("row_ready"), sem("row_stored")
        block = ctx.enter_context(nc.Block())

        def cols(w, at, width):
            return w.rearrange("(k p) c -> p k c", p=P)[:, :, bass.ds(at, width)]

        PASSES = ((0, 0), (0, 1), (1, 0))

        def known(i):
            return isinstance(i, int)

        def down_tiles(segs):
            out_tiles = []
            for d in range(KD):
                for seg in segs:
                    bank = 4 if len(segs) > 1 or d % 2 == 0 else 6
                    out_tiles.append((d, seg, tile(bank, seg[0], seg[1])))
            return out_tiles

        ffn_at = {0: 0, 2: 1, 3: 2, 5: 3}
        N_PRE = {0: 0, 1: 2, 2: 7, 3: 9, 4: 11, 5: 18}
        N_POST = {0: 1, 1: 6, 2: 8, 3: 10, 4: 17, 5: 19}
        N_CQ, N_CKV, N_LN, N_Q, N_K = 3, 4, 5, 12, 16
        x_new, x_sq, x_sum = sem("x_new"), sem("x_sq"), sem("x_sum")
        h_t, h_hi, h_lo = sem("h_t"), sem("h_hi"), sem("h_lo")
        y_zero, y_done, y_sq, y_acc, y_sum, y_t = (sem(n) for n in ("y_zero", "y_done", "y_sq", "y_acc", "y_sum", "y_t"))
        n_ln, n_r0, n_r2, n_b, n_rstd = (sem(n) for n in ("n_ln", "n_r0", "n_r2", "n_b", "n_rstd"))
        silu_done, hid_f, hid_hi, hid_lo, down_done = (sem(n) for n in ("silu_done", "hid_f", "hid_hi", "hid_lo", "down_done"))
        consts_in, vecs_in, tok_loaded = sem("consts_in"), sem("vecs_in"), sem("tok_loaded")
        vec_t, vecs_ready, cond_f_ready, cond_hi, cond_ready = (sem(n) for n in ("vec_t", "vecs_ready", "cond_f_ready", "cond_hi", "cond_ready"))
        tok_t = sem("tok_t")
        rows_in, rows_sum, rows_full, rows_t, mod_ready, coef_ready = (
            sem(n) for n in ("rows_in", "rows_sum", "rows_full", "rows_t", "mod_ready", "coef_ready"))
        y_base = {0: 0, 1: 176, 2: 184, 3: 360, 4: 536, 5: 544}
        y_end = {0: 176, 1: 184, 2: 360, 3: 536, 4: 544, 5: 632}
        x_aside, x_back = sem("x_aside"), sem("x_back")

        @block.sync
        def _(sp):
            def load(i, per, c, src, k, n):
                if not known(i) or i * per + c >= RAWS:
                    sp.wait_ge(w_lo, i * per + (c - 1))
                dst = raw[:, c % RAWS, 0:k * n]
                if k > 1:
                    dst = dst.rearrange("p (k c) -> p k c", k=k)
                sp.dma_start(dst, src).then_inc(w_loaded[c % RAWS], 16)

            def ffn(q, l, s):
                b = BASE[q]
                gate, up, down = w_gate[l, s], w_up[l, s], w_down[l, s]

                def up_chunk(i, c, w, f):
                    at = f * P if known(i) else sp.snap(f * P)
                    load(i, 12, c, cols(w, at, P), KD, P)

                def down_chunk(i, c, f):
                    at = f * P if known(i) else sp.snap(f * P)
                    load(i, 12, c, down[bass.ds(at, P), :], 1, CHUNK)

                for j in range(4):
                    up_chunk(0, b + j, (gate, up)[j % 2], j // 2)
                with sp.Fori(0, 5) as i:
                    for half in range(2):
                        c0 = b + 4 + 6 * half
                        for j in range(6):
                            if j < 4:
                                up_chunk(i, c0 + j, (gate, up)[j % 2], i * 4 + (2 + 2 * half + j // 2))
                            else:
                                down_chunk(i, c0 + j, i * 4 + (2 * half + j - 4))
                for j in range(2):
                    down_chunk(0, b + 64 + j, FT - 2 + j)
                if q == 5:
                    down_chunk(0, b + 66, 0)

            def set_aside(n, ready):
                sp.wait_ge(x_new, ready)
                sp.dma_start(x_scratch, x[:, :, :]).then_inc(x_aside, 16)

            def even_mixer():
                b = BASE[1]
                def in_tiles(i):
                    for c in range(4):
                        load(0, 4, b + 4 * i + c, cols(ev_w_in[0], (2 * i + c // 2) * P + (1 - c % 2) * CONV_CH, P), KD, P)
                in_tiles(0)
                set_aside(0, 16)
                sp.wait_ge(h_lo, 16)
                sp.wait_ge(x_aside, 16)
                sp.dma_start(e_mats[:, :], consts[:, C_N384:C_B64]).then_inc(sem("e_consts"), 16)
                sp.dma_start(e_rope[:, :, :], consts[:, C_MROPE:C_MROPE + 2 * SEQ].rearrange(
                    "p (a t) -> p a t", a=2)).then_inc(sem("e_consts"), 16)
                in_tiles(1)
                for m in range(KQ + KKV):
                    load(0, 4, b + 8 + m, cols(ev_w_in[0], 2 * CONV_CH + m * P, P), KD, P)
                load(0, 4, b + 13, cols(ev_w_in[0], 2 * CONV_CH + Q_LORA + KV_LORA, ROPE), KD, ROPE)
                for k in range(KKV):
                    load(0, 4, b + E_V + k, w_ukv[0][k * P:(k + 1) * P, :], 1, CHUNK)
                with sp.Fori(0, 2) as i:
                    for e in range(2):
                        at = sp.snap(i * 4 * QK + e * 2 * QK)
                        load(i, 4, b + E_PAIR + 2 * e, cols(w_uq[0], at, 2 * QK), KQ, 2 * QK)
                        at = sp.snap(i * 4 + 2 * e)
                        keys = [w_ukv[0][k * P:(k + 1) * P, :].rearrange("p (h d) -> p h d", h=HEADS)[
                            :, bass.ds(at, 2), 0:NOPE] for k in range(KKV)]
                        c = b + E_PAIR + 2 * e + 1
                        done = sp.snap(i * 32 + 16 * (e + 1))
                        sp.wait_ge(w_lo, i * 4 + (c - 1))
                        for k in range(KKV):
                            if k == 1:
                                sp.wait_ge(sem("e_ukv"), done)
                            sp.dma_start(raw[:, c % RAWS, k * P:(k + 1) * P].rearrange("p (h d) -> p h d", h=2),
                                         keys[k]).then_inc(w_loaded[c % RAWS] if k else sem("e_ukv"), 16)
                out_chunk = lambda i, c: load(i, 4, b + E_OUT + c, cols(ev_w_out[0], i * 4 * P + c * P if known(i)
                                              else sp.snap(i * 4 * P + c * P), P), KD, P)
                for c in range(4):
                    out_chunk(0, c)
                sp.wait_ge(sem("e_ln_lo"), KC)
                sp.dma_start(x[:, :, :], x_scratch).then_inc(x_back, 16)
                for c in range(4, 8):
                    out_chunk(0, c)

            def odd_mixer():
                b = BASE[4]
                in_tiles = lambda m0, m1: [load(0, 4, b + m, cols(od_w_in[0], m * P, P), KD, P) for m in range(m0, m1)]
                in_tiles(0, 4)
                set_aside(1, 40)
                sp.wait_ge(h_lo, 40)
                sp.wait_ge(x_aside, 32)
                for dst, at, n in ((o_mats[:, :, :], C_B64, 4 * P), (o_rope[:, :, :], C_GROPE, 2 * SEQ)):
                    sp.dma_start(dst, consts[:, at:at + n].rearrange("p (a t) -> p a t", a=dst.shape[1])).then_inc(
                        sem("o_consts"), 16)
                in_tiles(4, 10)
                for j in range(4):
                    load(0, 4, b + O_DFT + j, dft[j * P:(j + 1) * P, :], 1, CHUNK)
                out_chunk = lambda c: load(0, 4, b + O_OUT + c, cols(od_w_out[0], c * P, P), KD, P)
                for c in range(4):
                    out_chunk(c)
                sp.wait_ge(sem("o_lo"), 4)
                sp.dma_start(x[:, :, :], x_scratch).then_inc(x_back, 16)
                for c in range(4, 8):
                    out_chunk(c)

            sp.dma_start(ident[:, :], consts[:, C_ID:C_N384]).then_inc(consts_in, 16)
            for row, src in ((V_GPRE, g_pre.rearrange("l s (k p) -> (l s k) p", p=P)),
                             (V_GPOST, g_post.rearrange("l s (k p) -> (l s k) p", p=P)),
                             (V_C, c_in.rearrange("b (k p) -> (b k) p", p=P)),
                             (V_CCTX, c_ctx_in.rearrange("(k p) -> k p", p=P)),
                             (V_CONVB, conv_b.rearrange("b (k p) -> (b k) p", p=P)),
                             (V_LNG, ln_g.rearrange("b (k p) -> (b k) p", p=P)),
                             (V_LNB, ln_b.rearrange("b (k p) -> (b k) p", p=P)),
                             (V_GCQ, g_cq.rearrange("b (k p) -> (b k) p", p=P)),
                             (127, g_cq.rearrange("b (k p) -> (b k) p", p=P)[0:1, :])):
                sp.dma_start(vec_in[row:row + src.shape[0], 0, :], src).then_inc(vecs_in, 16)
            for row, src, at, n in ((0, conv_w.rearrange("b k (c p) -> (b k c) p", p=P), 0, P),
                                    (124, g_ckv.rearrange("b (k p) -> (b k) p", p=P), 0, P),
                                    (126, g_qn, 0, HD), (126, g_qn, HD, HD), (127, g_kn, 0, HD), (127, g_kn, HD, HD)):
                sp.dma_start(vec_in[row:row + src.shape[0], 1, at:at + n], src).then_inc(vecs_in, 16)
            sp.dma_start(tok_in[:, 0:2, :], ctx_in[0].rearrange("(j p) d -> p j d", p=P)).then_inc(tok_loaded, 16)
            sp.dma_start(tok_in[:, 2:6, :], x_in[0].rearrange("(j p) d -> p j d", p=P)).then_inc(tok_loaded, 16)
            ffn(0, 0, 0)
            even_mixer()
            ffn(2, 0, 1)
            ffn(3, 1, 0)
            odd_mixer()
            ffn(5, 1, 1)
            for j in range(4):
                sp.wait_ge(sem("out_ready"), j + 1)
                sp.dma_start(out[0, j * P:(j + 1) * P, :], tok_in[:, j, :]).then_inc(sem("out_stored"), 16)
            sp.wait_ge(sem("out_stored"), 64)

        @block.gpsimd
        def _(pool):
            def load_mod(i, c, layer, unit, k):
                blocks = w_mod.rearrange("l r (u c) -> (l r u) c", c=CHUNK)
                b0 = layer * (9 * D - 9) + (unit + 9 * P * k)
                if not known(i):
                    b0 = pool.snap(b0)
                if not known(i) or i * 24 + c >= MOD_SLOTS:
                    pool.wait_ge(m_lo, i * 24 + (c - 1))
                pool.dma_start(mod_raw[:, c % MOD_SLOTS, :], blocks[bass.ds(b0, P, 9), :]).then_inc(
                    m_loaded[c % MOD_SLOTS], 16)

            def store_row(i, u):
                at = 8 * u if known(i) else pool.snap(i * 24 + 8 * u)
                pool.wait_ge(row_ready, i * 3 + (u + 1))
                pool.dma_start(mod_scratch[bass.ds(at, 8)].rearrange("a s c -> s a c"),
                               mod_row[:, :].rearrange("s (a c) -> s a c", c=P)).then_inc(row_stored, 16)

            def zero_y(n, ready):
                pool.wait_ge(x_new, ready)
                nc.gpsimd.memset(y[:, :, :], 0.0).then_inc(y_zero, 1)

            def held(a):
                nc.gpsimd.tensor_tensor(small[:, 8 + a % 2:9 + a % 2], small[:, 6 + a % 2:7 + a % 2],
                                        small[:, 6 + a % 2:7 + a % 2], ALU.mult)

            for c in range(16):
                load_mod(0, c, 0, c // 8, c % 8)
                if c == 9:
                    store_row(0, 0)
            store_row(0, 1)
            pool.wait_ge(row_stored, 32)
            pool.dma_start(m_rows[0:16, 0, :, :], mod_scratch[0:16]).then_inc(rows_in, 16)
            pool.dma_start(m_bias[0:16, 0, :], b_mod[0].rearrange("(r c) -> r c", c=P)[0:16, :]).then_inc(rows_in, 16)
            zero_y(0, 8)
            for k in range(8):
                load_mod(0, 16 + k, 0, 2, k)
            with pool.Fori(0, 5) as i:
                for m in range(24):
                    load_mod(i, 24 + m, (i + 1) // 3, i * 3 + (3 + m // 8), m % 8)
                    if m % 8 == 1:
                        store_row(i, 2 + m // 8)
            store_row(0, UNITS - 1)
            pool.wait_ge(row_stored, 16 * UNITS)
            pool.wait_ge(mod_ready, 1)
            pool.wait_ge(w_done, 64)
            for l in range(2):
                pool.dma_start(m_rows[0:72, l, :, :], mod_scratch[72 * l:72 * l + 72]).then_inc(rows_in, 16)
                pool.dma_start(m_bias[0:72, l, :], b_mod[l].rearrange("(r c) -> r c", c=P)).then_inc(rows_in, 16)
            pool.wait_ge(x_aside, 16)
            pool.wait_ge(h_lo, 16)
            for at, n in ((0, HALO), (HALO + CTX, HALO), (HALO + GAPPED, HALO)):
                nc.gpsimd.memset(u[:, :, at:at + n], 0.0).then_inc(sem("e_zero"), 1)
            nc.gpsimd.memset(e_vz[:, :, :, VD:2 * VD].bitcast(F32), 0.0).then_inc(sem("e_zero"), 1)
            nc.gpsimd.memset(q_f[0:NOPE, 0, :], 0.0).then_inc(sem("e_zero"), 1)
            with pool.Fori(0, 4) as i:
                for a in range(12):
                    n = TOK if a % 6 < 4 else CTX
                    pool.wait_ge(sem("e_ri"), i * 12 + (a + 1))
                    held(a)
                    nc.gpsimd.tensor_scalar(prob[:, a % 2, 0:n], prob[:, a % 2, 0:n],
                                            small[:, 6 + a % 2:7 + a % 2], None, ALU.mult).then_inc(sem("e_pn"), 1)
            zero_y(1, 24)
            zero_y(2, 32)
            pool.wait_ge(x_aside, 32)
            pool.wait_ge(h_lo, 40)
            nc.gpsimd.memset(qz[:, :, :, :].bitcast(F32), 0.0).then_inc(sem("o_zero"), 1)
            nc.gpsimd.memset(o_vz[:, :, :, :].bitcast(F32), 0.0).then_inc(sem("o_zero"), 1)
            with pool.Fori(0, 4) as i:
                for a in range(8):
                    pool.wait_ge(sem("o_ri"), i * 8 + (a + 1))
                    held(a)
                    nc.gpsimd.tensor_scalar(o_prob[:, a % 2, :], o_prob[:, a % 2, :],
                                            small[:, 6 + a % 2:7 + a % 2], None, ALU.mult).then_inc(sem("o_pn"), 1)
            zero_y(3, 48)

        @block.tensor
        def _(pe):
            def weight(half, c, k, width, at=0, m=P):
                return w_half[half][:, c % SLOTS, k * width + at:k * width + at + m]

            def modulate(i, c):
                pe.wait_ge(m_lo, i * 24 + (c + 1))
                k = c % 8
                if k == 0 and (not known(i) or c > 0):
                    pe.wait_ge(row_ready, i * 3 + c // 8)
                for n in range(2):
                    for half in range(2):
                        mm = pe.matmul(bank_(6 + n, 512, 0, 4), cond[:, k, :, :].rearrange("p j h -> p (j h)"),
                                       m_half[half][:, c % MOD_SLOTS, n * 512:(n + 1) * 512],
                                       start=(k == 0 and half == 0), stop=(k == 7 and half == 1))
                mm.then_inc(m_done, 1)

            def project(i, per, c, place, segs, width=P, h_ready=None, mods=(), korder=range(KD), waits=None):
                pe.wait_ge(w_lo, i * per + (c + 1))
                for at, k in enumerate(korder):
                    if h_ready is not None:
                        pe.wait_ge(h_lo, h_ready + k + 1)
                    if waits is not None:
                        waits(k)
                    for p_, (a, b_) in enumerate(PASSES):
                        for c0, n, _ in segs:
                            mm = pe.matmul(tile(place, c0, n, 0, width), weight(a, c, k, width, 0, width),
                                           h[:, k, b_, c0:c0 + n], start=(at == 0 and p_ == 0),
                                           stop=(at == KD - 1 and p_ == 2))
                    if at == 3 and mods:
                        modulate(i, mods[0])
                mm.then_inc(w_done, 1)
                if mods:
                    modulate(i, mods[1])

            def ffn(q, segs):
                b, fi = BASE[q], ffn_at[q]
                nt = KD * len(segs)
                tiles = down_tiles(segs)
                y0, d0 = y_base[q], 165 * fi

                def up(i, c, t, first, m0):
                    for j in range(4):
                        if j % 2 == 0:
                            pe.wait_ge(silu_done, i * 4 + (22 * fi + 2 * t + j // 2))
                        else:
                            pe.wait_ge(hid_f, i * 4 + (22 * fi + 2 * t + j // 2))
                        project(i, 12, c + j, 2 * (j % 2), segs, h_ready=8 * q if first and j == 0 else None,
                                mods=(m0 + 2 * j, m0 + 2 * j + 1) if m0 is not None else ())

                def down(i, c, t, m0):
                    pe.wait_ge(w_lo, i * 12 + (c + 2))
                    pe.wait_ge(hid_lo, i * 4 + (22 * fi + 2 * t + 2))
                    for idx, (d, (c0, n, _), place) in enumerate(tiles):
                        if idx >= 2 or known(i):
                            pe.wait_ge(y_done, i * 2 * nt + (y0 + t * nt + idx - 1))
                        for kk in range(2):
                            for p_, (a, b_) in enumerate(PASSES):
                                mm = pe.matmul(place, w_half[a][:, (c + kk) % SLOTS, d * P:(d + 1) * P],
                                               hid[:, t % 2, kk, b_, c0:c0 + n],
                                               start=(kk == 0 and p_ == 0), stop=(kk == 1 and p_ == 2))
                            if idx == nt - 1:
                                mm.then_inc(w_done, 1)
                        if idx < nt - 1:
                            mm.then_inc(down_done, 1)
                        if m0 is not None and idx % 4 == 3:
                            modulate(i, m0 + idx // 4)

                up(0, b, 0, True, 16 if q == 0 else None)
                with pe.Fori(0, 5) as i:
                    for half in range(2):
                        m0 = 24 + 12 * half if q == 0 else None
                        up(i, b + 4 + 6 * half, 1 + half, False, m0)
                        down(i, b + 8 + 6 * half, half, m0 + 8 if q == 0 else None)
                down(0, b + 64, 10, None)

            def add_squares(n, done, segs):
                pe.wait_ge(y_acc, done)
                for c0, w, _ in segs:
                    mm = pe.matmul(tile(0, c0, w), n1024, sum_sq[:, c0:c0 + w], start=True, stop=True)
                mm.then_inc(y_sum, 1)

            def square_x(q, segs):
                for k in range(KD):
                    pe.wait_ge(x_sq, 8 * q + k + 1)
                    for c0, w, _ in segs:
                        mm = pe.matmul(tile(2, c0, w), n1024, sq[:, k % 2, c0:c0 + w],
                                       start=(k == 0), stop=(k == KD - 1))
                    mm.then_inc(x_sum, 1)

            def mod_rows(units_l, r, done):
                pe.wait_ge(rows_full, done)
                for l in range(units_l):
                    for j in range(2):
                        mm = pe.transpose(bank_(0)[:, (l * 2 + j) * 72:(l * 2 + j) * 72 + r],
                                          m_sum[0:r, l, j, :], idm[0:r, 0:r])
                mm.then_inc(rows_t, 1)

            def even_pair(i, e):
                b = BASE[1] + E_PAIR
                pair = lambda per, c: i * (2 * per) + (e * per + c)
                pe.wait_ge(w_lo, i * 4 + (b + 2 * e + 2))
                for hh in range(2):
                    for k in range(KQ):
                        for p_, (a, b_) in enumerate(PASSES):
                            for c0, n, _ in ALL:
                                mm = pe.matmul(tile(2 * hh, c0, n, 0, QK), weight(a, b + 2 * e, k, 2 * QK, hh * QK, QK),
                                               cn[:, k, b_, c0:c0 + n], start=(k == 0 and p_ == 0),
                                               stop=(k == KQ - 1 and p_ == 2))
                    mm.then_inc(sem("e_q") if hh == 0 else w_done, 1)
                for k in range(KKV):
                    for p_, (a, b_) in enumerate(PASSES):
                        for c0, n, _ in ALL:
                            mm = pe.matmul(tile(4, c0, n), weight(a, b + 2 * e + 1, k, P), cn[:, KQ + k, b_, c0:c0 + n],
                                           start=(k == 0 and p_ == 0), stop=(k == KKV - 1 and p_ == 2))
                mm.then_inc(w_done, 1)
                for hh in range(2):
                    pe.wait_ge(sem("e_qf"), pair(2, hh + 1))
                    pe.matmul(tile(2 * hh, CTX, SEQ, 0, QK), e_mats[0:QK, C_P96 - C_N384:C_P96 - C_N384 + QK],
                              q_f[0:QK, hh, CTX:TOK], start=True, stop=True).then_inc(sem("e_rot"), 1)

                def score(a):
                    hh, j = a // 6, a % 6
                    if a < 2:
                        pe.wait_ge(sem("e_q_lo"), pair(2, 2))
                        pe.wait_ge(sem("e_k_lo"), pair(2, 2))
                    else:
                        pe.wait_ge(sem("e_exp"), pair(12, a - 1))
                    q0 = CTX + j * P if j < 4 else (j - 4) * P
                    for p_, (qa, kb) in enumerate(PASSES):
                        for c0, n, _ in (ALL if j < 4 else (SEG_C,)):
                            mm = pe.matmul(tile(2 * (a % 2), c0, n), q_h[0:QK, hh, qa, q0:q0 + P],
                                           k_h[0:QK, hh, kb, c0:c0 + n], start=(p_ == 0), stop=(p_ == 2))
                    mm.then_inc(sem("e_s"), 1)

                def turn(a):
                    pe.wait_ge(sem("e_pn"), pair(12, a + 1))
                    if a >= 1:
                        pe.wait_ge(sem("e_pt_lo"), pair(12, a))
                    else:
                        pe.wait_ge(sem("e_k_lo"), pair(2, 2))
                    for kt in range(6 if a % 6 < 4 else 2):
                        mm = pe.transpose(tile(4, kt * P, P), prob[:, a % 2, kt * P:(kt + 1) * P], idm)
                    mm.then_inc(sem("e_tr"), 1)

                def values(hh, context):
                    pe.wait_ge(sem("e_pt_lo"), pair(12, 6 * hh + (6 if context else 4)))
                    if hh == 0 and not context:
                        pe.wait_ge(sem("e_vz_lo"), pair(1, 1))
                    keys, n = (2, CTX) if context else (6, SEQ)
                    for kt in range(keys):
                        for p_, (a, b_) in enumerate(PASSES):
                            mm = pe.matmul(bank_(7 if context else 6, n), e_vz[:, kt, a, hh * VD:hh * VD + P],
                                           pt[:, kt, b_, 0:n], start=(hh == 0 and kt == 0 and p_ == 0),
                                           stop=(hh == 1 and kt == keys - 1 and p_ == 2))
                    mm.then_inc(sem("e_pv"), 1)

                score(0)
                score(1)
                for a in range(12):
                    turn(a)
                    if a + 2 < 12:
                        score(a + 2)
                    if a % 6 == 3:
                        values(a // 6, False)
                    if a % 6 == 5:
                        values(a // 6, True)

            def even_mixer():
                b = BASE[1]
                for c in range(8):
                    if c >= 2:
                        pe.wait_ge(sem("e_u" if c % 2 else "e_sig"), c // 2)
                    project(0, 4, b + c, 2 * (c % 2), ALL, h_ready=8 if c == 0 else None)
                for m in range(6):
                    if m == 0:
                        pe.wait_ge(sem("e_sig"), 4)
                    elif m == 1:
                        pe.wait_ge(sem("e_u"), 4)
                    else:
                        pe.wait_ge(sem("e_cf"), m - 1)
                    project(0, 4, b + 8 + m, 2 * (m % 2), ALL, width=P if m < 5 else ROPE)
                pe.wait_ge(sem("e_consts"), 32)
                for m in range(5):
                    pe.wait_ge(sem("e_csq"), m + 1)
                    at = (C_N384 if m < KQ else C_N256) - C_N384
                    for c0, n, _ in ALL:
                        mm = pe.matmul(tile(4 if m < KQ else 6, c0, n),
                                       e_mats[:, at:at + P], sq[:, m % 2, c0:c0 + n],
                                       start=(m in (0, KQ)), stop=(m in (KQ - 1, 4)))
                    mm.then_inc(sem("e_csum"), 1)
                pe.wait_ge(sem("e_cf"), 6)
                pe.wait_ge(sem("e_zero"), 5)
                pe.matmul(tile(0, CTX, SEQ, 0, QK), e_mats[0:QK, C_P96 - C_N384:C_P96 - C_N384 + QK],
                          q_f[0:QK, 0, CTX:TOK], start=True, stop=True).then_inc(sem("e_krot"), 1)
                pe.wait_ge(w_lo, b + E_V + 2)
                pe.wait_ge(sem("e_cn_lo"), 5)
                for j in range(6):
                    if j >= 2:
                        pe.wait_ge(sem("e_v"), j - 1)
                    for k in range(KKV):
                        for p_, (a, b_) in enumerate(PASSES):
                            v_cols = w_half[b_][:, (b + E_V + k) % SLOTS, :].rearrange(
                                "p (h d) -> p h d", d=NOPE + VD)[:, :, NOPE:NOPE + VD]
                            mm = pe.matmul(bank_(2 + j % 2).rearrange("p (h d) -> p h d", d=VD),
                                           cn[:, KQ + k, a, j * P:(j + 1) * P], v_cols,
                                           start=(k == 0 and p_ == 0), stop=(k == KKV - 1 and p_ == 2))
                        if j == 5:
                            mm.then_inc(w_done, 1)
                    if j < 5:
                        mm.then_inc(sem("e_vmm"), 1)
                pe.wait_ge(sem("e_kpe_lo"), 2)
                pe.wait_ge(sem("e_v"), 6)
                with pe.Fori(0, 2) as i:
                    for e in range(2):
                        even_pair(i, e)
                for n_ in range(2):
                    for c in range(KC):
                        if n_ == 0:
                            pe.wait_ge(sem("e_conv"), (CONV_K + 1) * (c + 1))
                        else:
                            pe.wait_ge(sem("e_dsq"), c + 1)
                        for c0, n, _ in ALL:
                            at = (C_M512, C_N512)[n_] - C_N384
                            g0 = c0 + HALO if c0 else 0
                            src = u[:, c, g0:g0 + n] if n_ == 0 else sq[:, c % 2, c0:c0 + n]
                            mm = pe.matmul(tile(2 * n_, c0, n), e_mats[:, at:at + P], src,
                                           start=(c == 0), stop=(c == KC - 1))
                        mm.then_inc(sem("e_lsum"), 1)
                def attn_then_conv(k):
                    if k >= 4:
                        pe.wait_ge(sem("e_o_lo"), 4)
                    else:
                        pe.wait_ge(sem("e_ln_lo"), k + 1)
                for c in range(KD):
                    if c < 2:
                        pe.wait_ge(n_rstd, N_LN + 1)
                    else:
                        pe.wait_ge(y_done, y_base[1] + c - 1)
                    project(0, 4, b + E_OUT + c, 2 * (c % 2), ALL, korder=(4, 5, 6, 7, 0, 1, 2, 3),
                            waits=attn_then_conv if c == 0 else None)

            def odd_mixer():
                b = BASE[4]
                for m in range(10):
                    segs = ALL if m in (4, 5) else XONLY
                    if m >= 2:
                        pe.wait_ge(sem("o_pf"), m - 1)
                    project(0, 4, b + m, 2 * (m % 2), segs, h_ready=32 if m == 0 else None)
                    if m == 4:
                        pe.wait_ge(sem("o_consts"), 32)
                    if 6 <= m:
                        head_swap(m - 6)
                    if 5 <= m:
                        head_sum(m - 5)
                pe.wait_ge(sem("o_dftc"), 1)
                pe.wait_ge(w_lo, b + O_DFT + 4)
                for g in range(4):
                    pe.wait_ge(sem("o_f_lo"), g + 1)
                    for j in range(4):
                        if g * 4 + j >= 2:
                            pe.wait_ge(sem("o_ab_lo"), g * 4 + j - 1)
                        elif g == 0:
                            pe.wait_ge(sem("o_pf"), 10)
                        for p_, (a, b_) in enumerate(PASSES):
                            mm = pe.matmul(bank_(2 * (j % 2), 2 * P), f_h[:, a, j * P:(j + 1) * P], dft_c[:, b_, :],
                                           start=(p_ == 0), stop=(p_ == 2))
                        mm.then_inc(sem("o_ab"), 1)
                    if g == 1:
                        head_swap(4)
                    if g >= 1:
                        pe.wait_ge(sem("o_fn_lo"), g)
                    pe.wait_ge(sem("o_ab_lo"), 4 * g + 4)
                    for j in range(4):
                        for t_ in range(2):
                            for p_, (a, b_) in enumerate(PASSES):
                                mm = pe.matmul(bank_(4), ab[:, j, a, t_ * P:(t_ + 1) * P],
                                               w_half[b_][:, (b + O_DFT + j) % SLOTS, t_ * 512:(t_ + 1) * 512],
                                               start=(j == 0 and t_ == 0 and p_ == 0), stop=(j == 3 and t_ == 1 and p_ == 2))
                        if g == 3:
                            mm.then_inc(w_done, 1)
                    if g < 3:
                        mm.then_inc(sem("o_fn"), 1)
                pe.wait_ge(sem("o_ab_lo"), 16)
                for j in range(6):
                    mm = pe.transpose(tile(0, j * P, P), kv_f[:, 1, j * P:(j + 1) * P], idm)
                mm.then_inc(sem("o_vt"), 1)
                pe.wait_ge(sem("o_kd"), 4)
                pe.wait_ge(sem("o_vtf"), 1)
                with pe.Fori(0, 2) as i:
                    for e in range(2):
                        odd_pair(i, e)
                for c in range(KD):
                    if c < 2:
                        pe.wait_ge(sem("o_lo"), 4)
                    else:
                        pe.wait_ge(y_done, y_base[4] + c - 1)
                    project(0, 4, b + O_OUT + c, 2 * (c % 2), XONLY)

            def head_sum(m):
                pe.wait_ge(sem("o_qsq"), m + 1)
                if m:
                    pe.wait_ge(n_rstd, N_Q + m)
                for c0, w, _ in (XONLY if m < 4 else ALL):
                    mm = pe.matmul(tile(6, c0, w), o_mats[:, 0, :], sq[:, m % 2, c0:c0 + w], start=True, stop=True)
                mm.then_inc(sem("o_qsum"), 1)

            def head_swap(m):
                pe.wait_ge(sem("o_qn"), m + 1)
                if m:
                    pe.wait_ge(sem("o_rp"), m)
                src = q4[:, m, :] if m < 4 else kv_f[:, 0, CTX:TOK]
                pe.matmul(bank_(5), o_mats[:, 1, :], src, start=True, stop=True).then_inc(sem("o_rot"), 1)

            def odd_pair(i, e):
                pair = lambda per, c: i * (2 * per) + (e * per + c)

                def score(a):
                    hh, j = a // 4, a % 4
                    if a < 2:
                        pe.wait_ge(sem("o_qz_lo"), pair(2, 2))
                    else:
                        pe.wait_ge(sem("o_exp"), pair(8, a - 1))
                    for p_, (qa, kb) in enumerate(PASSES):
                        for c0, n, _ in ALL:
                            keys = k_dup[:, bass.ds(i, 1), kb, c0:c0 + n].rearrange("p a c -> p (a c)")
                            mm = pe.matmul(tile(2 * (a % 2), c0, n), qz[:, hh, qa, j * P:(j + 1) * P], keys,
                                           start=(p_ == 0), stop=(p_ == 2))
                    mm.then_inc(sem("o_s"), 1)

                def turn(a):
                    pe.wait_ge(sem("o_pn"), pair(8, a + 1))
                    if a >= 1:
                        pe.wait_ge(sem("o_pt_lo"), pair(8, a))
                    for kt in range(6):
                        mm = pe.transpose(tile(4, kt * P, P), o_prob[:, a % 2, kt * P:(kt + 1) * P], idm)
                    mm.then_inc(sem("o_tr"), 1)

                def values(hh):
                    pe.wait_ge(sem("o_pt_lo"), pair(8, 4 * hh + 4))
                    if hh == 0:
                        pe.wait_ge(sem("o_vz_lo"), i + 1)
                    for kt in range(6):
                        for p_, (a, b_) in enumerate(PASSES):
                            mm = pe.matmul(bank_(6), o_vz[:, kt, a, hh * VD:hh * VD + P], o_pt[:, kt, b_, :],
                                           start=(hh == 0 and kt == 0 and p_ == 0),
                                           stop=(hh == 1 and kt == 5 and p_ == 2))
                    mm.then_inc(sem("o_pv"), 1)

                score(0)
                score(1)
                for a in range(8):
                    turn(a)
                    if a + 2 < 8:
                        score(a + 2)
                    if a % 4 == 3:
                        values(a // 4)

            pe.wait_ge(consts_in, 16)
            pe.wait_ge(vecs_in, 16 * 15)
            for j in range(2):
                mm = pe.transpose(bank_(0)[:, j * P:(j + 1) * P], vec_in[:, j, :], idm)
            mm.then_inc(vec_t, 1)
            pe.wait_ge(tok_loaded, 32)
            for k in range(KD):
                if k == 0:
                    pe.wait_ge(vecs_ready, 1)
                if k >= 2:
                    pe.wait_ge(x_new, k - 1)
                for j in range(6):
                    mm = pe.transpose(tile(2 * (k % 2), j * P, P), tok_in[:, j, k * P:(k + 1) * P], idm)
                mm.then_inc(tok_t, 1)
            pe.wait_ge(x_new, KD)
            square_x(0, ALL)
            pe.wait_ge(cond_ready, 1)
            for c in range(16):
                modulate(0, c)
            mod_rows(1, 16, 1)
            pe.wait_ge(mod_ready, 1)
            ffn(0, ALL)
            mod_rows(2, 72, 2)
            pe.wait_ge(mod_ready, 2)
            add_squares(0, 8, ALL)
            square_x(1, ALL)
            even_mixer()
            add_squares(1, 16, ALL)
            square_x(2, ALL)
            ffn(2, ALL)
            add_squares(2, 24, ALL)
            square_x(3, ALL)
            ffn(3, ALL)
            add_squares(3, 32, ALL)
            square_x(4, ALL)
            odd_mixer()
            add_squares(4, 40, XONLY)
            square_x(5, XONLY)
            ffn(5, XONLY)
            add_squares(5, 48, XONLY)
            for j in range(4):
                pe.wait_ge(x_new, 56)
                if j >= 2:
                    pe.wait_ge(sem("out_ready"), j - 1)
                for k in range(KD):
                    mm = pe.transpose(bank_(2 + 2 * (j % 2) + k // 4)[:, k % 4 * P:(k % 4 + 1) * P],
                                      x[:, k, CTX + j * P:CTX + (j + 1) * P], idm)
                mm.then_inc(sem("out_t"), 1)

        @block.scalar
        def _(act):
            copy = lambda dst, src: nc.scalar.activation(dst, src, ACT.Copy)

            def split(i, per, c):
                act.wait_ge(w_loaded[c % RAWS], i * (8 * per) + 16 * (c // RAWS + 1))
                if not known(i) or i * per + c >= SLOTS:
                    act.wait_ge(w_done, i * per + (c - SLOTS + 1))
                copy(w_half[0][:, c % SLOTS, :], raw[:, c % RAWS, :]).then_inc(w_hi, 1)

            def split_mod(i, c):
                act.wait_ge(m_loaded[c % MOD_SLOTS], i * (24 * 8) + 16 * (c // MOD_SLOTS + 1))
                if not known(i) or i * 24 + c >= MOD_SLOTS:
                    act.wait_ge(m_done, i * 24 + (c - 1))
                copy(m_half[0][:, c % MOD_SLOTS, :], mod_raw[:, c % MOD_SLOTS, :]).then_inc(m_hi, 1)

            def take_row(i, c):
                act.wait_ge(m_done, i * 24 + (c + 1))
                if c // 8 or not known(i):
                    act.wait_ge(row_stored, i * 48 + 16 * (c // 8))
                copy(mod_row[:, :], ps[0:4, 6 * 512:8 * 512]).then_inc(row_ready, 1)

            def norm(n, src, ra, rb, wait, count):
                act.wait_ge(wait, count)
                nc.scalar.activation(ra, src, ACT.Ln, scale=-2.0, bias=EPS).then_inc(n_ln, 1)
                act.wait_ge(n_ln, n + 1)
                nc.scalar.activation(rb, ra, ACT.Exp, scale=-0.5).then_inc(n_r0, 1)
                act.wait_ge(n_r0, n + 1)
                nc.scalar.activation(ra, rb, ACT.Square).then_inc(n_r2, 1)

            def places(segs):
                return segs[0][0], TOK - segs[0][0]

            def square_x(q, segs):
                c0, n = places(segs)
                for k in range(KD):
                    act.wait_ge(x_new, 8 * q + k + 1)
                    if k >= 2:
                        act.wait_ge(x_sum, 8 * q + k - 1)
                    nc.scalar.activation(sq[:, k % 2, c0:c0 + n], x[:, k, c0:c0 + n], ACT.Square).then_inc(x_sq, 1)

            def pre(q, segs):
                c0, n = places(segs)
                norm(N_PRE[q], tile(2, c0, n), t[:, 0, c0:c0 + n], t[:, 1, c0:c0 + n], x_sum, 8 * q + KD)
                for k in range(KD):
                    act.wait_ge(h_t, 8 * q + k + 1)
                    for c0_, n_, j in segs:
                        ins = nc.scalar.activation(h[:, k, 0, c0_:c0_ + n_], t[:, k % 2, c0_:c0_ + n_], ACT.Identity,
                                                   bias=mod[:, q, 0, k, j:j + 1])
                    ins.then_inc(h_hi, 1)

            def square_y(q, k, segs, n_tiles):
                c0, n = places(segs)
                act.wait_ge(y_done, y_end[q] - n_tiles * (KD - 1 - k))
                if k >= 2:
                    act.wait_ge(y_acc, 8 * q + k - 1)
                nc.scalar.activation(sq[:, k % 2, c0:c0 + n], y[:, k, c0:c0 + n], ACT.Square).then_inc(y_sq, 1)

            def post(q, segs):
                c0, n = places(segs)
                norm(N_POST[q], tile(0, c0, n), t[:, 0, c0:c0 + n], t[:, 1, c0:c0 + n], y_sum, q + 1)

            def ffn(q, segs):
                b, fi = BASE[q], ffn_at[q]
                c0, n = places(segs)

                def up(i, c, t_, m0):
                    for j in range(4):
                        split(i, 12, c + j + 3)
                        if m0 is not None:
                            split_mod(i, m0 + 2 * j)
                            split_mod(i, m0 + 2 * j + 1)
                            if (m0 + 2 * j + 1) % 8 == 7:
                                take_row(i, m0 + 2 * j + 1)
                        f = 22 * fi + 2 * t_ + j // 2
                        if j % 2 == 0:
                            act.wait_ge(w_done, i * 12 + (c + j + 1))
                            act.wait_ge(hid_f, i * 4 + f)
                            nc.scalar.activation(sq[:, 0, c0:c0 + n], tile(0, c0, n), ACT.Silu).then_inc(silu_done, 1)
                        else:
                            act.wait_ge(hid_f, i * 4 + (f + 1))
                            copy(hid[:, t_ % 2, j // 2, 0, c0:c0 + n], sq[:, 1, c0:c0 + n]).then_inc(hid_hi, 1)

                def down(i, c, m0):
                    split(i, 12, c + 3)
                    if m0 is not None:
                        for e in range(4):
                            split_mod(i, m0 + e)
                            if (m0 + e) % 8 == 7:
                                take_row(i, m0 + e)
                    split(i, 12, c + 4)

                up(0, b, 0, 16 if q == 0 else None)
                with act.Fori(0, 5) as i:
                    for half in range(2):
                        m0 = 24 + 12 * half if q == 0 else None
                        up(i, b + 4 + 6 * half, 1 + half, m0)
                        down(i, b + 8 + 6 * half, m0 + 8 if q == 0 else None)
                if q != 5:
                    split(0, 12, b + 64 + 3)
                for k in range(KD):
                    square_y(q, k, segs, len(segs))
                if q != 5:
                    split(0, 12, b + 64 + 4)

            def even_pair(i, e):
                b = BASE[1] + E_PAIR
                pair = lambda per, c: i * (2 * per) + (e * per + c)
                split(i, 4, b + 2 * e + 3)
                for hh in range(2):
                    if hh == 0:
                        act.wait_ge(sem("e_q"), pair(1, 1))
                    else:
                        act.wait_ge(w_done, i * 4 + (b + 2 * e + 1))
                    copy(q_f[0:QK, hh, :], tile(2 * hh, 0, TOK, 0, QK)).then_inc(sem("e_qf"), 1)
                act.wait_ge(w_done, i * 4 + (b + 2 * e + 2))
                for hh in range(2):
                    copy(k_h[0:NOPE, hh, 0, :], tile(4, 0, TOK, hh * NOPE, (hh + 1) * NOPE)).then_inc(sem("e_k_hi"), 1)
                split(i, 4, b + 2 * e + 4)
                for hh in range(2):
                    act.wait_ge(sem("e_qr"), pair(2, hh + 1))
                    copy(q_h[0:QK, hh, 0, :], q_f[0:QK, hh, :]).then_inc(sem("e_q_hi"), 1)
                for hh in range(2):
                    at = act.snap(i * 4 * VD + (2 * e + hh) * VD)
                    copy(e_vz[:, :, 0, 2 * VD * hh:2 * VD * hh + VD], v_all[:, :, bass.ds(at, VD)]).then_inc(sem("e_vz_hi"), 1)
                for s_ in range(14):
                    if s_ >= 2:
                        a = s_ - 2
                        hh, j = a // 6, a % 6
                        act.wait_ge(sem("e_tr"), pair(12, a + 1))
                        if j == 4:
                            act.wait_ge(sem("e_pv"), pair(4, 2 * hh + 1))
                        if a == 6:
                            act.wait_ge(sem("e_pv"), pair(4, 2))
                        kt, q0 = (6, j * P) if j < 4 else (2, (j - 4) * P)
                        copy(pt[:, 0:kt, 0, q0:q0 + P],
                             tile(4, 0, kt * P).rearrange("p (k q) -> p k q", q=P)).then_inc(sem("e_pt_hi"), 1)
                    if s_ < 12:
                        a = s_
                        n = TOK if a % 6 < 4 else CTX
                        act.wait_ge(sem("e_nm"), pair(12, a + 1))
                        if a >= 2:
                            act.wait_ge(sem("e_tr"), pair(12, a - 1))
                        nc.scalar.activation(prob[:, a % 2, 0:n], tile(2 * (a % 2), 0, n), ACT.Exp,
                                             bias=small[:, 2 + a % 2:3 + a % 2], scale=MLA_SCALE,
                                             accum_out=small[:, 4 + a % 2:5 + a % 2]).then_inc(sem("e_exp"), 1)
                at = act.snap(i * 2 + (4 + e))
                act.wait_ge(sem("e_pv"), pair(4, 4))
                for place, c0, n in ((bank_(6), CTX, SEQ), (bank_(7, CTX), 0, CTX)):
                    copy(h[:, bass.ds(at, 1), 0, c0:c0 + n].rearrange("p a c -> p (a c)"), place).then_inc(sem("e_o_hi"), 1)

            def even_mixer():
                b = BASE[1]
                act.wait_ge(x_aside, 16)
                for c in range(8):
                    split(0, 4, b + c + 3)
                    if c % 2 == 0:
                        act.wait_ge(w_done, b + c + 1)
                        if c:
                            act.wait_ge(sem("e_u"), c // 2)
                        nc.scalar.activation(sq[:, 0, :], tile(0), ACT.Sigmoid).then_inc(sem("e_sig"), 1)
                for m in range(6):
                    split(0, 4, b + 8 + m + 3)
                    act.wait_ge(w_done, b + 8 + m + 1)
                    if m < 5:
                        copy(cqkv[:, m, :], tile(2 * (m % 2))).then_inc(sem("e_cf"), 1)
                    else:
                        copy(q_f[NOPE:QK, 0, :], tile(2, 0, TOK, 0, ROPE)).then_inc(sem("e_cf"), 1)
                for m in range(5):
                    act.wait_ge(sem("e_cf"), m + 1)
                    if m >= 2:
                        act.wait_ge(sem("e_csum"), m - 1)
                    else:
                        act.wait_ge(sem("e_u"), 4)
                    nc.scalar.activation(sq[:, m % 2, :], cqkv[:, m, :], ACT.Square).then_inc(sem("e_csq"), 1)
                for g, (place, first, last) in enumerate(((4, 0, KQ), (6, KQ, 5))):
                    norm(N_CQ + g, tile(place), prob[:, 0, :], prob[:, 1, :], sem("e_csum"), last)
                    for m in range(first, last):
                        act.wait_ge(sem("e_ct"), m + 1)
                        copy(cn[:, m, 0, :], cqkv[:, m, :]).then_inc(sem("e_cn_hi"), 1)
                    if g == 0:
                        act.wait_ge(n_rstd, N_CQ + 1)
                act.wait_ge(sem("e_cn_lo"), 5)
                act.wait_ge(sem("e_kr"), 1)
                for hh in range(2):
                    copy(k_h[NOPE:QK, hh, 0, :], q_f[NOPE:QK, 0, :]).then_inc(sem("e_kpe_hi"), 1)
                split(0, 4, b + E_V + 3)
                for j in range(6):
                    if j < 5:
                        act.wait_ge(sem("e_vmm"), j + 1)
                    else:
                        act.wait_ge(w_done, b + E_V + 2)
                    copy(v_all[:, j, :], bank_(2 + j % 2)).then_inc(sem("e_v"), 1)
                split(0, 4, b + E_V + 4)
                act.wait_ge(sem("e_v"), 6)
                act.wait_ge(sem("e_kpe_lo"), 2)
                act.wait_ge(sem("e_zero"), 5)
                with act.Fori(0, 2) as i:
                    for e in range(2):
                        even_pair(i, e)
                for c in range(KC):
                    act.wait_ge(sem("e_d"), c + 1)
                    if c >= 2:
                        act.wait_ge(sem("e_lsum"), KC + c - 1)
                    for c0, n, _ in ALL:
                        g0 = c0 + HALO if c0 else 0
                        ins = nc.scalar.activation(sq[:, c % 2, c0:c0 + n], u[:, c, g0:g0 + n], ACT.Square)
                    ins.then_inc(sem("e_dsq"), 1)
                norm(N_LN, tile(2), prob[:, 0, :], prob[:, 1, :], sem("e_lsum"), 2 * KC)
                for c in range(KC):
                    act.wait_ge(sem("e_lt"), c + 1)
                    nc.scalar.activation(sq[:, c % 2, :], sq[:, c % 2, :], ACT.Silu, scale=vecs[:, V_LNG + c:V_LNG + c + 1],
                                         bias=vecs[:, V_LNB + c:V_LNB + c + 1]).then_inc(sem("e_act"), 1)
                    act.wait_ge(sem("e_act"), c + 1)
                    copy(h[:, c, 0, :], sq[:, c % 2, :]).then_inc(sem("e_ln_hi"), 1)
                for c in range(KD):
                    split(0, 4, b + E_OUT + c + 3)
                    if c == 0:
                        act.wait_ge(sem("e_ln_lo"), KC)
                    square_y(1, c, ALL, 1)

            def odd_mixer():
                b = BASE[4]
                act.wait_ge(x_aside, 32)
                for m in range(10):
                    split(0, 4, b + m + 3)
                    act.wait_ge(w_done, b + m + 1)
                    place = 2 * (m % 2)
                    if m < 4:
                        ins = copy(q4[:, m, :], tile(place, CTX, SEQ))
                    elif m < 6:
                        ins = copy(kv_f[:, m - 4, :], tile(place))
                    else:
                        ins = copy(f4[:, m - 6, :], tile(place, CTX, SEQ))
                    ins.then_inc(sem("o_pf"), 1)
                    if m == 4:
                        act.wait_ge(sem("o_consts"), 32)
                        copy(dft_c[:, 0, :], o_mats[:, 2:4, :].rearrange("p a c -> p (a c)")).then_inc(sem("o_dft_hi"), 1)
                        head_square(0)
                    if m >= 5:
                        norm_head(m - 5)
                        if m < 9:
                            head_square(m - 4)
                split(0, 4, b + O_DFT + 3)
                for g in range(4):
                    act.wait_ge(sem("o_pf"), 7 + g)
                    if g:
                        act.wait_ge(sem("o_ab"), 4 * g)
                    copy(f_h[:, 0, :], f4[:, g, :]).then_inc(sem("o_f_hi"), 1)
                    for j in range(4):
                        act.wait_ge(sem("o_ab"), 4 * g + j + 1)
                        if g:
                            act.wait_ge(sem("o_fn"), g)
                        copy(ab[:, j, 0, :], bank_(2 * (j % 2), 2 * P)).then_inc(sem("o_ab_hi"), 1)
                    if g < 3:
                        act.wait_ge(sem("o_fn"), g + 1)
                    else:
                        act.wait_ge(w_done, b + O_DFT + 4)
                    copy(h[:, 4 + g, 0, CTX:TOK], bank_(4)).then_inc(sem("o_fn_hi"), 1)
                for c in range(1, 4):
                    split(0, 4, b + O_DFT + c + 3)
                act.wait_ge(sem("o_vt"), 1)
                copy(v_t[:, :, :].rearrange("p j c -> p (j c)"), tile(0)).then_inc(sem("o_vtf"), 1)
                act.wait_ge(sem("o_rp"), 5)
                for g in range(GQA_KV):
                    r = slice(g * HD, (g + 1) * HD)
                    copy(k_dup[r, g, 0, :], kv_f[r, 0, :]).then_inc(sem("o_k_hi"), 1)
                act.wait_ge(sem("o_vtf"), 1)
                act.wait_ge(sem("o_zero"), 2)
                with act.Fori(0, 2) as i:
                    at = act.snap(i * HD)
                    for hh in range(2):
                        copy(o_vz[:, :, 0, 2 * VD * hh:2 * VD * hh + VD], v_t[:, :, bass.ds(at, HD)]).then_inc(sem("o_vz_hi"), 1)
                    for e in range(2):
                        odd_pair(i, e)
                for c in range(KD):
                    split(0, 4, b + O_OUT + c + 3)
                    square_y(4, c, XONLY, 1)

            def head_square(m):
                act.wait_ge(sem("o_pf"), m + 1)
                if m >= 2:
                    act.wait_ge(sem("o_qsum"), m - 1)
                n = SEQ if m < 4 else TOK
                src = q4[:, m, :] if m < 4 else kv_f[:, 0, :]
                nc.scalar.activation(sq[:, m % 2, TOK - n:TOK], src, ACT.Square).then_inc(sem("o_qsq"), 1)

            def norm_head(m):
                n = SEQ if m < 4 else TOK
                if m:
                    act.wait_ge(n_rstd, N_Q + m)
                norm(N_Q + m, tile(6, TOK - n, n), o_prob[:, 0, TOK - n:TOK], o_prob[:, 1, TOK - n:TOK],
                     sem("o_qsum"), m + 1)

            def odd_pair(i, e):
                pair = lambda per, c: i * (2 * per) + (e * per + c)
                at = act.snap(i * 2 + e)
                for hh in range(2):
                    r = slice(hh * HD, (hh + 1) * HD)
                    copy(qz[r, hh, 0, :], q4[r, bass.ds(at, 1), :].rearrange("p a c -> p (a c)")).then_inc(sem("o_qz_hi"), 1)
                for s_ in range(10):
                    if s_ >= 2:
                        a = s_ - 2
                        act.wait_ge(sem("o_tr"), pair(8, a + 1))
                        if a == 4:
                            act.wait_ge(sem("o_pv"), pair(2, 1))
                        copy(o_pt[:, :, 0, a % 4 * P:(a % 4 + 1) * P],
                             tile(4).rearrange("p (k q) -> p k q", q=P)).then_inc(sem("o_pt_hi"), 1)
                    if s_ < 8:
                        a = s_
                        act.wait_ge(sem("o_nm"), pair(8, a + 1))
                        if a >= 2:
                            act.wait_ge(sem("o_tr"), pair(8, a - 1))
                        nc.scalar.activation(o_prob[:, a % 2, :], tile(2 * (a % 2)), ACT.Exp,
                                             bias=small[:, 2 + a % 2:3 + a % 2], scale=GQA_SCALE,
                                             accum_out=small[:, 4 + a % 2:5 + a % 2]).then_inc(sem("o_exp"), 1)
                act.wait_ge(sem("o_pv"), pair(2, 2))
                copy(h[:, bass.ds(at, 1), 0, CTX:TOK].rearrange("p a c -> p (a c)"), bank_(6)).then_inc(sem("o_hi"), 1)

            for c in range(3):
                split(0, 4, c)
            act.wait_ge(vecs_ready, 1)
            nc.scalar.activation(cond_f[:, :, :].rearrange("p j k -> p (j k)"), vecs[:, V_C:V_C + 2 * KD],
                                 ACT.Silu).then_inc(cond_f_ready, 1)
            act.wait_ge(cond_f_ready, 1)
            copy(cond[:, :, :, 0].rearrange("p k j -> p j k"), cond_f[:, :, :]).then_inc(cond_hi, 1)
            for k in range(KD):
                act.wait_ge(x_new, k + 1)
                if k >= 2:
                    act.wait_ge(x_sum, k - 1)
                nc.scalar.activation(sq[:, k % 2, :], x[:, k, :], ACT.Square).then_inc(x_sq, 1)
            for c in range(16):
                split_mod(0, c)
                if c % 8 == 7:
                    take_row(0, c)
            pre(0, ALL)
            ffn(0, ALL)
            post(0, ALL)
            square_x(1, ALL)
            pre(1, ALL)
            even_mixer()
            post(1, ALL)
            square_x(2, ALL)
            pre(2, ALL)
            ffn(2, ALL)
            post(2, ALL)
            square_x(3, ALL)
            pre(3, ALL)
            ffn(3, ALL)
            post(3, ALL)
            square_x(4, ALL)
            pre(4, ALL)
            odd_mixer()
            post(4, XONLY)
            square_x(5, XONLY)
            pre(5, XONLY)
            ffn(5, XONLY)
            post(5, XONLY)

        @block.vector
        def _(dve):
            tt, stt, copy = nc.vector.tensor_tensor, nc.vector.scalar_tensor_tensor, nc.vector.tensor_copy

            def f(ap):
                return ap.bitcast(F32)

            def split(i, per, c):
                dve.wait_ge(w_hi, i * per + (c + 1))
                tt(w_half[1][:, c % SLOTS, :], raw[:, c % RAWS, :], f(w_half[0][:, c % SLOTS, :]),
                   ALU.subtract).then_inc(w_lo, 1)

            def split_mod(i, c):
                dve.wait_ge(m_hi, i * 24 + (c + 1))
                tt(m_half[1][:, c % MOD_SLOTS, :], mod_raw[:, c % MOD_SLOTS, :], f(m_half[0][:, c % MOD_SLOTS, :]),
                   ALU.subtract).then_inc(m_lo, 1)

            def norm(n, src, ra, rb, out_):
                dve.wait_ge(n_r2, n + 1)
                stt(ra, src, -0.5 * EPS, ra, ALU.add, ALU.mult).then_inc(n_b, 1)
                dve.wait_ge(n_b, n + 1)
                stt(out_, ra, 1.5, rb, ALU.add, ALU.mult).then_inc(n_rstd, 1)
                dve.wait_ge(n_rstd, n + 1)

            def places(segs):
                return segs[0][0], TOK - segs[0][0]

            def pre(q, segs):
                c0, n = places(segs)
                norm(N_PRE[q], tile(2, c0, n), t[:, 0, c0:c0 + n], t[:, 1, c0:c0 + n], rstd[:, c0:c0 + n])
                for k in range(KD + 1):
                    if k < KD:
                        if k >= 2:
                            dve.wait_ge(h_lo, 8 * q + k - 1)
                        for c0, n, j in segs:
                            ins = stt(t[:, k % 2, c0:c0 + n], x[:, k, c0:c0 + n], coef_pre[:, q, k, j:j + 1],
                                      rstd[:, c0:c0 + n], ALU.mult, ALU.mult)
                        ins.then_inc(h_t, 1)
                    if k >= 1:
                        dve.wait_ge(h_hi, 8 * q + k)
                        for c0, n, j in segs:
                            ins = stt(h[:, k - 1, 1, c0:c0 + n], t[:, (k - 1) % 2, c0:c0 + n], mod[:, q, 0, k - 1, j:j + 1],
                                      f(h[:, k - 1, 0, c0:c0 + n]), ALU.add, ALU.subtract)
                        ins.then_inc(h_lo, 1)

            def add_square(q, k, segs):
                c0, n = places(segs)
                dve.wait_ge(y_sq, 8 * q + k + 1)
                if k == 0:
                    copy(sum_sq[:, c0:c0 + n], sq[:, 0, c0:c0 + n]).then_inc(y_acc, 1)
                else:
                    dve.wait_ge(y_acc, 8 * q + k)
                    tt(sum_sq[:, c0:c0 + n], sum_sq[:, c0:c0 + n], sq[:, k % 2, c0:c0 + n], ALU.add).then_inc(y_acc, 1)

            def post(q, segs):
                c0, n = places(segs)
                norm(N_POST[q], tile(0, c0, n), t[:, 0, c0:c0 + n], t[:, 1, c0:c0 + n], rstd[:, c0:c0 + n])
                for k in range(KD + 1):
                    if k < KD:
                        if k >= 2:
                            dve.wait_ge(x_new, 8 * (q + 1) + k - 1)
                        for c0, n, j in segs:
                            ins = stt(t[:, k % 2, c0:c0 + n], y[:, k, c0:c0 + n], coef_post[:, q, k, j:j + 1],
                                      rstd[:, c0:c0 + n], ALU.mult, ALU.mult)
                        ins.then_inc(y_t, 1)
                    if k >= 1:
                        c0, n = places(segs)
                        dve.wait_ge(y_t, 8 * q + k)
                        tt(x[:, k - 1, c0:c0 + n], x[:, k - 1, c0:c0 + n], t[:, (k - 1) % 2, c0:c0 + n],
                           ALU.add).then_inc(x_new, 1)

            def columns(layers, r, done):
                dve.wait_ge(rows_in, 32 if done == 1 else 96)
                for l in range(layers):
                    tt(m_sum[0:r, l, :, :], m_rows[0:r, l, 0:4:2, :], m_rows[0:r, l, 1:4:2, :], ALU.add).then_inc(rows_sum, 1)
                dve.wait_ge(rows_sum, 1 if done == 1 else 3)
                for l in range(layers):
                    for j in range(2):
                        ins = tt(m_sum[0:r, l, j, :], m_sum[0:r, l, j, :], m_bias[0:r, l, :], ALU.add)
                ins.then_inc(rows_full, 1)
                dve.wait_ge(rows_t, done)
                flat = mod[:, :, :, :, :].rearrange("p q a k j -> p (q a k) j")
                for l in range(layers):
                    for j in range(2):
                        ins = copy(flat[:, 72 * l:72 * l + r, j], bank_(0)[:, (l * 2 + j) * 72:(l * 2 + j) * 72 + r])
                ins.then_inc(mod_ready, 1)
                dve.wait_ge(mod_ready, done)
                gain = lambda at, q0, q1: vecs[:, at:at + 6 * KD].rearrange("p (q k) -> p q k", k=KD)[:, q0:q1, :]
                nq = 1 if done == 1 else 6
                for j in range(2):
                    ins = stt(coef_pre[:, 0:nq, :, j], mod[:, 0:nq, 1, :, j], 1.0, gain(V_GPRE, 0, nq), ALU.add, ALU.mult)
                    if done == 2:
                        for q in range(6):
                            ins = stt(coef_post[:, q, :, j], mod[:, q, 2, :, j], 1.0 if q % 3 == 1 else 0.5,
                                      gain(V_GPOST, q, q + 1).rearrange("p q k -> p (q k)"), ALU.mult, ALU.mult)
                ins.then_inc(coef_ready, 1)
                dve.wait_ge(coef_ready, done)

            def ffn(q, segs):
                b, fi = BASE[q], ffn_at[q]
                c0, n = places(segs)
                nt = KD * len(segs)
                tiles = down_tiles(segs)

                def up(i, c, t_, m0):
                    for j in range(4):
                        split(i, 12, c + j + 3)
                        if m0 is not None:
                            split_mod(i, m0 + 2 * j)
                            split_mod(i, m0 + 2 * j + 1)
                        if j % 2 == 1:
                            hidden = 22 * fi + 2 * t_ + j // 2
                            dve.wait_ge(w_done, i * 12 + (c + j + 1))
                            dve.wait_ge(silu_done, i * 4 + (hidden + 1))
                            dve.wait_ge(hid_lo, i * 4 + hidden)
                            tt(sq[:, 1, c0:c0 + n], sq[:, 0, c0:c0 + n], tile(2, c0, n), ALU.mult).then_inc(hid_f, 1)
                            dve.wait_ge(hid_hi, i * 4 + (hidden + 1))
                            tt(hid[:, t_ % 2, j // 2, 1, c0:c0 + n], sq[:, 1, c0:c0 + n],
                               f(hid[:, t_ % 2, j // 2, 0, c0:c0 + n]), ALU.subtract).then_inc(hid_lo, 1)

                def add_tile(i, c, t_, idx):
                    d, (s0, w, _), place = tiles[idx]
                    if idx < nt - 1:
                        dve.wait_ge(down_done, i * 2 * (nt - 1) + (165 * fi + t_ * (nt - 1) + idx + 1))
                    else:
                        dve.wait_ge(w_done, i * 12 + (c + 2))
                    tt(y[:, d, s0:s0 + w], y[:, d, s0:s0 + w], place, ALU.add).then_inc(y_done, 1)

                def down(i, c, t_, m0):
                    split(i, 12, c + 3)
                    if m0 is not None:
                        split_mod(i, m0)
                        split_mod(i, m0 + 1)
                    for idx in range(nt):
                        add_tile(i, c, t_, idx)
                        if m0 is not None and idx in (7, 11):
                            split_mod(i, m0 + 2 + (idx - 7) // 4)
                    split(i, 12, c + 4)

                up(0, b, 0, 16 if q == 0 else None)
                dve.wait_ge(y_zero, fi + 1)
                with dve.Fori(0, 5) as i:
                    for half in range(2):
                        m0 = 24 + 12 * half if q == 0 else None
                        up(i, b + 4 + 6 * half, 1 + half, m0)
                        down(i, b + 8 + 6 * half, half, m0 + 8 if q == 0 else None)
                if q != 5:
                    split(0, 12, b + 64 + 3)
                for idx in range(nt):
                    add_tile(0, b + 64, 10, idx)
                    d = (idx + 1) // len(segs) - 1
                    if (idx + 1) % len(segs) == 0 and d >= 1:
                        add_square(q, d - 1, segs)
                add_square(q, KD - 1, segs)
                if q != 5:
                    split(0, 12, b + 64 + 4)

            def conv_tap(chunk, count, k):
                src = u[:, bass.ds(chunk, 1), k % CONV_K:k % CONV_K + GAPPED].rearrange("p a c -> p (a c)")
                if k == 0:
                    cw = vecs[:, V_CONVW:V_CONVW + CONV_K * KC].rearrange("p (k c) -> p c k", c=KC)
                    cb = vecs[:, V_CONVB:V_CONVB + KC]
                    if not known(chunk) or chunk > 0:
                        dve.wait_ge(sem("e_conv"), count)
                    copy(taps[:, 0:CONV_K], cw[:, bass.ds(chunk, 1), :].rearrange("p a k -> p (a k)")).then_inc(sem("e_tap"), 1)
                    copy(taps[:, CONV_K:CONV_K + 1], cb[:, bass.ds(chunk, 1)]).then_inc(sem("e_tap"), 1)
                    dve.wait_ge(sem("e_tap"), chunk * 2 + 2)
                    nc.vector.tensor_scalar(sum_sq[:, :], src, taps[:, 0:1], None, ALU.mult).then_inc(sem("e_conv"), 1)
                elif k < CONV_K:
                    dve.wait_ge(sem("e_conv"), count + k)
                    stt(sum_sq[:, :], src, taps[:, k:k + 1], sum_sq[:, :], ALU.mult, ALU.add).then_inc(sem("e_conv"), 1)
                else:
                    dve.wait_ge(sem("e_conv"), count + k)
                    dst = u[:, bass.ds(chunk, 1), 0:GAPPED].rearrange("p a c -> p (a c)")
                    nc.vector.tensor_scalar(dst, sum_sq[:, :], taps[:, CONV_K:CONV_K + 1], None, ALU.add).then_inc(sem("e_conv"), 1)

            def conv(chunk, count, k0, k1):
                for k in range(k0, min(k1, CONV_K + 1)):
                    conv_tap(chunk, count, k)

            def rope(rows, q_ap, rot, tab, tmp, step, count, done):
                tt(tmp, rot, tab[rows, 1, :], ALU.mult).then_inc(step, 1)
                tt(q_ap, q_ap, tab[rows, 0, :], ALU.mult).then_inc(step, 1)
                dve.wait_ge(step, count + 2)
                tt(q_ap, q_ap, tmp, ALU.add).then_inc(done, 1)

            def even_pair(i, e):
                b = BASE[1] + E_PAIR
                pair = lambda per, c: i * (2 * per) + (e * per + c)
                chunk, count = i + 2, i * 32 + 64
                split(i, 4, b + 2 * e + 3)
                r = slice(NOPE, QK)
                for hh in range(2):
                    dve.wait_ge(sem("e_k_hi"), pair(2, hh + 1))
                    tt(k_h[0:NOPE, hh, 1, :], tile(4, 0, TOK, hh * NOPE, (hh + 1) * NOPE), f(k_h[0:NOPE, hh, 0, :]),
                       ALU.subtract).then_inc(sem("e_k_lo"), 1)
                split(i, 4, b + 2 * e + 4)
                for hh in range(2):
                    dve.wait_ge(sem("e_rot"), pair(2, hh + 1))
                    rope(r, q_f[r, hh, CTX:TOK], tile(2 * hh, CTX, SEQ, NOPE, QK), e_rope, sq[r, hh, CTX:TOK],
                         sem("e_qrs"), pair(4, 2 * hh), sem("e_qr"))
                for hh in range(2):
                    dve.wait_ge(sem("e_q_hi"), pair(2, hh + 1))
                    tt(q_h[0:QK, hh, 1, :], q_f[0:QK, hh, :], f(q_h[0:QK, hh, 0, :]), ALU.subtract).then_inc(sem("e_q_lo"), 1)
                at = [dve.snap(i * 4 * VD + (2 * e + hh) * VD) for hh in range(2)]
                for hh in range(2):
                    dve.wait_ge(sem("e_vz_hi"), pair(2, hh + 1))
                    d0 = 2 * VD * hh
                    ins = tt(e_vz[:, :, 1, d0:d0 + VD], v_all[:, :, bass.ds(at[hh], VD)], f(e_vz[:, :, 0, d0:d0 + VD]), ALU.subtract)
                ins.then_inc(sem("e_vz_lo"), 1)
                taps_ = iter(range(16 * e, 16 * e + 16))
                for s_ in range(14):
                    if s_ < 12:
                        a = s_
                        n = TOK if a % 6 < 4 else CTX
                        dve.wait_ge(sem("e_s"), pair(12, a + 1))
                        nc.vector.tensor_reduce(small[:, a % 2:a % 2 + 1], tile(2 * (a % 2), 0, n), AX_X, ALU.max).then_inc(sem("e_mx"), 1)
                        dve.wait_ge(sem("e_mx"), pair(12, a + 1))
                        nc.vector.tensor_scalar(small[:, 2 + a % 2:3 + a % 2], small[:, a % 2:a % 2 + 1], -MLA_SCALE, None,
                                                ALU.mult).then_inc(sem("e_nm"), 1)
                    if 1 <= s_ <= 12:
                        a = s_ - 1
                        dve.wait_ge(sem("e_exp"), pair(12, a + 1))
                        nc.vector.reciprocal(small[:, 6 + a % 2:7 + a % 2], small[:, 4 + a % 2:5 + a % 2]).then_inc(sem("e_ri"), 1)
                    for k in range(1 if s_ < 12 else 2):
                        conv(chunk, count, *(lambda k_: (k_, k_ + 1))(next(taps_)))
                    if s_ >= 2:
                        a = s_ - 2
                        j = a % 6
                        kt, q0 = (6, j * P) if j < 4 else (2, (j - 4) * P)
                        dve.wait_ge(sem("e_pt_hi"), pair(12, a + 1))
                        tt(pt[:, 0:kt, 1, q0:q0 + P], tile(4, 0, kt * P).rearrange("p (k q) -> p k q", q=P),
                           f(pt[:, 0:kt, 0, q0:q0 + P]), ALU.subtract).then_inc(sem("e_pt_lo"), 1)
                dst = dve.snap(i * 2 + (4 + e))
                dve.wait_ge(sem("e_o_hi"), pair(2, 2))
                for place, c0, n in ((bank_(6), CTX, SEQ), (bank_(7, CTX), 0, CTX)):
                    hi, lo = (h[:, bass.ds(dst, 1), g, c0:c0 + n].rearrange("p a c -> p (a c)") for g in range(2))
                    ins = tt(lo, place, f(hi), ALU.subtract)
                ins.then_inc(sem("e_o_lo"), 1)

            def even_mixer():
                b = BASE[1]
                dve.wait_ge(x_aside, 16)
                dve.wait_ge(sem("e_zero"), 3)
                for c in range(8):
                    split(0, 4, b + c + 3)
                    if c % 2 == 1:
                        dve.wait_ge(w_done, b + c + 1)
                        dve.wait_ge(sem("e_sig"), c // 2 + 1)
                        for c0, n, _ in ALL:
                            g0 = c0 + HALO + (HALO if c0 else 0)
                            ins = tt(u[:, c // 2, g0:g0 + n], tile(2, c0, n), sq[:, 0, c0:c0 + n], ALU.mult)
                        ins.then_inc(sem("e_u"), 1)
                dve.wait_ge(sem("e_u"), 4)
                for m in range(6):
                    split(0, 4, b + 8 + m + 3)
                    for g in range(11 * m, min(11 * m + 11, 64)):
                        conv(g // 32, g // 32 * 32, g % 32, g % 32 + 1)
                dve.wait_ge(sem("e_consts"), 32)
                dve.wait_ge(sem("e_krot"), 1)
                r = slice(NOPE, QK)
                rope(r, q_f[r, 0, CTX:TOK], tile(0, CTX, SEQ, NOPE, QK), e_rope, rstd_e[r, 0:SEQ], sem("e_krs"), 0, sem("e_kr"))
                for g, (place, first, last) in enumerate(((4, 0, KQ), (6, KQ, 5))):
                    norm(N_CQ + g, tile(place), prob[:, 0, :], prob[:, 1, :], rstd_e[:, :])
                    for m in range(first, last):
                        gain = vecs[:, V_GCQ + m:V_GCQ + m + 1] if m < KQ else vecs[:, V_GCKV + m - KQ:V_GCKV + m - KQ + 1]
                        stt(cqkv[:, m, :], cqkv[:, m, :], gain, rstd_e[:, :], ALU.mult, ALU.mult).then_inc(sem("e_ct"), 1)
                    for m in range(first, last):
                        dve.wait_ge(sem("e_cn_hi"), m + 1)
                        tt(cn[:, m, 1, :], cqkv[:, m, :], f(cn[:, m, 0, :]), ALU.subtract).then_inc(sem("e_cn_lo"), 1)
                for hh in range(2):
                    dve.wait_ge(sem("e_kpe_hi"), hh + 1)
                    tt(k_h[r, hh, 1, :], q_f[r, 0, :], f(k_h[r, hh, 0, :]), ALU.subtract).then_inc(sem("e_kpe_lo"), 1)
                split(0, 4, b + E_V + 3)
                split(0, 4, b + E_V + 4)
                with dve.Fori(0, 2) as i:
                    for e in range(2):
                        even_pair(i, e)
                for c in range(KC):
                    if c == 0:
                        dve.wait_ge(sem("e_lsum"), KC)
                    for c0, n, _ in ALL:
                        g0 = c0 + HALO if c0 else 0
                        ins = tt(u[:, c, g0:g0 + n], u[:, c, g0:g0 + n], tile(0, c0, n), ALU.subtract)
                    ins.then_inc(sem("e_d"), 1)
                norm(N_LN, tile(2), prob[:, 0, :], prob[:, 1, :], rstd_e[:, :])
                for c in range(KC + 1):
                    if c < KC:
                        if c >= 2:
                            dve.wait_ge(sem("e_ln_lo"), c - 1)
                        for c0, n, _ in ALL:
                            g0 = c0 + HALO if c0 else 0
                            ins = tt(sq[:, c % 2, c0:c0 + n], u[:, c, g0:g0 + n], rstd_e[:, c0:c0 + n], ALU.mult)
                        ins.then_inc(sem("e_lt"), 1)
                    if c >= 1:
                        dve.wait_ge(sem("e_ln_hi"), c)
                        tt(h[:, c - 1, 1, :], sq[:, (c - 1) % 2, :], f(h[:, c - 1, 0, :]), ALU.subtract).then_inc(sem("e_ln_lo"), 1)
                out_tiles(1, b + E_OUT, ALL)
                dve.wait_ge(x_back, 16)

            def out_tiles(q, b, segs):
                c0, n = places(segs)
                for c in range(KD):
                    split(0, 4, b + c + 3)
                    dve.wait_ge(w_done, b + c + 1)
                    copy(y[:, c, c0:c0 + n], tile(2 * (c % 2), c0, n)).then_inc(y_done, 1)
                    if c >= 1:
                        add_square(q, c - 1, segs)
                add_square(q, KD - 1, segs)

            def odd_mixer():
                b = BASE[4]
                dve.wait_ge(x_aside, 32)
                for m in range(10):
                    split(0, 4, b + m + 3)
                    if m == 4:
                        dve.wait_ge(sem("o_dft_hi"), 1)
                        tt(dft_c[:, 1, :], o_mats[:, 2:4, :].rearrange("p a c -> p (a c)"), f(dft_c[:, 0, :]), ALU.subtract).then_inc(sem("o_dftc"), 1)
                    if m >= 5:
                        if m >= 6:
                            head_rope(m - 6)
                        head_gain(m - 5)
                split(0, 4, b + O_DFT + 3)
                for g in range(4):
                    dve.wait_ge(sem("o_f_hi"), g + 1)
                    tt(f_h[:, 1, :], f4[:, g, :], f(f_h[:, 0, :]), ALU.subtract).then_inc(sem("o_f_lo"), 1)
                    for j in range(4):
                        dve.wait_ge(sem("o_ab_hi"), 4 * g + j + 1)
                        tt(ab[:, j, 1, :], bank_(2 * (j % 2), 2 * P), f(ab[:, j, 0, :]), ALU.subtract).then_inc(sem("o_ab_lo"), 1)
                    if g == 1:
                        head_rope(4)
                    dve.wait_ge(sem("o_fn_hi"), g + 1)
                    tt(h[:, 4 + g, 1, CTX:TOK], bank_(4), f(h[:, 4 + g, 0, CTX:TOK]), ALU.subtract).then_inc(sem("o_fn_lo"), 1)
                for c in range(1, 4):
                    split(0, 4, b + O_DFT + c + 3)
                for g in range(GQA_KV):
                    r = slice(g * HD, (g + 1) * HD)
                    dve.wait_ge(sem("o_k_hi"), g + 1)
                    tt(k_dup[r, g, 1, :], kv_f[r, 0, :], f(k_dup[r, g, 0, :]), ALU.subtract).then_inc(sem("o_k_lo"), 1)
                dve.wait_ge(sem("o_k_lo"), 2)
                for g in range(GQA_KV):
                    r, other = slice(g * HD, (g + 1) * HD), slice((1 - g) * HD, (2 - g) * HD)
                    for a in range(2):
                        copy(k_dup[other, g, a, :], f(k_dup[r, g, a, :])).then_inc(sem("o_kd"), 1)
                with dve.Fori(0, 2) as i:
                    at = dve.snap(i * HD)
                    for hh in range(2):
                        dve.wait_ge(sem("o_vz_hi"), i * 2 + (hh + 1))
                        d0 = 2 * VD * hh
                        ins = tt(o_vz[:, :, 1, d0:d0 + VD], v_t[:, :, bass.ds(at, HD)], f(o_vz[:, :, 0, d0:d0 + VD]), ALU.subtract)
                    ins.then_inc(sem("o_vz_lo"), 1)
                    for e in range(2):
                        odd_pair(i, e)
                out_tiles(4, b + O_OUT, XONLY)
                dve.wait_ge(x_back, 32)

            def head_gain(m):
                n = SEQ if m < 4 else TOK
                norm(N_Q + m, tile(6, TOK - n, n), o_prob[:, 0, TOK - n:TOK], o_prob[:, 1, TOK - n:TOK], rstd_o[:, TOK - n:TOK])
                x_ = q4[:, m, :] if m < 4 else kv_f[:, 0, :]
                g = V_GQN if m < 4 else V_GKN
                stt(x_, x_, vecs[:, g:g + 1], rstd_o[:, TOK - n:TOK], ALU.mult, ALU.mult).then_inc(sem("o_qn"), 1)

            def head_rope(m):
                dve.wait_ge(sem("o_rot"), m + 1)
                x_ = q4[:, m, :] if m < 4 else kv_f[:, 0, CTX:TOK]
                rope(slice(0, P), x_, bank_(5), o_rope, sum_sq[:, 0:SEQ], sem("o_rps"), 2 * m, sem("o_rp"))

            def odd_pair(i, e):
                pair = lambda per, c: i * (2 * per) + (e * per + c)
                at = dve.snap(i * 2 + e)
                for hh in range(2):
                    r = slice(hh * HD, (hh + 1) * HD)
                    dve.wait_ge(sem("o_qz_hi"), pair(2, hh + 1))
                    tt(qz[r, hh, 1, :], q4[r, bass.ds(at, 1), :].rearrange("p a c -> p (a c)"), f(qz[r, hh, 0, :]),
                       ALU.subtract).then_inc(sem("o_qz_lo"), 1)
                for s_ in range(10):
                    if s_ < 8:
                        a = s_
                        dve.wait_ge(sem("o_s"), pair(8, a + 1))
                        nc.vector.tensor_reduce(small[:, a % 2:a % 2 + 1], tile(2 * (a % 2)), AX_X, ALU.max).then_inc(sem("o_mx"), 1)
                        dve.wait_ge(sem("o_mx"), pair(8, a + 1))
                        nc.vector.tensor_scalar(small[:, 2 + a % 2:3 + a % 2], small[:, a % 2:a % 2 + 1], -GQA_SCALE, None,
                                                ALU.mult).then_inc(sem("o_nm"), 1)
                    if 1 <= s_ <= 8:
                        a = s_ - 1
                        dve.wait_ge(sem("o_exp"), pair(8, a + 1))
                        nc.vector.reciprocal(small[:, 6 + a % 2:7 + a % 2], small[:, 4 + a % 2:5 + a % 2]).then_inc(sem("o_ri"), 1)
                    if s_ >= 2:
                        a = s_ - 2
                        dve.wait_ge(sem("o_pt_hi"), pair(8, a + 1))
                        q0 = a % 4 * P
                        tt(o_pt[:, :, 1, q0:q0 + P], tile(4).rearrange("p (k q) -> p k q", q=P),
                           f(o_pt[:, :, 0, q0:q0 + P]), ALU.subtract).then_inc(sem("o_pt_lo"), 1)
                dve.wait_ge(sem("o_hi"), pair(1, 1))
                hi, lo = (h[:, bass.ds(at, 1), g, CTX:TOK].rearrange("p a c -> p (a c)") for g in range(2))
                tt(lo, bank_(6), f(hi), ALU.subtract).then_inc(sem("o_lo"), 1)

            dve.wait_ge(vec_t, 1)
            copy(vecs[:, :], bank_(0)[:, 0:2 * P]).then_inc(vecs_ready, 1)
            for c in range(3):
                split(0, 4, c)
            dve.wait_ge(cond_hi, 1)
            tt(cond[:, :, :, 1].rearrange("p k j -> p j k"), cond_f[:, :, :],
               f(cond[:, :, :, 0]).rearrange("p k j -> p j k"), ALU.subtract).then_inc(cond_ready, 1)
            for k in range(KD):
                dve.wait_ge(tok_t, k + 1)
                copy(x[:, k, :], tile(2 * (k % 2))).then_inc(x_new, 1)
            for c in range(16):
                split_mod(0, c)
            columns(1, 16, 1)
            pre(0, ALL)
            ffn(0, ALL)
            columns(2, 72, 2)
            post(0, ALL)
            pre(1, ALL)
            even_mixer()
            post(1, ALL)
            pre(2, ALL)
            ffn(2, ALL)
            post(2, ALL)
            pre(3, ALL)
            ffn(3, ALL)
            post(3, ALL)
            pre(4, ALL)
            odd_mixer()
            post(4, XONLY)
            pre(5, XONLY)
            ffn(5, XONLY)
            post(5, XONLY)
            for j in range(4):
                dve.wait_ge(sem("out_t"), j + 1)
                copy(tok_in[:, j, :], ps[:, (2 + 2 * (j % 2)) * 512:(4 + 2 * (j % 2)) * 512]).then_inc(sem("out_ready"), 1)


_INS = ['x', 'c', 'ctx', 'c_ctx', 'w_mod', 'b_mod', 'g_pre', 'g_post', 'ffn_w_gate', 'ffn_w_up', 'ffn_w_down',
        'ev_w_in', 'ev_conv_w', 'ev_conv_b', 'ev_ln_g', 'ev_ln_b', 'ev_g_cq', 'ev_w_uq', 'ev_g_ckv', 'ev_w_ukv',
        'ev_w_out', 'od_w_in', 'od_g_qn', 'od_g_kn', 'od_w_out']


def kernel(**inputs):
    import numpy as _np
    import concourse.bacc as _bacc
    from concourse import mybir as _mybir
    from concourse.bass_utils import run_bass_kernel_spmd as _run

    nc = _bacc.Bacc("TRN2", target_bir_lowering=False, num_devices=1)
    arrays, args = {}, []
    given = {name: _np.ascontiguousarray(inputs[name]) for name in _INS}
    given["consts"], given["dft"] = constant_array(), dft_array()
    for name, a in given.items():
        arrays[f"in_{name}_dram"] = a
        args.append(nc.dram_tensor(f"in_{name}_dram", a.shape, _mybir.dt.from_np(a.dtype), kind="ExternalInput").ap())
    args.append(nc.dram_tensor("out_dram", (1, SEQ, D), _mybir.dt.float32, kind="ExternalOutput").ap())
    trunk(nc, *args)
    r = _run(nc, [arrays], core_ids=[0])
    return r.results[0]["out_dram"]
```

```python
from contextlib import ExitStack

import numpy as np

import concourse.bass as bass
from concourse import mybir

F32 = mybir.dt.float32
F32R = mybir.dt.float32r
ACT = mybir.ActivationFunctionType
ALU = mybir.AluOpType
AX_X = mybir.AxisListType.X

P = 128
D = 1024
KD = D // P
CTX, SEQ = 256, 512
TOK = CTX + SEQ
EPS = 1e-6
D_FF = 2816
FT = D_FF // P
STEPS = FT // 2
CHUNK = 1024
RAWS, SLOTS = 2, 4
MOD_SLOTS = 2
UNITS = 18
SEG_C, SEG_X = (0, CTX, 1), (CTX, SEQ, 0)
ALL, XONLY = (SEG_C, SEG_X), (SEG_X,)

CONV_CH, CONV_K = 512, 31
KC = CONV_CH // P
HALO = CONV_K // 2
GAPPED = CTX + HALO + SEQ
PADDED = GAPPED + 2 * HALO
HEADS, NOPE, ROPE, VD = 8, 64, 32, 64
QK = NOPE + ROPE
Q_LORA, KV_LORA = 384, 256
KQ, KKV = Q_LORA // P, KV_LORA // P
MLA_SCALE = QK ** -0.5
GQA_HEADS, GQA_KV, HD = 8, 2, 64
GQA_SCALE = HD ** -0.5
GRID_W = 64
ROPE_THETA = 10000.0

FFN_CHUNKS = 3 * FT
E_IN, E_V, E_PAIR, E_OUT = 0, 14, 16, 24
E_CHUNKS = 32
O_IN, O_DFT, O_OUT = 0, 10, 14
O_CHUNKS = 22
BASE = {0: 0, 1: FFN_CHUNKS, 2: FFN_CHUNKS + E_CHUNKS, 3: 2 * FFN_CHUNKS + E_CHUNKS,
        4: 3 * FFN_CHUNKS + E_CHUNKS, 5: 3 * FFN_CHUNKS + E_CHUNKS + O_CHUNKS}

V_GPRE, V_GPOST, V_C, V_CCTX, V_CONVB, V_LNG, V_LNB, V_GCQ = 0, 48, 96, 104, 112, 116, 120, 124
V_CONVW, V_GCKV, V_GQN, V_GKN = 128, 252, 254, 255

C_ID, C_N1024, C_N384, C_N256, C_N512, C_P96, C_B64, C_P128, C_DFT = (P * i for i in range(9))
C_MROPE = C_DFT + 2 * P
C_GROPE = C_MROPE + 2 * SEQ
C_END = C_GROPE + 2 * SEQ


def rope_rows(rot_dim):
    nf = rot_dim // 4
    inv = ROPE_THETA ** (-np.arange(nf, dtype=np.float32) / np.float32(nf))
    row = np.repeat(np.arange(SEQ // GRID_W), GRID_W).astype(np.float32)
    col = np.tile(np.arange(GRID_W), SEQ // GRID_W).astype(np.float32)
    cos, sin, swap = [], [], []
    for axis, place in enumerate((row, col)):
        for half in range(2):
            for f in range(nf):
                ang = place * inv[f]
                cos.append(np.cos(ang))
                sin.append(np.sin(ang))
                d = (axis * 2 + half) * nf + f
                swap.append((d, (axis * 2 + 1 - half) * nf + f, 1.0 if half else -1.0))
    return np.array(cos, np.float32), np.array(sin, np.float32), swap


def constant_array():
    k = np.zeros((P, C_END), np.float32)
    k[:, C_ID:C_ID + P] = np.eye(P)
    for at, v in ((C_N1024, -0.5 / D), (C_N384, -0.5 / Q_LORA), (C_N256, -0.5 / KV_LORA),
                  (C_N512, -0.5 / CONV_CH)):
        k[:, at:at + P] = v
    cos, sin, swap = rope_rows(ROPE)
    for d, s, sign in swap:
        k[NOPE + s, C_P96 + NOPE + d] = sign
    k[NOPE:QK, C_MROPE:C_MROPE + SEQ] = cos
    k[NOPE:QK, C_MROPE + SEQ:C_MROPE + 2 * SEQ] = sin
    cos, sin, swap = rope_rows(HD)
    for h in range(2):
        k[h * HD:(h + 1) * HD, C_B64 + h * HD:C_B64 + (h + 1) * HD] = -0.5 / HD
        for d, s, sign in swap:
            k[h * HD + s, C_P128 + h * HD + d] = sign
        k[h * HD:(h + 1) * HD, C_GROPE:C_GROPE + SEQ] = cos
        k[h * HD:(h + 1) * HD, C_GROPE + SEQ:C_GROPE + 2 * SEQ] = sin
    a = 2 * np.pi * (np.outer(np.arange(P), np.arange(P)) % P) / P
    k[:, C_DFT:C_DFT + P] = np.cos(a) / np.sqrt(P)
    k[:, C_DFT + P:C_DFT + 2 * P] = np.sin(a) / np.sqrt(P)
    return k


def dft_array():
    a = 2 * np.pi * (np.outer(np.arange(SEQ), np.arange(SEQ)) % SEQ) / SEQ
    return np.concatenate([np.cos(a), -np.sin(a)], axis=1).astype(np.float32) / np.float32(np.sqrt(SEQ))


def trunk(nc, x_in, c_in, ctx_in, c_ctx_in, w_mod, b_mod, g_pre, g_post, w_gate, w_up, w_down,
          ev_w_in, conv_w, conv_b, ln_g, ln_b, g_cq, w_uq, g_ckv, w_ukv, ev_w_out,
          od_w_in, g_qn, g_kn, od_w_out, consts, dft, out):
    mod_scratch = nc.dram_tensor("mod_scratch", (UNITS * 8, 4, P), F32).ap()
    x_scratch = nc.dram_tensor("x_scratch", (P, KD, TOK), F32).ap()
    ctx = ExitStack()
    names = {}

    def sb(stack, name, shape, dt=F32):
        return stack.enter_context(nc.sbuf_tensor(name, shape, dt))

    def sem(name):
        if name not in names:
            names[name] = ctx.enter_context(nc.semaphore(name))
        return names[name]

    with ctx:
        h = sb(ctx, "h", [P, KD, 2, TOK], F32R)
        raw = sb(ctx, "raw", [P, RAWS, CHUNK])
        w_half = [sb(ctx, "w_hi", [P, SLOTS, CHUNK], F32R), sb(ctx, "w_lo", [P, SLOTS, CHUNK], F32R)]
        sq = sb(ctx, "sq", [P, 2, TOK])
        sum_sq = sb(ctx, "sum_sq", [P, GAPPED])
        ident = sb(ctx, "ident", [P, 2 * P])
        vecs = sb(ctx, "vecs", [P, 2 * P])
        mod = sb(ctx, "mod", [P, 6, 3, KD, 2])
        coef_pre = sb(ctx, "coef_pre", [P, 6, KD, 2])
        coef_post = sb(ctx, "coef_post", [P, 6, KD, 2])
        small = sb(ctx, "small", [P, 10])
        n1024 = ident[:, P:2 * P]
        idm = ident[:, 0:P]
        with ExitStack() as s:
            x = sb(s, "x", [P, KD, TOK])
            y = sb(s, "y", [P, KD, TOK])
            hid = sb(s, "hid", [P, 2, 2, 2, TOK], F32R)
            mod_raw = sb(s, "mod_raw", [P, MOD_SLOTS, CHUNK])
            m_half = [sb(s, "m_hi", [P, MOD_SLOTS, CHUNK], F32R), sb(s, "m_lo", [P, MOD_SLOTS, CHUNK], F32R)]
            mod_row = sb(s, "mod_row", [4, CHUNK])
            cond = sb(s, "cond", [P, KD, 2, 2], F32R)
        with ExitStack() as s:
            sb(s, "x_", [P, KD, TOK])
            sb(s, "y_", [P, KD, TOK])
            t = sb(s, "t", [P, 2, TOK])
            rstd = sb(s, "rstd", [P, TOK])
            sb(s, "pad_", [P, TOK])
            fin = sb(s, "fin", [P, 14, P])
        m_rows = fin[:, 0:8, :].rearrange("r (l s) c -> r l s c", l=2)
        m_sum = fin[:, 8:12, :].rearrange("r (l j) c -> r l j c", l=2)
        m_bias = fin[:, 12:14, :]
        with ExitStack() as s:
            sb(s, "x__", [P, KD, TOK])
            tok_in = sb(s, "tok_in", [P, TOK // P, D])
            sb(s, "t__", [P, 3, TOK])
            vec_in = sb(s, "vec_in", [P, 2, P])
            cond_f = sb(s, "cond_f", [P, 2, KD])
        with ExitStack() as s:
            u = sb(s, "u", [P, KC, PADDED])
            cn = sb(s, "cn", [P, KQ + KKV, 2, TOK], F32R)
            v_all = sb(s, "v_all", [P, TOK // P, HEADS * VD])
            e_vh = sb(s, "e_vh", [P, TOK // P, 2, 2 * VD], F32R)
            prob = sb(s, "prob", [P, 2, TOK])
            q_f = sb(s, "q_f", [P, 2, TOK])
            e_diag = sb(s, "e_diag", [P, 2, P])
            e_mats = sb(s, "e_mats", [P, C_B64 - C_N384])
            e_rope = sb(s, "e_rope", [P, 2, SEQ])
            conv_tap = sb(s, "conv_tap", [P, GAPPED])
            with ExitStack() as s2:
                q_h = sb(s2, "q_h", [P, 2, 2, TOK], F32R)
                k_h = sb(s2, "k_h", [P, 2, 2, TOK], F32R)
            with ExitStack() as s2:
                cqkv = sb(s2, "cqkv", [P, KQ + KKV, TOK])
                rstd_e = sb(s2, "rstd_e", [P, TOK])
                conv_sum = sb(s2, "conv_sum", [P, GAPPED])
        pt = h[:, 0:4, :, :].rearrange("p a b c -> p (a b c)").rearrange("p (r k g q) -> p r k g q", r=2, k=6, g=2)
        with ExitStack() as s:
            q4 = sb(s, "q4", [P, 4, SEQ])
            kv_f = sb(s, "kv_f", [P, 2, TOK])
            o_rope = sb(s, "o_rope", [P, 2, SEQ])
            o_mats = sb(s, "o_mats", [P, 4, P])
            dft_c = sb(s, "dft_c", [P, 2, 2 * P], F32R)
            k_dup = sb(s, "k_dup", [P, GQA_KV, 2, TOK], F32R)
            v_t = sb(s, "v_t", [P, TOK // P, P])
            o_vh = sb(s, "o_vh", [P, TOK // P, 2, HD], F32R)
            o_diag = sb(s, "o_diag", [P, 2, P])
            o_prob = sb(s, "o_prob", [P, 2, TOK])
            rstd_o = sb(s, "rstd_o", [P, TOK])
            qz = sb(s, "qz", [P, 2, 2, SEQ], F32R)
            with ExitStack() as s2:
                f4 = sb(s2, "f4", [P, 4, SEQ])
                f_h = sb(s2, "f_h", [P, 2, SEQ], F32R)
                ab = sb(s2, "ab", [P, 4, 2, 2 * P], F32R)
            with ExitStack() as s2:
                o_pt = sb(s2, "o_pt", [P, 2, TOK // P, 2, 2 * P], F32R)

        ps = ctx.enter_context(nc.psum_tensor("ps", [P, 8 * 512], F32))

        def tile(bank, c0=0, n=TOK, r0=0, r1=P):
            return ps[r0:r1, bank * 512 + 256 + c0:bank * 512 + 256 + c0 + n]

        def bank_(b, n=512, r0=0, r1=P):
            return ps[r0:r1, b * 512:b * 512 + n]

        w_loaded = [sem(f"w_loaded{j}") for j in range(RAWS)]
        w_hi, w_lo, w_done = sem("w_hi"), sem("w_lo"), sem("w_done")
        m_loaded = [sem(f"m_loaded{j}") for j in range(MOD_SLOTS)]
        m_hi, m_lo, m_done = sem("m_hi"), sem("m_lo"), sem("m_done")
        row_ready, row_stored = sem("row_ready"), sem("row_stored")
        block = ctx.enter_context(nc.Block())

        def cols(w, at, width):
            return w.rearrange("(k p) c -> p k c", p=P)[:, :, bass.ds(at, width)]

        PASSES = ((0, 0), (0, 1), (1, 0))

        def known(i):
            return isinstance(i, int)

        def down_tiles(q, segs):
            banks = (0, 1, 4, 5) if q == 0 else (4, 5, 6, 7)
            order = [(d, seg) for d in range(KD) for seg in segs]
            return [(d, seg, bank_(banks[n % 4], seg[1])) for n, (d, seg) in enumerate(order)]

        class Mixer:
            def __init__(self, m, contexts, prob_, pt_, vh, vh_at, diag, out_at, qc0):
                self.m, self.prob, self.pt, self.vh, self.vh_at, self.diag = m, prob_, pt_, vh, vh_at, diag
                self.out_at, self.qc0 = out_at, qc0
                self.groups = [(hh, c, n) for hh in range(2) for c, n in (
                    [(CTX, 6), (CTX + 2 * P, 6)] + ([(0, 2)] if contexts else []))]
                self.tiles = [(g, c + j * P, n) for g, (_, c, n) in enumerate(self.groups) for j in range(2)]
                self.halves = [(a, k0, min(3, n - k0)) for a, (_, _, n) in enumerate(self.tiles) for k0 in range(0, n, 3)]
                self.n_t, self.n_g, self.n_h = len(self.tiles), len(self.groups), len(self.halves)

            def sem(self, name):
                return sem(self.m + name)

            def of_tile(self, a):
                return [n for n, (t_, _, _) in enumerate(self.halves) if t_ == a]

        EVEN = Mixer("e_", True, prob, pt, e_vh, VD, e_diag, 4, 0)
        ODD = Mixer("o_", False, o_prob, o_pt, o_vh, 0, o_diag, 0, CTX)
        turned = lambda n, kn: bank_(4 + n % 3, kn * P)
        pv_place, inv_place = bank_(7, 2 * P, 0, VD), bank_(0, 2 * P, 0, VD)

        ffn_at = {0: 0, 2: 1, 3: 2, 5: 3}
        N_PRE = {0: 0, 1: 2, 2: 7, 3: 9, 4: 11, 5: 18}
        N_POST = {0: 1, 1: 6, 2: 8, 3: 10, 4: 17, 5: 19}
        N_CQ, N_CKV, N_LN, N_Q, N_K = 3, 4, 5, 12, 16
        x_new, x_sq, x_sum = sem("x_new"), sem("x_sq"), sem("x_sum")
        h_t, h_hi, h_lo = sem("h_t"), sem("h_hi"), sem("h_lo")
        y_zero, y_done, y_sq, y_acc, y_sum, y_t = (sem(n) for n in ("y_zero", "y_done", "y_sq", "y_acc", "y_sum", "y_t"))
        n_ln, n_r0, n_r2, n_b, n_rstd = (sem(n) for n in ("n_ln", "n_r0", "n_r2", "n_b", "n_rstd"))
        silu_done, hid_f, hid_hi, hid_lo, down_done = (sem(n) for n in ("silu_done", "hid_f", "hid_hi", "hid_lo", "down_done"))
        consts_in, vecs_in, tok_loaded = sem("consts_in"), sem("vecs_in"), sem("tok_loaded")
        vec_t, vecs_ready, cond_f_ready, cond_hi, cond_ready = (sem(n) for n in ("vec_t", "vecs_ready", "cond_f_ready", "cond_hi", "cond_ready"))
        tok_t = sem("tok_t")
        rows_in, rows_sum, rows_full, rows_t, mod_ready, coef_ready = (
            sem(n) for n in ("rows_in", "rows_sum", "rows_full", "rows_t", "mod_ready", "coef_ready"))
        y_base = {0: 4, 1: 180, 2: 188, 3: 364, 4: 540, 5: 548}
        y_end = {0: 180, 1: 188, 2: 364, 3: 540, 4: 548, 5: 636}
        x_aside, x_back = sem("x_aside"), sem("x_back")

        @block.sync
        def _(sp):
            def load(i, per, c, src, k, n):
                if not known(i) or i * per + c >= RAWS:
                    sp.wait_ge(w_lo, i * per + (c - 1))
                dst = raw[:, c % RAWS, 0:k * n]
                if k > 1:
                    dst = dst.rearrange("p (k c) -> p k c", k=k)
                sp.dma_start(dst, src).then_inc(w_loaded[c % RAWS], 16)

            def ffn(q, l, s):
                b = BASE[q]
                gate, up, down = w_gate[l, s], w_up[l, s], w_down[l, s]

                def up_chunk(i, c, w, f):
                    at = f * P if known(i) else sp.snap(f * P)
                    load(i, 12, c, cols(w, at, P), KD, P)

                def down_chunk(i, c, f):
                    at = f * P if known(i) else sp.snap(f * P)
                    load(i, 12, c, down[bass.ds(at, P), :], 1, CHUNK)

                for j in range(4):
                    up_chunk(0, b + j, (gate, up)[j % 2], j // 2)
                with sp.Fori(0, 5) as i:
                    for half in range(2):
                        c0 = b + 4 + 6 * half
                        for j in range(6):
                            if j < 4:
                                up_chunk(i, c0 + j, (gate, up)[j % 2], i * 4 + (2 + 2 * half + j // 2))
                            else:
                                down_chunk(i, c0 + j, i * 4 + (2 * half + j - 4))
                for j in range(2):
                    down_chunk(0, b + 64 + j, FT - 2 + j)
                if q == 5:
                    down_chunk(0, b + 66, 0)

            def set_aside(n, ready):
                sp.wait_ge(x_new, ready)
                sp.dma_start(x_scratch, x[:, :, :]).then_inc(x_aside, 16)

            def even_mixer():
                b = BASE[1]
                def in_tiles(i):
                    for c in range(4):
                        load(0, 4, b + 4 * i + c, cols(ev_w_in[0], (2 * i + c // 2) * P + (1 - c % 2) * CONV_CH, P), KD, P)
                in_tiles(0)
                set_aside(0, 16)
                sp.wait_ge(h_lo, 16)
                sp.wait_ge(x_aside, 16)
                sp.dma_start(e_mats[:, :], consts[:, C_N384:C_B64]).then_inc(sem("e_consts"), 16)
                sp.dma_start(e_rope[:, :, :], consts[:, C_MROPE:C_MROPE + 2 * SEQ].rearrange(
                    "p (a t) -> p a t", a=2)).then_inc(sem("e_consts"), 16)
                in_tiles(1)
                for m in range(KQ + KKV):
                    load(0, 4, b + 8 + m, cols(ev_w_in[0], 2 * CONV_CH + m * P, P), KD, P)
                load(0, 4, b + 13, cols(ev_w_in[0], 2 * CONV_CH + Q_LORA + KV_LORA, ROPE), KD, ROPE)
                for k in range(KKV):
                    load(0, 4, b + E_V + k, w_ukv[0][k * P:(k + 1) * P, :], 1, CHUNK)
                with sp.Fori(0, 2) as i:
                    for e in range(2):
                        at = sp.snap(i * 4 * QK + e * 2 * QK)
                        load(i, 4, b + E_PAIR + 2 * e, cols(w_uq[0], at, 2 * QK), KQ, 2 * QK)
                        at = sp.snap(i * 4 + 2 * e)
                        keys = [w_ukv[0][k * P:(k + 1) * P, :].rearrange("p (h d) -> p h d", h=HEADS)[
                            :, bass.ds(at, 2), 0:NOPE] for k in range(KKV)]
                        c = b + E_PAIR + 2 * e + 1
                        done = sp.snap(i * 32 + 16 * (e + 1))
                        sp.wait_ge(w_lo, i * 4 + (c - 1))
                        for k in range(KKV):
                            if k == 1:
                                sp.wait_ge(sem("e_ukv"), done)
                            sp.dma_start(raw[:, c % RAWS, k * P:(k + 1) * P].rearrange("p (h d) -> p h d", h=2),
                                         keys[k]).then_inc(w_loaded[c % RAWS] if k else sem("e_ukv"), 16)
                out_chunk = lambda i, c: load(i, 4, b + E_OUT + c, cols(ev_w_out[0], i * 4 * P + c * P if known(i)
                                              else sp.snap(i * 4 * P + c * P), P), KD, P)
                for c in range(4):
                    out_chunk(0, c)
                sp.wait_ge(sem("e_ln_lo"), KC)
                sp.dma_start(x[:, :, :], x_scratch).then_inc(x_back, 16)
                for c in range(4, 8):
                    out_chunk(0, c)

            def odd_mixer():
                b = BASE[4]
                in_tiles = lambda m0, m1: [load(0, 4, b + m, cols(od_w_in[0], m * P, P), KD, P) for m in range(m0, m1)]
                in_tiles(0, 4)
                set_aside(1, 40)
                sp.wait_ge(h_lo, 40)
                sp.wait_ge(x_aside, 32)
                for dst, at, n in ((o_mats[:, :, :], C_B64, 4 * P), (o_rope[:, :, :], C_GROPE, 2 * SEQ)):
                    sp.dma_start(dst, consts[:, at:at + n].rearrange("p (a t) -> p a t", a=dst.shape[1])).then_inc(
                        sem("o_consts"), 16)
                in_tiles(4, 10)
                for j in range(4):
                    load(0, 4, b + O_DFT + j, dft[j * P:(j + 1) * P, :], 1, CHUNK)
                out_chunk = lambda c: load(0, 4, b + O_OUT + c, cols(od_w_out[0], c * P, P), KD, P)
                for c in range(4):
                    out_chunk(c)
                sp.wait_ge(sem("o_lo"), 4 * ODD.n_g)
                sp.dma_start(x[:, :, :], x_scratch).then_inc(x_back, 16)
                for c in range(4, 8):
                    out_chunk(c)

            sp.dma_start(ident[:, :], consts[:, C_ID:C_N384]).then_inc(consts_in, 16)
            for row, src in ((V_GPRE, g_pre.rearrange("l s (k p) -> (l s k) p", p=P)),
                             (V_GPOST, g_post.rearrange("l s (k p) -> (l s k) p", p=P)),
                             (V_C, c_in.rearrange("b (k p) -> (b k) p", p=P)),
                             (V_CCTX, c_ctx_in.rearrange("(k p) -> k p", p=P)),
                             (V_CONVB, conv_b.rearrange("b (k p) -> (b k) p", p=P)),
                             (V_LNG, ln_g.rearrange("b (k p) -> (b k) p", p=P)),
                             (V_LNB, ln_b.rearrange("b (k p) -> (b k) p", p=P)),
                             (V_GCQ, g_cq.rearrange("b (k p) -> (b k) p", p=P)),
                             (127, g_cq.rearrange("b (k p) -> (b k) p", p=P)[0:1, :])):
                sp.dma_start(vec_in[row:row + src.shape[0], 0, :], src).then_inc(vecs_in, 16)
            for row, src, at, n in ((0, conv_w.rearrange("b k (c p) -> (b k c) p", p=P), 0, P),
                                    (124, g_ckv.rearrange("b (k p) -> (b k) p", p=P), 0, P),
                                    (126, g_qn, 0, HD), (126, g_qn, HD, HD), (127, g_kn, 0, HD), (127, g_kn, HD, HD)):
                sp.dma_start(vec_in[row:row + src.shape[0], 1, at:at + n], src).then_inc(vecs_in, 16)
            sp.dma_start(tok_in[:, 0:2, :], ctx_in[0].rearrange("(j p) d -> p j d", p=P)).then_inc(tok_loaded, 16)
            sp.dma_start(tok_in[:, 2:6, :], x_in[0].rearrange("(j p) d -> p j d", p=P)).then_inc(tok_loaded, 16)
            ffn(0, 0, 0)
            even_mixer()
            ffn(2, 0, 1)
            ffn(3, 1, 0)
            odd_mixer()
            ffn(5, 1, 1)
            for j in range(4):
                sp.wait_ge(sem("out_ready"), j + 1)
                sp.dma_start(out[0, j * P:(j + 1) * P, :], tok_in[:, j, :]).then_inc(sem("out_stored"), 16)
            sp.wait_ge(sem("out_stored"), 64)

        @block.gpsimd
        def _(pool):
            def load_mod(i, c, layer, unit, k):
                blocks = w_mod.rearrange("l r (u c) -> (l r u) c", c=CHUNK)
                b0 = layer * (9 * D - 9) + (unit + 9 * P * k)
                if not known(i):
                    b0 = pool.snap(b0)
                if not known(i) or i * 24 + c >= MOD_SLOTS:
                    pool.wait_ge(m_lo, i * 24 + (c - 1))
                pool.dma_start(mod_raw[:, c % MOD_SLOTS, :], blocks[bass.ds(b0, P, 9), :]).then_inc(
                    m_loaded[c % MOD_SLOTS], 16)

            def store_row(i, u):
                at = 8 * u if known(i) else pool.snap(i * 24 + 8 * u)
                pool.wait_ge(row_ready, i * 3 + (u + 1))
                pool.dma_start(mod_scratch[bass.ds(at, 8)].rearrange("a s c -> s a c"),
                               mod_row[:, :].rearrange("s (a c) -> s a c", c=P)).then_inc(row_stored, 16)

            def zero_y(ready):
                pool.wait_ge(x_new, ready)
                nc.gpsimd.memset(y[:, :, :], 0.0).then_inc(y_zero, 1)

            for c in range(16):
                load_mod(0, c, 0, c // 8, c % 8)
                if c == 9:
                    store_row(0, 0)
            store_row(0, 1)
            pool.wait_ge(row_stored, 32)
            pool.dma_start(m_rows[0:16, 0, :, :], mod_scratch[0:16]).then_inc(rows_in, 16)
            pool.dma_start(m_bias[0:16, 0, :], b_mod[0].rearrange("(r c) -> r c", c=P)[0:16, :]).then_inc(rows_in, 16)
            for k in range(8):
                load_mod(0, 16 + k, 0, 2, k)
            with pool.Fori(0, 5) as i:
                for m in range(24):
                    load_mod(i, 24 + m, (i + 1) // 3, i * 3 + (3 + m // 8), m % 8)
                    if m % 8 == 1:
                        store_row(i, 2 + m // 8)
            store_row(0, UNITS - 1)
            pool.wait_ge(row_stored, 16 * UNITS)
            pool.wait_ge(mod_ready, 1)
            pool.wait_ge(w_done, 64)
            for l in range(2):
                pool.dma_start(m_rows[0:72, l, :, :], mod_scratch[72 * l:72 * l + 72]).then_inc(rows_in, 16)
                pool.dma_start(m_bias[0:72, l, :], b_mod[l].rearrange("(r c) -> r c", c=P)).then_inc(rows_in, 16)
            pool.wait_ge(x_aside, 16)
            pool.wait_ge(h_lo, 16)
            for at, n in ((0, HALO), (HALO + CTX, HALO), (HALO + GAPPED, HALO)):
                nc.gpsimd.memset(u[:, :, at:at + n], 0.0).then_inc(sem("e_zero"), 1)
            nc.gpsimd.memset(q_f[0:NOPE, 0, :], 0.0).then_inc(sem("e_zero"), 1)
            for c in range(2, KC):
                pool.wait_ge(sem("e_u"), c + 1)
                for k in range(CONV_K + 1):
                    n, m = (c - 2) * (CONV_K + 1) + k, (c - 2) * (CONV_K - 1) + k
                    src = u[:, c, k % CONV_K:k % CONV_K + GAPPED]
                    tap = vecs[:, V_CONVW + k * KC + c:V_CONVW + k * KC + c + 1]
                    if n:
                        pool.wait_ge(sem("e_conv_b"), n)
                    if k == 0:
                        ins = nc.gpsimd.tensor_scalar(sum_sq[:, :], src, tap, None, ALU.mult)
                    elif k < CONV_K:
                        nc.gpsimd.tensor_scalar(conv_tap[:, :], src, tap, None, ALU.mult).then_inc(sem("e_tap"), 1)
                        pool.wait_ge(sem("e_tap"), m)
                        ins = nc.gpsimd.tensor_tensor(sum_sq[:, :], sum_sq[:, :], conv_tap[:, :], ALU.add)
                    else:
                        ins = nc.gpsimd.tensor_scalar(u[:, c, 0:GAPPED], sum_sq[:, :],
                                                      vecs[:, V_CONVB + c:V_CONVB + c + 1], None, ALU.add)
                    ins.then_inc(sem("e_conv_b"), 1)
            zero_y(24)
            zero_y(32)
            pool.wait_ge(x_aside, 32)
            pool.wait_ge(h_lo, 40)
            nc.gpsimd.memset(qz[:, :, :, :].bitcast(F32), 0.0).then_inc(sem("o_zero"), 1)
            zero_y(48)

        @block.tensor
        def _(pe):
            def weight(half, c, k, width, at=0, m=P):
                return w_half[half][:, c % SLOTS, k * width + at:k * width + at + m]

            def modulate(i, c):
                pe.wait_ge(m_lo, i * 24 + (c + 1))
                k = c % 8
                if k == 0 and (not known(i) or c > 0):
                    pe.wait_ge(row_ready, i * 3 + c // 8)
                for n in range(2):
                    for half in range(2):
                        mm = pe.matmul(bank_(6 + n, 512, 0, 4), cond[:, k, :, :].rearrange("p j h -> p (j h)"),
                                       m_half[half][:, c % MOD_SLOTS, n * 512:(n + 1) * 512],
                                       start=(k == 0 and half == 0), stop=(k == 7 and half == 1))
                mm.then_inc(m_done, 1)

            def project(i, per, c, place, segs, width=P, h_ready=None, mods=(), korder=range(KD), waits=None):
                pe.wait_ge(w_lo, i * per + (c + 1))
                for at, k in enumerate(korder):
                    if h_ready is not None:
                        pe.wait_ge(h_lo, h_ready + k + 1)
                    if waits is not None:
                        waits(k)
                    for p_, (a, b_) in enumerate(PASSES):
                        for c0, n, _ in segs:
                            mm = pe.matmul(tile(place, c0, n, 0, width), weight(a, c, k, width, 0, width),
                                           h[:, k, b_, c0:c0 + n], start=(at == 0 and p_ == 0),
                                           stop=(at == KD - 1 and p_ == 2))
                    if at == 3 and mods:
                        modulate(i, mods[0])
                mm.then_inc(w_done, 1)
                if mods:
                    modulate(i, mods[1])

            def ffn(q, segs):
                b, fi = BASE[q], ffn_at[q]
                nt = KD * len(segs)
                tiles = down_tiles(q, segs)
                y0, d0 = y_base[q], 165 * fi

                def up(i, c, t, first, m0):
                    if q == 0 and not first:
                        pe.wait_ge(y_done, i * 2 * nt + (y0 + (t - 1) * nt - 2))
                    for j in range(4):
                        if j % 2 == 0:
                            pe.wait_ge(silu_done, i * 4 + (22 * fi + 2 * t + j // 2))
                        else:
                            pe.wait_ge(hid_f, i * 4 + (22 * fi + 2 * t + j // 2))
                        project(i, 12, c + j, 2 * (j % 2), segs, h_ready=8 * q if first and j == 0 else None,
                                mods=(m0 + 2 * j, m0 + 2 * j + 1) if m0 is not None else ())

                def down(i, c, t, m0):
                    pe.wait_ge(w_lo, i * 12 + (c + 2))
                    pe.wait_ge(hid_lo, i * 4 + (22 * fi + 2 * t + 2))
                    if q == 0:
                        pe.wait_ge(silu_done, i * 4 + (22 * fi + min(2 * t + 4, 22)))
                    for idx, (d, (c0, n, _), place) in enumerate(tiles):
                        if idx >= 4 or known(i):
                            pe.wait_ge(y_done, i * 2 * nt + (y0 + t * nt + idx - 3))
                        for kk in range(2):
                            for p_, (a, b_) in enumerate(PASSES):
                                mm = pe.matmul(place, w_half[a][:, (c + kk) % SLOTS, d * P:(d + 1) * P],
                                               hid[:, t % 2, kk, b_, c0:c0 + n],
                                               start=(kk == 0 and p_ == 0), stop=(kk == 1 and p_ == 2))
                            if idx == nt - 1:
                                mm.then_inc(w_done, 1)
                        if idx < nt - 1:
                            mm.then_inc(down_done, 1)
                        if m0 is not None and idx % 4 == 3:
                            modulate(i, m0 + idx // 4)

                up(0, b, 0, True, 16 if q == 0 else None)
                with pe.Fori(0, 5) as i:
                    for half in range(2):
                        m0 = 24 + 12 * half if q == 0 else None
                        up(i, b + 4 + 6 * half, 1 + half, False, m0)
                        down(i, b + 8 + 6 * half, half, m0 + 8 if q == 0 else None)
                down(0, b + 64, 10, None)

            def add_squares(n, done, segs):
                pe.wait_ge(y_acc, done)
                for c0, w, _ in segs:
                    mm = pe.matmul(tile(0, c0, w), n1024, sum_sq[:, c0:c0 + w], start=True, stop=True)
                mm.then_inc(y_sum, 1)

            def square_x(q, segs):
                for k in range(KD):
                    pe.wait_ge(x_sq, 8 * q + k + 1)
                    for c0, w, _ in segs:
                        mm = pe.matmul(tile(2, c0, w), n1024, sq[:, k % 2, c0:c0 + w],
                                       start=(k == 0), stop=(k == KD - 1))
                    mm.then_inc(x_sum, 1)

            def mod_rows(units_l, r, done):
                pe.wait_ge(rows_full, done)
                for l in range(units_l):
                    for j in range(2):
                        mm = pe.transpose(bank_(0)[:, (l * 2 + j) * 72:(l * 2 + j) * 72 + r],
                                          m_sum[0:r, l, j, :], idm[0:r, 0:r])
                mm.then_inc(rows_t, 1)

            def even_pair(i, e):
                b = BASE[1] + E_PAIR
                pair = lambda per, c: i * (2 * per) + (e * per + c)
                pe.wait_ge(w_lo, i * 4 + (b + 2 * e + 2))
                for hh in range(2):
                    for k in range(KQ):
                        for p_, (a, b_) in enumerate(PASSES):
                            for c0, n, _ in ALL:
                                mm = pe.matmul(tile(2 * hh, c0, n, 0, QK), weight(a, b + 2 * e, k, 2 * QK, hh * QK, QK),
                                               cn[:, k, b_, c0:c0 + n], start=(k == 0 and p_ == 0),
                                               stop=(k == KQ - 1 and p_ == 2))
                    mm.then_inc(sem("e_q") if hh == 0 else w_done, 1)
                for k in range(KKV):
                    for p_, (a, b_) in enumerate(PASSES):
                        for c0, n, _ in ALL:
                            mm = pe.matmul(tile(4, c0, n), weight(a, b + 2 * e + 1, k, P), cn[:, KQ + k, b_, c0:c0 + n],
                                           start=(k == 0 and p_ == 0), stop=(k == KKV - 1 and p_ == 2))
                mm.then_inc(w_done, 1)
                for hh in range(2):
                    pe.wait_ge(sem("e_qf"), pair(2, hh + 1))
                    pe.matmul(tile(2 * hh, CTX, SEQ, 0, QK), e_mats[0:QK, C_P96 - C_N384:C_P96 - C_N384 + QK],
                              q_f[0:QK, hh, CTX:TOK], start=True, stop=True).then_inc(sem("e_rot"), 1)

                def product(a):
                    g, col, keys = EVEN.tiles[a]
                    hh = EVEN.groups[g][0]
                    if a < 2:
                        pe.wait_ge(sem("e_q_lo"), pair(2, 2))
                        pe.wait_ge(sem("e_k_lo"), pair(2, 2))
                    for p_, (qa, kb) in enumerate(PASSES):
                        for c0, n, _ in (ALL if keys == 6 else (SEG_C,)):
                            mm = pe.matmul(tile(2 * (a % 2), c0, n), q_h[0:QK, hh, qa, col:col + P],
                                           k_h[0:QK, hh, kb, c0:c0 + n], start=(p_ == 0), stop=(p_ == 2))
                    return mm

                pe.wait_ge(sem("e_k_lo"), pair(2, 2))
                pe.wait_ge(sem("e_vh_lo"), pair(1, 1))
                attention(EVEN, pair, product)

            def attention(mx, pair, product):
                def score(a):
                    if a >= 2:
                        pe.wait_ge(mx.sem("exp"), pair(mx.n_t, a - 1))
                    product(a).then_inc(mx.sem("s"), 1)

                def turn(a):
                    pe.wait_ge(mx.sem("exp"), pair(mx.n_t, a + 1))
                    for n in mx.of_tile(a):
                        _, k0, kn = mx.halves[n]
                        if n >= 3:
                            pe.wait_ge(mx.sem("pt_lo"), pair(mx.n_h, n - 2))
                        for k in range(kn):
                            mm = pe.transpose(turned(n, kn)[:, k * P:(k + 1) * P],
                                              mx.prob[:, a % 2, (k0 + k) * P:(k0 + k + 1) * P], idm)
                        mm.then_inc(mx.sem("tr"), 1)

                def inverse(g):
                    pe.wait_ge(mx.sem("dg"), pair(mx.n_g, g + 1))
                    pe.matmul(inv_place, n1024[:, 0:VD], mx.diag[:, :, :].rearrange("p a c -> p (a c)"),
                              start=True, stop=True).then_inc(mx.sem("inv"), 1)

                def values(g, part):
                    hh, _, keys = mx.groups[g]
                    if part == 0 and g >= 1:
                        pe.wait_ge(mx.sem("of"), pair(mx.n_g, g))
                    if part == 1:
                        pe.wait_ge(mx.sem("inv_out"), pair(mx.n_g, g + 1))
                    per = (keys + 1) // 2
                    last = mx.of_tile(2 * g + 1)[min(part, len(mx.of_tile(2 * g + 1)) - 1)]
                    pe.wait_ge(mx.sem("pt_lo"), pair(mx.n_h, last + 1))
                    at = hh * mx.vh_at
                    for kt in range(part * per, part * per + per):
                        for p_, (a, b_) in enumerate(PASSES):
                            mm = pe.matmul(pv_place, mx.vh[:, kt, a, at:at + VD], mx.pt[:, g % 2, kt, b_, :],
                                           start=(kt == 0 and p_ == 0), stop=(kt == keys - 1 and p_ == 2))
                    if part == 1:
                        mm.then_inc(mx.sem("pv"), 1)

                score(0)
                score(1)
                for a in range(mx.n_t):
                    turn(a)
                    if a >= 2 and a % 2 == 0:
                        inverse(a // 2 - 1)
                    if a + 2 < mx.n_t:
                        score(a + 2)
                    if a >= 2:
                        values(a // 2 - 1, a % 2)
                inverse(mx.n_g - 1)
                values(mx.n_g - 1, 0)
                values(mx.n_g - 1, 1)

            def even_mixer():
                b = BASE[1]
                for c in range(8):
                    if c >= 2:
                        pe.wait_ge(sem("e_u" if c % 2 else "e_sig"), c // 2)
                    project(0, 4, b + c, 2 * (c % 2), ALL, h_ready=8 if c == 0 else None)
                for m in range(6):
                    if m == 0:
                        pe.wait_ge(sem("e_sig"), 4)
                    elif m == 1:
                        pe.wait_ge(sem("e_u"), 4)
                    else:
                        pe.wait_ge(sem("e_cf"), m - 1)
                    project(0, 4, b + 8 + m, 2 * (m % 2), ALL, width=P if m < 5 else ROPE)
                pe.wait_ge(sem("e_consts"), 32)
                for m in range(5):
                    pe.wait_ge(sem("e_csq"), m + 1)
                    at = (C_N384 if m < KQ else C_N256) - C_N384
                    for c0, n, _ in ALL:
                        mm = pe.matmul(tile(4 if m < KQ else 6, c0, n),
                                       e_mats[:, at:at + P], sq[:, m % 2, c0:c0 + n],
                                       start=(m in (0, KQ)), stop=(m in (KQ - 1, 4)))
                    mm.then_inc(sem("e_csum"), 1)
                pe.wait_ge(sem("e_cf"), 6)
                pe.wait_ge(sem("e_zero"), 4)
                pe.matmul(tile(0, CTX, SEQ, 0, QK), e_mats[0:QK, C_P96 - C_N384:C_P96 - C_N384 + QK],
                          q_f[0:QK, 0, CTX:TOK], start=True, stop=True).then_inc(sem("e_krot"), 1)
                pe.wait_ge(w_lo, b + E_V + 2)
                pe.wait_ge(sem("e_cn_lo"), 5)
                for j in range(6):
                    if j >= 2:
                        pe.wait_ge(sem("e_v"), j - 1)
                    for k in range(KKV):
                        for p_, (a, b_) in enumerate(PASSES):
                            v_cols = w_half[b_][:, (b + E_V + k) % SLOTS, :].rearrange(
                                "p (h d) -> p h d", d=NOPE + VD)[:, :, NOPE:NOPE + VD]
                            mm = pe.matmul(bank_(2 + j % 2).rearrange("p (h d) -> p h d", d=VD),
                                           cn[:, KQ + k, a, j * P:(j + 1) * P], v_cols,
                                           start=(k == 0 and p_ == 0), stop=(k == KKV - 1 and p_ == 2))
                        if j == 5:
                            mm.then_inc(w_done, 1)
                    if j < 5:
                        mm.then_inc(sem("e_vmm"), 1)
                pe.wait_ge(sem("e_kpe_lo"), 2)
                pe.wait_ge(sem("e_v"), 6)
                with pe.Fori(0, 2) as i:
                    for e in range(2):
                        even_pair(i, e)
                for n_ in range(2):
                    for c in range(KC):
                        if n_ == 0:
                            pe.wait_ge(sem("e_conv_a" if c < 2 else "e_conv_b"), (CONV_K + 1) * (c % 2 + 1))
                        else:
                            pe.wait_ge(sem("e_dsq"), c + 1)
                        for c0, n, _ in ALL:
                            at = (C_N256, C_N512)[n_] - C_N384
                            g0 = c0 + HALO if c0 else 0
                            src = u[:, c, g0:g0 + n] if n_ == 0 else sq[:, c % 2, c0:c0 + n]
                            mm = pe.matmul(tile(2 * n_, c0, n), e_mats[:, at:at + P], src,
                                           start=(c == 0), stop=(c == KC - 1))
                        mm.then_inc(sem("e_lsum"), 1)
                def attn_then_conv(k):
                    if k >= 4:
                        pe.wait_ge(sem("e_lo"), 4 * EVEN.n_g)
                    else:
                        pe.wait_ge(sem("e_ln_lo"), k + 1)
                for c in range(KD):
                    if c < 2:
                        pe.wait_ge(n_rstd, N_LN + 1)
                    else:
                        pe.wait_ge(y_done, y_base[1] + c - 1)
                    project(0, 4, b + E_OUT + c, 2 * (c % 2), ALL, korder=(4, 5, 6, 7, 0, 1, 2, 3),
                            waits=attn_then_conv if c == 0 else None)

            def odd_mixer():
                b = BASE[4]
                for m in range(10):
                    segs = ALL if m in (4, 5) else XONLY
                    if m >= 2:
                        pe.wait_ge(sem("o_pf"), m - 1)
                    project(0, 4, b + m, 2 * (m % 2), segs, h_ready=32 if m == 0 else None)
                    if m == 4:
                        pe.wait_ge(sem("o_consts"), 32)
                    if 6 <= m:
                        head_swap(m - 6)
                    if 5 <= m:
                        head_sum(m - 5)
                pe.wait_ge(sem("o_dftc"), 1)
                pe.wait_ge(w_lo, b + O_DFT + 4)
                for g in range(4):
                    pe.wait_ge(sem("o_f_lo"), g + 1)
                    for j in range(4):
                        if g * 4 + j >= 2:
                            pe.wait_ge(sem("o_ab_lo"), g * 4 + j - 1)
                        elif g == 0:
                            pe.wait_ge(sem("o_pf"), 10)
                        for p_, (a, b_) in enumerate(PASSES):
                            mm = pe.matmul(bank_(2 * (j % 2), 2 * P), f_h[:, a, j * P:(j + 1) * P], dft_c[:, b_, :],
                                           start=(p_ == 0), stop=(p_ == 2))
                        mm.then_inc(sem("o_ab"), 1)
                    if g == 1:
                        head_swap(4)
                    if g >= 1:
                        pe.wait_ge(sem("o_fn_lo"), g)
                    pe.wait_ge(sem("o_ab_lo"), 4 * g + 4)
                    for j in range(4):
                        for t_ in range(2):
                            for p_, (a, b_) in enumerate(PASSES):
                                mm = pe.matmul(bank_(4), ab[:, j, a, t_ * P:(t_ + 1) * P],
                                               w_half[b_][:, (b + O_DFT + j) % SLOTS, t_ * 512:(t_ + 1) * 512],
                                               start=(j == 0 and t_ == 0 and p_ == 0), stop=(j == 3 and t_ == 1 and p_ == 2))
                        if g == 3:
                            mm.then_inc(w_done, 1)
                    if g < 3:
                        mm.then_inc(sem("o_fn"), 1)
                pe.wait_ge(sem("o_ab_lo"), 16)
                for j in range(6):
                    mm = pe.transpose(tile(0, j * P, P), kv_f[:, 1, j * P:(j + 1) * P], idm)
                mm.then_inc(sem("o_vt"), 1)
                pe.wait_ge(sem("o_kd"), 4)
                pe.wait_ge(sem("o_vtf"), 1)
                with pe.Fori(0, 2) as i:
                    for e in range(2):
                        odd_pair(i, e)
                for c in range(KD):
                    if c < 2:
                        pe.wait_ge(sem("o_lo"), 4 * ODD.n_g)
                    else:
                        pe.wait_ge(y_done, y_base[4] + c - 1)
                    project(0, 4, b + O_OUT + c, 2 * (c % 2), XONLY)

            def head_sum(m):
                pe.wait_ge(sem("o_qsq"), m + 1)
                if m:
                    pe.wait_ge(n_rstd, N_Q + m)
                for c0, w, _ in (XONLY if m < 4 else ALL):
                    mm = pe.matmul(tile(6, c0, w), o_mats[:, 0, :], sq[:, m % 2, c0:c0 + w], start=True, stop=True)
                mm.then_inc(sem("o_qsum"), 1)

            def head_swap(m):
                pe.wait_ge(sem("o_qn"), m + 1)
                if m:
                    pe.wait_ge(sem("o_rp"), m)
                src = q4[:, m, :] if m < 4 else kv_f[:, 0, CTX:TOK]
                pe.matmul(bank_(5), o_mats[:, 1, :], src, start=True, stop=True).then_inc(sem("o_rot"), 1)

            def odd_pair(i, e):
                pair = lambda per, c: i * (2 * per) + (e * per + c)

                def product(a):
                    g, col, _ = ODD.tiles[a]
                    hh = ODD.groups[g][0]
                    if a < 2:
                        pe.wait_ge(sem("o_qz_lo"), pair(2, 2))
                    for p_, (qa, kb) in enumerate(PASSES):
                        for c0, n, _ in ALL:
                            keys = k_dup[:, bass.ds(i, 1), kb, c0:c0 + n].rearrange("p a c -> p (a c)")
                            mm = pe.matmul(tile(2 * (a % 2), c0, n), qz[:, hh, qa, col - CTX:col - CTX + P], keys,
                                           start=(p_ == 0), stop=(p_ == 2))
                    return mm

                pe.wait_ge(sem("o_vh_lo"), i + 1)
                attention(ODD, pair, product)

            pe.wait_ge(consts_in, 16)
            pe.wait_ge(vecs_in, 16 * 15)
            for j in range(2):
                mm = pe.transpose(bank_(0)[:, j * P:(j + 1) * P], vec_in[:, j, :], idm)
            mm.then_inc(vec_t, 1)
            pe.wait_ge(tok_loaded, 32)
            for k in range(KD):
                if k == 0:
                    pe.wait_ge(vecs_ready, 1)
                if k >= 2:
                    pe.wait_ge(x_new, k - 1)
                for j in range(6):
                    mm = pe.transpose(tile(2 * (k % 2), j * P, P), tok_in[:, j, k * P:(k + 1) * P], idm)
                mm.then_inc(tok_t, 1)
            pe.wait_ge(x_new, KD)
            square_x(0, ALL)
            pe.wait_ge(cond_ready, 1)
            for c in range(16):
                modulate(0, c)
            mod_rows(1, 16, 1)
            pe.wait_ge(mod_ready, 1)
            ffn(0, ALL)
            mod_rows(2, 72, 2)
            pe.wait_ge(mod_ready, 2)
            add_squares(0, 8, ALL)
            square_x(1, ALL)
            even_mixer()
            add_squares(1, 16, ALL)
            square_x(2, ALL)
            ffn(2, ALL)
            add_squares(2, 24, ALL)
            square_x(3, ALL)
            ffn(3, ALL)
            add_squares(3, 32, ALL)
            square_x(4, ALL)
            odd_mixer()
            add_squares(4, 40, XONLY)
            square_x(5, XONLY)
            ffn(5, XONLY)
            add_squares(5, 48, XONLY)
            for j in range(4):
                pe.wait_ge(x_new, 56)
                if j >= 2:
                    pe.wait_ge(sem("out_ready"), j - 1)
                for k in range(KD):
                    mm = pe.transpose(bank_(2 + 2 * (j % 2) + k // 4)[:, k % 4 * P:(k % 4 + 1) * P],
                                      x[:, k, CTX + j * P:CTX + (j + 1) * P], idm)
                mm.then_inc(sem("out_t"), 1)

        @block.scalar
        def _(act):
            copy = lambda dst, src: nc.scalar.activation(dst, src, ACT.Copy)

            def split(i, per, c):
                act.wait_ge(w_loaded[c % RAWS], i * (8 * per) + 16 * (c // RAWS + 1))
                if not known(i) or i * per + c >= SLOTS:
                    act.wait_ge(w_done, i * per + (c - SLOTS + 1))
                copy(w_half[0][:, c % SLOTS, :], raw[:, c % RAWS, :]).then_inc(w_hi, 1)

            def split_mod(i, c):
                act.wait_ge(m_loaded[c % MOD_SLOTS], i * (24 * 8) + 16 * (c // MOD_SLOTS + 1))
                if not known(i) or i * 24 + c >= MOD_SLOTS:
                    act.wait_ge(m_done, i * 24 + (c - 1))
                copy(m_half[0][:, c % MOD_SLOTS, :], mod_raw[:, c % MOD_SLOTS, :]).then_inc(m_hi, 1)

            def take_row(i, c):
                act.wait_ge(m_done, i * 24 + (c + 1))
                if c // 8 or not known(i):
                    act.wait_ge(row_stored, i * 48 + 16 * (c // 8))
                copy(mod_row[:, :], ps[0:4, 6 * 512:8 * 512]).then_inc(row_ready, 1)

            def norm(n, src, ra, rb, wait, count):
                act.wait_ge(wait, count)
                nc.scalar.activation(ra, src, ACT.Ln, scale=-2.0, bias=EPS).then_inc(n_ln, 1)
                act.wait_ge(n_ln, n + 1)
                nc.scalar.activation(rb, ra, ACT.Exp, scale=-0.5).then_inc(n_r0, 1)
                act.wait_ge(n_r0, n + 1)
                nc.scalar.activation(ra, rb, ACT.Square).then_inc(n_r2, 1)

            def places(segs):
                return segs[0][0], TOK - segs[0][0]

            def square_x(q, segs):
                c0, n = places(segs)
                for k in range(KD):
                    act.wait_ge(x_new, 8 * q + k + 1)
                    if k >= 2:
                        act.wait_ge(x_sum, 8 * q + k - 1)
                    nc.scalar.activation(sq[:, k % 2, c0:c0 + n], x[:, k, c0:c0 + n], ACT.Square).then_inc(x_sq, 1)

            def pre(q, segs):
                c0, n = places(segs)
                norm(N_PRE[q], tile(2, c0, n), t[:, 0, c0:c0 + n], t[:, 1, c0:c0 + n], x_sum, 8 * q + KD)
                for k in range(KD):
                    act.wait_ge(h_t, 8 * q + k + 1)
                    for c0_, n_, j in segs:
                        ins = nc.scalar.activation(h[:, k, 0, c0_:c0_ + n_], t[:, k % 2, c0_:c0_ + n_], ACT.Identity,
                                                   bias=mod[:, q, 0, k, j:j + 1])
                    ins.then_inc(h_hi, 1)

            def square_y(q, k, segs, n_tiles):
                c0, n = places(segs)
                act.wait_ge(y_done, y_end[q] - n_tiles * (KD - 1 - k))
                if k >= 2:
                    act.wait_ge(y_acc, 8 * q + k - 1)
                nc.scalar.activation(sq[:, k % 2, c0:c0 + n], y[:, k, c0:c0 + n], ACT.Square).then_inc(y_sq, 1)

            def post(q, segs):
                c0, n = places(segs)
                norm(N_POST[q], tile(0, c0, n), t[:, 0, c0:c0 + n], t[:, 1, c0:c0 + n], y_sum, q + 1)

            def ffn(q, segs):
                b, fi = BASE[q], ffn_at[q]
                c0, n = places(segs)

                def up(i, c, t_, m0):
                    for j in range(4):
                        split(i, 12, c + j + 3)
                        if m0 is not None:
                            split_mod(i, m0 + 2 * j)
                            split_mod(i, m0 + 2 * j + 1)
                            if (m0 + 2 * j + 1) % 8 == 7:
                                take_row(i, m0 + 2 * j + 1)
                        f = 22 * fi + 2 * t_ + j // 2
                        if j % 2 == 0:
                            act.wait_ge(w_done, i * 12 + (c + j + 1))
                            act.wait_ge(hid_f, i * 4 + f)
                            nc.scalar.activation(sq[:, 0, c0:c0 + n], tile(0, c0, n), ACT.Silu).then_inc(silu_done, 1)
                        else:
                            act.wait_ge(hid_f, i * 4 + (f + 1))
                            copy(hid[:, t_ % 2, j // 2, 0, c0:c0 + n], sq[:, 1, c0:c0 + n]).then_inc(hid_hi, 1)

                def down(i, c, m0):
                    split(i, 12, c + 3)
                    if m0 is not None:
                        for e in range(4):
                            split_mod(i, m0 + e)
                            if (m0 + e) % 8 == 7:
                                take_row(i, m0 + e)
                    split(i, 12, c + 4)

                up(0, b, 0, 16 if q == 0 else None)
                with act.Fori(0, 5) as i:
                    for half in range(2):
                        m0 = 24 + 12 * half if q == 0 else None
                        up(i, b + 4 + 6 * half, 1 + half, m0)
                        down(i, b + 8 + 6 * half, m0 + 8 if q == 0 else None)
                if q != 5:
                    split(0, 12, b + 64 + 3)
                for k in range(KD):
                    square_y(q, k, segs, len(segs))
                if q != 5:
                    split(0, 12, b + 64 + 4)

            def even_pair(i, e):
                b = BASE[1] + E_PAIR
                pair = lambda per, c: i * (2 * per) + (e * per + c)
                split(i, 4, b + 2 * e + 3)
                for hh in range(2):
                    if hh == 0:
                        act.wait_ge(sem("e_q"), pair(1, 1))
                    else:
                        act.wait_ge(w_done, i * 4 + (b + 2 * e + 1))
                    nc.scalar.activation(q_f[0:QK, hh, :], tile(2 * hh, 0, TOK, 0, QK), ACT.Copy,
                                         scale=MLA_SCALE).then_inc(sem("e_qf"), 1)
                act.wait_ge(w_done, i * 4 + (b + 2 * e + 2))
                for hh in range(2):
                    copy(k_h[0:NOPE, hh, 0, :], tile(4, 0, TOK, hh * NOPE, (hh + 1) * NOPE)).then_inc(sem("e_k_hi"), 1)
                split(i, 4, b + 2 * e + 4)
                for hh in range(2):
                    act.wait_ge(sem("e_qr"), pair(2, hh + 1))
                    copy(q_h[0:QK, hh, 0, :], q_f[0:QK, hh, :]).then_inc(sem("e_q_hi"), 1)
                at = act.snap(i * 4 * VD + 2 * e * VD)
                copy(e_vh[:, :, 0, :], v_all[:, :, bass.ds(at, 2 * VD)]).then_inc(sem("e_vh_hi"), 1)
                attention(EVEN, i, e, pair)

            def attention(mx, i, e, pair):
                at = act.snap(i * 2 + (mx.out_at + e))
                for s_ in range(mx.n_t + 5):
                    if 0 <= s_ - 2 < mx.n_t:
                        a = s_ - 2
                        g = a // 2
                        for n in mx.of_tile(a):
                            _, k0, kn = mx.halves[n]
                            act.wait_ge(mx.sem("tr"), pair(mx.n_h, n + 1))
                            if g >= 2 and a % 2 == 0 and k0 == 0:
                                act.wait_ge(mx.sem("pv"), pair(mx.n_g, g - 1))
                            copy(mx.pt[:, g % 2, k0:k0 + kn, 0, a % 2 * P:(a % 2 + 1) * P],
                                 turned(n, kn).rearrange("p (k q) -> p k q", q=P)).then_inc(mx.sem("pt_hi"), 1)
                    if s_ < mx.n_t:
                        a, keys = s_, mx.tiles[s_][2] * P
                        act.wait_ge(mx.sem("nm"), pair(mx.n_t, a + 1))
                        if a >= 2:
                            act.wait_ge(mx.sem("tr"), pair(mx.n_h, mx.of_tile(a - 2)[-1] + 1))
                        if a >= 4 and a % 2 == 0:
                            act.wait_ge(mx.sem("ri"), pair(mx.n_g, a // 2 - 1))
                        nc.scalar.activation(mx.prob[:, a % 2, 0:keys], tile(2 * (a % 2), 0, keys), ACT.Exp,
                                             bias=small[:, a % 2:a % 2 + 1], scale=1.0,
                                             accum_out=small[:, 2 + a % 4:3 + a % 4]).then_inc(mx.sem("exp"), 1)
                    if s_ >= 6 and s_ % 2 == 0:
                        g = (s_ - 6) // 2
                        hh, col, _ = mx.groups[g]
                        r = slice(hh * VD, (hh + 1) * VD)
                        act.wait_ge(mx.sem("of"), pair(mx.n_g, g + 1))
                        copy(h[r, bass.ds(at, 1), 0, col:col + 2 * P].rearrange("p a c -> p (a c)"),
                             sq[r, g % 2, 0:2 * P]).then_inc(mx.sem("hi"), 1)

            def even_mixer():
                b = BASE[1]
                act.wait_ge(x_aside, 16)
                for c in range(8):
                    split(0, 4, b + c + 3)
                    if c % 2 == 0:
                        act.wait_ge(w_done, b + c + 1)
                        if c:
                            act.wait_ge(sem("e_u"), c // 2)
                        nc.scalar.activation(sq[:, 0, :], tile(0), ACT.Sigmoid).then_inc(sem("e_sig"), 1)
                for m in range(6):
                    split(0, 4, b + 8 + m + 3)
                    act.wait_ge(w_done, b + 8 + m + 1)
                    if m < 5:
                        copy(cqkv[:, m, :], tile(2 * (m % 2))).then_inc(sem("e_cf"), 1)
                    else:
                        copy(q_f[NOPE:QK, 0, :], tile(2, 0, TOK, 0, ROPE)).then_inc(sem("e_cf"), 1)
                for m in range(5):
                    act.wait_ge(sem("e_cf"), m + 1)
                    if m >= 2:
                        act.wait_ge(sem("e_csum"), m - 1)
                    else:
                        act.wait_ge(sem("e_u"), 4)
                    nc.scalar.activation(sq[:, m % 2, :], cqkv[:, m, :], ACT.Square).then_inc(sem("e_csq"), 1)
                for g, (place, first, last) in enumerate(((4, 0, KQ), (6, KQ, 5))):
                    norm(N_CQ + g, tile(place), prob[:, 0, :], prob[:, 1, :], sem("e_csum"), last)
                    for m in range(first, last):
                        act.wait_ge(sem("e_ct"), m + 1)
                        copy(cn[:, m, 0, :], cqkv[:, m, :]).then_inc(sem("e_cn_hi"), 1)
                    if g == 0:
                        act.wait_ge(n_rstd, N_CQ + 1)
                act.wait_ge(sem("e_cn_lo"), 5)
                act.wait_ge(sem("e_kr"), 1)
                for hh in range(2):
                    copy(k_h[NOPE:QK, hh, 0, :], q_f[NOPE:QK, 0, :]).then_inc(sem("e_kpe_hi"), 1)
                split(0, 4, b + E_V + 3)
                for j in range(6):
                    if j < 5:
                        act.wait_ge(sem("e_vmm"), j + 1)
                    else:
                        act.wait_ge(w_done, b + E_V + 2)
                    copy(v_all[:, j, :], bank_(2 + j % 2)).then_inc(sem("e_v"), 1)
                split(0, 4, b + E_V + 4)
                act.wait_ge(sem("e_v"), 6)
                act.wait_ge(sem("e_kpe_lo"), 2)
                with act.Fori(0, 2) as i:
                    for e in range(2):
                        even_pair(i, e)
                for c in range(KC):
                    act.wait_ge(sem("e_d"), c + 1)
                    if c >= 2:
                        act.wait_ge(sem("e_lsum"), KC + c - 1)
                    for c0, n, _ in ALL:
                        g0 = c0 + HALO if c0 else 0
                        ins = nc.scalar.activation(sq[:, c % 2, c0:c0 + n], u[:, c, g0:g0 + n], ACT.Square)
                    ins.then_inc(sem("e_dsq"), 1)
                norm(N_LN, tile(2), prob[:, 0, :], prob[:, 1, :], sem("e_lsum"), 2 * KC)
                for c in range(KC):
                    act.wait_ge(sem("e_lt"), c + 1)
                    nc.scalar.activation(sq[:, c % 2, :], sq[:, c % 2, :], ACT.Silu, scale=vecs[:, V_LNG + c:V_LNG + c + 1],
                                         bias=vecs[:, V_LNB + c:V_LNB + c + 1]).then_inc(sem("e_act"), 1)
                    act.wait_ge(sem("e_act"), c + 1)
                    copy(h[:, c, 0, :], sq[:, c % 2, :]).then_inc(sem("e_ln_hi"), 1)
                for c in range(KD):
                    split(0, 4, b + E_OUT + c + 3)
                    if c == 0:
                        act.wait_ge(sem("e_ln_lo"), KC)
                    square_y(1, c, ALL, 1)

            def odd_mixer():
                b = BASE[4]
                act.wait_ge(x_aside, 32)
                for m in range(10):
                    split(0, 4, b + m + 3)
                    act.wait_ge(w_done, b + m + 1)
                    place = 2 * (m % 2)
                    if m < 4:
                        ins = copy(q4[:, m, :], tile(place, CTX, SEQ))
                    elif m < 6:
                        ins = copy(kv_f[:, m - 4, :], tile(place))
                    else:
                        ins = copy(f4[:, m - 6, :], tile(place, CTX, SEQ))
                    ins.then_inc(sem("o_pf"), 1)
                    if m == 4:
                        act.wait_ge(sem("o_consts"), 32)
                        copy(dft_c[:, 0, :], o_mats[:, 2:4, :].rearrange("p a c -> p (a c)")).then_inc(sem("o_dft_hi"), 1)
                        head_square(0)
                    if m >= 5:
                        norm_head(m - 5)
                        if m < 9:
                            head_square(m - 4)
                split(0, 4, b + O_DFT + 3)
                for g in range(4):
                    act.wait_ge(sem("o_pf"), 7 + g)
                    if g:
                        act.wait_ge(sem("o_ab"), 4 * g)
                    copy(f_h[:, 0, :], f4[:, g, :]).then_inc(sem("o_f_hi"), 1)
                    for j in range(4):
                        act.wait_ge(sem("o_ab"), 4 * g + j + 1)
                        if g:
                            act.wait_ge(sem("o_fn"), g)
                        copy(ab[:, j, 0, :], bank_(2 * (j % 2), 2 * P)).then_inc(sem("o_ab_hi"), 1)
                    if g < 3:
                        act.wait_ge(sem("o_fn"), g + 1)
                    else:
                        act.wait_ge(w_done, b + O_DFT + 4)
                    copy(h[:, 4 + g, 0, CTX:TOK], bank_(4)).then_inc(sem("o_fn_hi"), 1)
                for c in range(1, 4):
                    split(0, 4, b + O_DFT + c + 3)
                act.wait_ge(sem("o_vt"), 1)
                copy(v_t[:, :, :].rearrange("p j c -> p (j c)"), tile(0)).then_inc(sem("o_vtf"), 1)
                act.wait_ge(sem("o_rp"), 5)
                for g in range(GQA_KV):
                    r = slice(g * HD, (g + 1) * HD)
                    copy(k_dup[r, g, 0, :], kv_f[r, 0, :]).then_inc(sem("o_k_hi"), 1)
                act.wait_ge(sem("o_vtf"), 1)
                act.wait_ge(sem("o_zero"), 1)
                with act.Fori(0, 2) as i:
                    at = act.snap(i * HD)
                    copy(o_vh[:, :, 0, :], v_t[:, :, bass.ds(at, HD)]).then_inc(sem("o_vh_hi"), 1)
                    for e in range(2):
                        odd_pair(i, e)
                for c in range(KD):
                    split(0, 4, b + O_OUT + c + 3)
                    square_y(4, c, XONLY, 1)

            def head_square(m):
                act.wait_ge(sem("o_pf"), m + 1)
                if m >= 2:
                    act.wait_ge(sem("o_qsum"), m - 1)
                n = SEQ if m < 4 else TOK
                src = q4[:, m, :] if m < 4 else kv_f[:, 0, :]
                nc.scalar.activation(sq[:, m % 2, TOK - n:TOK], src, ACT.Square).then_inc(sem("o_qsq"), 1)

            def norm_head(m):
                n = SEQ if m < 4 else TOK
                if m:
                    act.wait_ge(n_rstd, N_Q + m)
                norm(N_Q + m, tile(6, TOK - n, n), o_prob[:, 0, TOK - n:TOK], o_prob[:, 1, TOK - n:TOK],
                     sem("o_qsum"), m + 1)

            def odd_pair(i, e):
                pair = lambda per, c: i * (2 * per) + (e * per + c)
                at = act.snap(i * 2 + e)
                for hh in range(2):
                    r = slice(hh * HD, (hh + 1) * HD)
                    nc.scalar.activation(qz[r, hh, 0, :], q4[r, bass.ds(at, 1), :].rearrange("p a c -> p (a c)"), ACT.Copy,
                                         scale=GQA_SCALE).then_inc(sem("o_qz_hi"), 1)
                attention(ODD, i, e, pair)

            for c in range(3):
                split(0, 4, c)
            act.wait_ge(vecs_ready, 1)
            nc.scalar.activation(cond_f[:, :, :].rearrange("p j k -> p (j k)"), vecs[:, V_C:V_C + 2 * KD],
                                 ACT.Silu).then_inc(cond_f_ready, 1)
            act.wait_ge(cond_f_ready, 1)
            copy(cond[:, :, :, 0].rearrange("p k j -> p j k"), cond_f[:, :, :]).then_inc(cond_hi, 1)
            for k in range(KD):
                act.wait_ge(x_new, k + 1)
                if k >= 2:
                    act.wait_ge(x_sum, k - 1)
                nc.scalar.activation(sq[:, k % 2, :], x[:, k, :], ACT.Square).then_inc(x_sq, 1)
            for c in range(16):
                split_mod(0, c)
                if c % 8 == 7:
                    take_row(0, c)
            pre(0, ALL)
            ffn(0, ALL)
            post(0, ALL)
            square_x(1, ALL)
            pre(1, ALL)
            even_mixer()
            post(1, ALL)
            square_x(2, ALL)
            pre(2, ALL)
            ffn(2, ALL)
            post(2, ALL)
            square_x(3, ALL)
            pre(3, ALL)
            ffn(3, ALL)
            post(3, ALL)
            square_x(4, ALL)
            pre(4, ALL)
            odd_mixer()
            post(4, XONLY)
            square_x(5, XONLY)
            pre(5, XONLY)
            ffn(5, XONLY)
            post(5, XONLY)

        @block.vector
        def _(dve):
            tt, stt, copy = nc.vector.tensor_tensor, nc.vector.scalar_tensor_tensor, nc.vector.tensor_copy

            def f(ap):
                return ap.bitcast(F32)

            def split(i, per, c):
                dve.wait_ge(w_hi, i * per + (c + 1))
                tt(w_half[1][:, c % SLOTS, :], raw[:, c % RAWS, :], f(w_half[0][:, c % SLOTS, :]),
                   ALU.subtract).then_inc(w_lo, 1)

            def split_mod(i, c):
                dve.wait_ge(m_hi, i * 24 + (c + 1))
                tt(m_half[1][:, c % MOD_SLOTS, :], mod_raw[:, c % MOD_SLOTS, :], f(m_half[0][:, c % MOD_SLOTS, :]),
                   ALU.subtract).then_inc(m_lo, 1)

            def norm(n, src, ra, rb, out_):
                dve.wait_ge(n_r2, n + 1)
                stt(ra, src, -0.5 * EPS, ra, ALU.add, ALU.mult).then_inc(n_b, 1)
                dve.wait_ge(n_b, n + 1)
                stt(out_, ra, 1.5, rb, ALU.add, ALU.mult).then_inc(n_rstd, 1)
                dve.wait_ge(n_rstd, n + 1)

            def places(segs):
                return segs[0][0], TOK - segs[0][0]

            def pre(q, segs):
                c0, n = places(segs)
                norm(N_PRE[q], tile(2, c0, n), t[:, 0, c0:c0 + n], t[:, 1, c0:c0 + n], rstd[:, c0:c0 + n])
                for k in range(KD + 1):
                    if k < KD:
                        if k >= 2:
                            dve.wait_ge(h_lo, 8 * q + k - 1)
                        for c0, n, j in segs:
                            ins = stt(t[:, k % 2, c0:c0 + n], x[:, k, c0:c0 + n], coef_pre[:, q, k, j:j + 1],
                                      rstd[:, c0:c0 + n], ALU.mult, ALU.mult)
                        ins.then_inc(h_t, 1)
                    if k >= 1:
                        dve.wait_ge(h_hi, 8 * q + k)
                        for c0, n, j in segs:
                            ins = stt(h[:, k - 1, 1, c0:c0 + n], t[:, (k - 1) % 2, c0:c0 + n], mod[:, q, 0, k - 1, j:j + 1],
                                      f(h[:, k - 1, 0, c0:c0 + n]), ALU.add, ALU.subtract)
                        ins.then_inc(h_lo, 1)

            def add_square(q, k, segs):
                c0, n = places(segs)
                dve.wait_ge(y_sq, 8 * q + k + 1)
                if k == 0:
                    copy(sum_sq[:, c0:c0 + n], sq[:, 0, c0:c0 + n]).then_inc(y_acc, 1)
                else:
                    dve.wait_ge(y_acc, 8 * q + k)
                    tt(sum_sq[:, c0:c0 + n], sum_sq[:, c0:c0 + n], sq[:, k % 2, c0:c0 + n], ALU.add).then_inc(y_acc, 1)

            def post(q, segs):
                c0, n = places(segs)
                norm(N_POST[q], tile(0, c0, n), t[:, 0, c0:c0 + n], t[:, 1, c0:c0 + n], rstd[:, c0:c0 + n])
                for k in range(KD + 1):
                    if k < KD:
                        if k >= 2:
                            dve.wait_ge(x_new, 8 * (q + 1) + k - 1)
                        for c0, n, j in segs:
                            ins = stt(t[:, k % 2, c0:c0 + n], y[:, k, c0:c0 + n], coef_post[:, q, k, j:j + 1],
                                      rstd[:, c0:c0 + n], ALU.mult, ALU.mult)
                        ins.then_inc(y_t, 1)
                    if k >= 1:
                        c0, n = places(segs)
                        dve.wait_ge(y_t, 8 * q + k)
                        tt(x[:, k - 1, c0:c0 + n], x[:, k - 1, c0:c0 + n], t[:, (k - 1) % 2, c0:c0 + n],
                           ALU.add).then_inc(x_new, 1)

            def columns(layers, r, done):
                dve.wait_ge(rows_in, 32 if done == 1 else 96)
                for l in range(layers):
                    tt(m_sum[0:r, l, :, :], m_rows[0:r, l, 0:4:2, :], m_rows[0:r, l, 1:4:2, :], ALU.add).then_inc(rows_sum, 1)
                dve.wait_ge(rows_sum, 1 if done == 1 else 3)
                for l in range(layers):
                    for j in range(2):
                        ins = tt(m_sum[0:r, l, j, :], m_sum[0:r, l, j, :], m_bias[0:r, l, :], ALU.add)
                ins.then_inc(rows_full, 1)
                dve.wait_ge(rows_t, done)
                flat = mod[:, :, :, :, :].rearrange("p q a k j -> p (q a k) j")
                for l in range(layers):
                    for j in range(2):
                        ins = copy(flat[:, 72 * l:72 * l + r, j], bank_(0)[:, (l * 2 + j) * 72:(l * 2 + j) * 72 + r])
                ins.then_inc(mod_ready, 1)
                dve.wait_ge(mod_ready, done)
                gain = lambda at, q0, q1: vecs[:, at:at + 6 * KD].rearrange("p (q k) -> p q k", k=KD)[:, q0:q1, :]
                nq = 1 if done == 1 else 6
                for j in range(2):
                    ins = stt(coef_pre[:, 0:nq, :, j], mod[:, 0:nq, 1, :, j], 1.0, gain(V_GPRE, 0, nq), ALU.add, ALU.mult)
                    if done == 2:
                        for q in range(6):
                            ins = stt(coef_post[:, q, :, j], mod[:, q, 2, :, j], 1.0 if q % 3 == 1 else 0.5,
                                      gain(V_GPOST, q, q + 1).rearrange("p q k -> p (q k)"), ALU.mult, ALU.mult)
                ins.then_inc(coef_ready, 1)
                dve.wait_ge(coef_ready, done)

            def ffn(q, segs):
                b, fi = BASE[q], ffn_at[q]
                c0, n = places(segs)
                nt = KD * len(segs)
                tiles = down_tiles(q, segs)

                def up(i, c, t_, m0):
                    for j in range(4):
                        split(i, 12, c + j + 3)
                        if m0 is not None:
                            split_mod(i, m0 + 2 * j)
                            split_mod(i, m0 + 2 * j + 1)
                        if j % 2 == 1:
                            hidden = 22 * fi + 2 * t_ + j // 2
                            dve.wait_ge(w_done, i * 12 + (c + j + 1))
                            dve.wait_ge(silu_done, i * 4 + (hidden + 1))
                            dve.wait_ge(hid_lo, i * 4 + hidden)
                            tt(sq[:, 1, c0:c0 + n], sq[:, 0, c0:c0 + n], tile(2, c0, n), ALU.mult).then_inc(hid_f, 1)
                            dve.wait_ge(hid_hi, i * 4 + (hidden + 1))
                            tt(hid[:, t_ % 2, j // 2, 1, c0:c0 + n], sq[:, 1, c0:c0 + n],
                               f(hid[:, t_ % 2, j // 2, 0, c0:c0 + n]), ALU.subtract).then_inc(hid_lo, 1)

                def add_tile(i, c, t_, idx):
                    d, (s0, w, _), place = tiles[idx]
                    if idx < nt - 1:
                        dve.wait_ge(down_done, i * 2 * (nt - 1) + (165 * fi + t_ * (nt - 1) + idx + 1))
                    else:
                        dve.wait_ge(w_done, i * 12 + (c + 2))
                    tt(y[:, d, s0:s0 + w], y[:, d, s0:s0 + w], place, ALU.add).then_inc(y_done, 1)

                def down(i, c, t_, m0):
                    split(i, 12, c + 3)
                    if m0 is not None:
                        split_mod(i, m0)
                        split_mod(i, m0 + 1)
                    for idx in range(nt):
                        add_tile(i, c, t_, idx)
                        if m0 is not None and idx in (7, 11):
                            split_mod(i, m0 + 2 + (idx - 7) // 4)
                    split(i, 12, c + 4)

                up(0, b, 0, 16 if q == 0 else None)
                if q == 0:
                    dve.wait_ge(y_done, 4)
                else:
                    dve.wait_ge(y_zero, fi)
                with dve.Fori(0, 5) as i:
                    for half in range(2):
                        m0 = 24 + 12 * half if q == 0 else None
                        up(i, b + 4 + 6 * half, 1 + half, m0)
                        down(i, b + 8 + 6 * half, half, m0 + 8 if q == 0 else None)
                if q != 5:
                    split(0, 12, b + 64 + 3)
                for idx in range(nt):
                    add_tile(0, b + 64, 10, idx)
                    d = (idx + 1) // len(segs) - 1
                    if (idx + 1) % len(segs) == 0 and d >= 1:
                        add_square(q, d - 1, segs)
                add_square(q, KD - 1, segs)
                if q != 5:
                    split(0, 12, b + 64 + 4)

            def conv(first, last):
                for n in range(first, min(last, 2 * (CONV_K + 1))):
                    c, k = n // (CONV_K + 1), n % (CONV_K + 1)
                    src = u[:, c, k % CONV_K:k % CONV_K + GAPPED]
                    tap = vecs[:, V_CONVW + k * KC + c:V_CONVW + k * KC + c + 1]
                    if n:
                        dve.wait_ge(sem("e_conv_a"), n)
                    if k == 0:
                        ins = nc.vector.tensor_scalar(conv_sum[:, :], src, tap, None, ALU.mult)
                    elif k < CONV_K:
                        ins = stt(conv_sum[:, :], src, tap, conv_sum[:, :], ALU.mult, ALU.add)
                    else:
                        ins = nc.vector.tensor_scalar(u[:, c, 0:GAPPED], conv_sum[:, :],
                                                      vecs[:, V_CONVB + c:V_CONVB + c + 1], None, ALU.add)
                    ins.then_inc(sem("e_conv_a"), 1)

            def rope(rows, q_ap, rot, tab, tmp, step, count, done):
                tt(tmp, rot, tab[rows, 1, :], ALU.mult).then_inc(step, 1)
                tt(q_ap, q_ap, tab[rows, 0, :], ALU.mult).then_inc(step, 1)
                dve.wait_ge(step, count + 2)
                tt(q_ap, q_ap, tmp, ALU.add).then_inc(done, 1)

            def even_pair(i, e):
                b = BASE[1] + E_PAIR
                pair = lambda per, c: i * (2 * per) + (e * per + c)
                split(i, 4, b + 2 * e + 3)
                r = slice(NOPE, QK)
                for hh in range(2):
                    dve.wait_ge(sem("e_k_hi"), pair(2, hh + 1))
                    tt(k_h[0:NOPE, hh, 1, :], tile(4, 0, TOK, hh * NOPE, (hh + 1) * NOPE), f(k_h[0:NOPE, hh, 0, :]),
                       ALU.subtract).then_inc(sem("e_k_lo"), 1)
                split(i, 4, b + 2 * e + 4)
                for hh in range(2):
                    dve.wait_ge(sem("e_rot"), pair(2, hh + 1))
                    rope(r, q_f[r, hh, CTX:TOK], tile(2 * hh, CTX, SEQ, NOPE, QK), e_rope, sq[r, hh, CTX:TOK],
                         sem("e_qrs"), pair(4, 2 * hh), sem("e_qr"))
                for hh in range(2):
                    dve.wait_ge(sem("e_q_hi"), pair(2, hh + 1))
                    tt(q_h[0:QK, hh, 1, :], q_f[0:QK, hh, :], f(q_h[0:QK, hh, 0, :]), ALU.subtract).then_inc(sem("e_q_lo"), 1)
                at = dve.snap(i * 4 * VD + 2 * e * VD)
                dve.wait_ge(sem("e_vh_hi"), pair(1, 1))
                tt(e_vh[:, :, 1, :], v_all[:, :, bass.ds(at, 2 * VD)], f(e_vh[:, :, 0, :]), ALU.subtract).then_inc(sem("e_vh_lo"), 1)
                attention(EVEN, i, e, pair)

            def attention(mx, i, e, pair):
                at = dve.snap(i * 2 + (mx.out_at + e))
                for s_ in range(mx.n_t + 5):
                    if s_ < mx.n_t:
                        a, keys = s_, mx.tiles[s_][2] * P
                        dve.wait_ge(mx.sem("s"), pair(mx.n_t, a + 1))
                    if s_ >= 4 and s_ % 2 == 0 and s_ // 2 - 2 < mx.n_g:
                        g = s_ // 2 - 2
                        dve.wait_ge(mx.sem("inv"), pair(mx.n_g, g + 1))
                        copy(sq[0:VD, g % 2, 2 * P:4 * P], inv_place).then_inc(mx.sem("inv_out"), 1)
                    if s_ < mx.n_t:
                        nc.vector.tensor_reduce(small[:, a % 2:a % 2 + 1], tile(2 * (a % 2), 0, keys), AX_X, ALU.max,
                                                negate=True).then_inc(mx.sem("nm"), 1)
                    if 2 <= s_ <= mx.n_t and s_ % 2 == 0:
                        g = s_ // 2 - 1
                        r = slice(6 + g % 2 * 2, 8 + g % 2 * 2)
                        dve.wait_ge(mx.sem("exp"), pair(mx.n_t, s_))
                        nc.vector.reciprocal(small[:, r], small[:, 2 + g % 2 * 2:4 + g % 2 * 2]).then_inc(mx.sem("ri"), 1)
                        if g >= 1:
                            dve.wait_ge(mx.sem("inv"), pair(mx.n_g, g))
                        dve.wait_ge(mx.sem("ri"), pair(mx.n_g, g + 1))
                        for j in range(2):
                            ins = nc.vector.tensor_scalar(mx.diag[:, j, :], idm, small[:, r.start + j:r.start + j + 1],
                                                          None, ALU.mult)
                        ins.then_inc(mx.sem("dg"), 1)
                    if 0 <= s_ - 2 < mx.n_t:
                        a = s_ - 2
                        for n in mx.of_tile(a):
                            _, k0, kn = mx.halves[n]
                            dst = mx.pt[:, a // 2 % 2, k0:k0 + kn, :, a % 2 * P:(a % 2 + 1) * P]
                            dve.wait_ge(mx.sem("pt_hi"), pair(mx.n_h, n + 1))
                            tt(dst[:, :, 1, :], turned(n, kn).rearrange("p (k q) -> p k q", q=P), f(dst[:, :, 0, :]),
                               ALU.subtract).then_inc(mx.sem("pt_lo"), 1)
                    if s_ >= 5 and s_ % 2 == 1:
                        g = (s_ - 5) // 2
                        r = slice(mx.groups[g][0] * VD, (mx.groups[g][0] + 1) * VD)
                        dve.wait_ge(mx.sem("pv"), pair(mx.n_g, g + 1))
                        if g >= 2:
                            dve.wait_ge(mx.sem("lo"), pair(mx.n_g, g - 1))
                        dve.wait_ge(mx.sem("inv_out"), pair(mx.n_g, g + 1))
                        stt(sq[r, g % 2, 0:2 * P], pv_place, -2.0 * D, sq[0:VD, g % 2, 2 * P:4 * P], ALU.mult, ALU.mult).then_inc(mx.sem("of"), 1)
                    if s_ >= 6 and s_ % 2 == 0:
                        g = (s_ - 6) // 2
                        hh, col, _ = mx.groups[g]
                        r = slice(hh * VD, (hh + 1) * VD)
                        dve.wait_ge(mx.sem("hi"), pair(mx.n_g, g + 1))
                        hi, lo = (h[r, bass.ds(at, 1), a, col:col + 2 * P].rearrange("p a c -> p (a c)") for a in range(2))
                        tt(lo, sq[r, g % 2, 0:2 * P], f(hi), ALU.subtract).then_inc(mx.sem("lo"), 1)

            def even_mixer():
                b = BASE[1]
                dve.wait_ge(x_aside, 16)
                dve.wait_ge(sem("e_zero"), 3)
                for c in range(8):
                    split(0, 4, b + c + 3)
                    if c % 2 == 1:
                        dve.wait_ge(w_done, b + c + 1)
                        dve.wait_ge(sem("e_sig"), c // 2 + 1)
                        for c0, n, _ in ALL:
                            g0 = c0 + HALO + (HALO if c0 else 0)
                            ins = tt(u[:, c // 2, g0:g0 + n], tile(2, c0, n), sq[:, 0, c0:c0 + n], ALU.mult)
                        ins.then_inc(sem("e_u"), 1)
                    if c >= 2:
                        if c == 2:
                            dve.wait_ge(sem("e_u"), 1)
                        conv(4 * (c - 2), 4 * (c - 1))
                dve.wait_ge(sem("e_u"), 4)
                for m in range(6):
                    split(0, 4, b + 8 + m + 3)
                    conv(24 + 7 * m, 31 + 7 * m)
                dve.wait_ge(sem("e_consts"), 32)
                dve.wait_ge(sem("e_krot"), 1)
                r = slice(NOPE, QK)
                rope(r, q_f[r, 0, CTX:TOK], tile(0, CTX, SEQ, NOPE, QK), e_rope, rstd_e[r, 0:SEQ], sem("e_krs"), 0, sem("e_kr"))
                for g, (place, first, last) in enumerate(((4, 0, KQ), (6, KQ, 5))):
                    norm(N_CQ + g, tile(place), prob[:, 0, :], prob[:, 1, :], rstd_e[:, :])
                    for m in range(first, last):
                        gain = vecs[:, V_GCQ + m:V_GCQ + m + 1] if m < KQ else vecs[:, V_GCKV + m - KQ:V_GCKV + m - KQ + 1]
                        stt(cqkv[:, m, :], cqkv[:, m, :], gain, rstd_e[:, :], ALU.mult, ALU.mult).then_inc(sem("e_ct"), 1)
                    for m in range(first, last):
                        dve.wait_ge(sem("e_cn_hi"), m + 1)
                        tt(cn[:, m, 1, :], cqkv[:, m, :], f(cn[:, m, 0, :]), ALU.subtract).then_inc(sem("e_cn_lo"), 1)
                for hh in range(2):
                    dve.wait_ge(sem("e_kpe_hi"), hh + 1)
                    tt(k_h[r, hh, 1, :], q_f[r, 0, :], f(k_h[r, hh, 0, :]), ALU.subtract).then_inc(sem("e_kpe_lo"), 1)
                split(0, 4, b + E_V + 3)
                split(0, 4, b + E_V + 4)
                with dve.Fori(0, 2) as i:
                    for e in range(2):
                        even_pair(i, e)
                for c in range(KC):
                    if c == 0:
                        dve.wait_ge(sem("e_lsum"), KC)
                    for c0, n, _ in ALL:
                        g0 = c0 + HALO if c0 else 0
                        ins = tt(u[:, c, g0:g0 + n], u[:, c, g0:g0 + n], tile(0, c0, n), ALU.add)
                    ins.then_inc(sem("e_d"), 1)
                norm(N_LN, tile(2), prob[:, 0, :], prob[:, 1, :], rstd_e[:, :])
                for c in range(KC + 1):
                    if c < KC:
                        if c >= 2:
                            dve.wait_ge(sem("e_ln_lo"), c - 1)
                        for c0, n, _ in ALL:
                            g0 = c0 + HALO if c0 else 0
                            ins = tt(sq[:, c % 2, c0:c0 + n], u[:, c, g0:g0 + n], rstd_e[:, c0:c0 + n], ALU.mult)
                        ins.then_inc(sem("e_lt"), 1)
                    if c >= 1:
                        dve.wait_ge(sem("e_ln_hi"), c)
                        tt(h[:, c - 1, 1, :], sq[:, (c - 1) % 2, :], f(h[:, c - 1, 0, :]), ALU.subtract).then_inc(sem("e_ln_lo"), 1)
                out_tiles(1, b + E_OUT, ALL)
                dve.wait_ge(x_back, 16)

            def out_tiles(q, b, segs):
                c0, n = places(segs)
                for c in range(KD):
                    split(0, 4, b + c + 3)
                    dve.wait_ge(w_done, b + c + 1)
                    copy(y[:, c, c0:c0 + n], tile(2 * (c % 2), c0, n)).then_inc(y_done, 1)
                    if c >= 1:
                        add_square(q, c - 1, segs)
                add_square(q, KD - 1, segs)

            def odd_mixer():
                b = BASE[4]
                dve.wait_ge(x_aside, 32)
                for m in range(10):
                    split(0, 4, b + m + 3)
                    if m == 4:
                        dve.wait_ge(sem("o_dft_hi"), 1)
                        tt(dft_c[:, 1, :], o_mats[:, 2:4, :].rearrange("p a c -> p (a c)"), f(dft_c[:, 0, :]), ALU.subtract).then_inc(sem("o_dftc"), 1)
                    if m >= 5:
                        if m >= 6:
                            head_rope(m - 6)
                        head_gain(m - 5)
                split(0, 4, b + O_DFT + 3)
                for g in range(4):
                    dve.wait_ge(sem("o_f_hi"), g + 1)
                    tt(f_h[:, 1, :], f4[:, g, :], f(f_h[:, 0, :]), ALU.subtract).then_inc(sem("o_f_lo"), 1)
                    for j in range(4):
                        dve.wait_ge(sem("o_ab_hi"), 4 * g + j + 1)
                        tt(ab[:, j, 1, :], bank_(2 * (j % 2), 2 * P), f(ab[:, j, 0, :]), ALU.subtract).then_inc(sem("o_ab_lo"), 1)
                    if g == 1:
                        head_rope(4)
                    dve.wait_ge(sem("o_fn_hi"), g + 1)
                    tt(h[:, 4 + g, 1, CTX:TOK], bank_(4), f(h[:, 4 + g, 0, CTX:TOK]), ALU.subtract).then_inc(sem("o_fn_lo"), 1)
                for c in range(1, 4):
                    split(0, 4, b + O_DFT + c + 3)
                for g in range(GQA_KV):
                    r = slice(g * HD, (g + 1) * HD)
                    dve.wait_ge(sem("o_k_hi"), g + 1)
                    tt(k_dup[r, g, 1, :], kv_f[r, 0, :], f(k_dup[r, g, 0, :]), ALU.subtract).then_inc(sem("o_k_lo"), 1)
                dve.wait_ge(sem("o_k_lo"), 2)
                for g in range(GQA_KV):
                    r, other = slice(g * HD, (g + 1) * HD), slice((1 - g) * HD, (2 - g) * HD)
                    for a in range(2):
                        copy(k_dup[other, g, a, :], f(k_dup[r, g, a, :])).then_inc(sem("o_kd"), 1)
                with dve.Fori(0, 2) as i:
                    at = dve.snap(i * HD)
                    dve.wait_ge(sem("o_vh_hi"), i + 1)
                    tt(o_vh[:, :, 1, :], v_t[:, :, bass.ds(at, HD)], f(o_vh[:, :, 0, :]), ALU.subtract).then_inc(sem("o_vh_lo"), 1)
                    for e in range(2):
                        odd_pair(i, e)
                out_tiles(4, b + O_OUT, XONLY)
                dve.wait_ge(x_back, 32)

            def head_gain(m):
                n = SEQ if m < 4 else TOK
                norm(N_Q + m, tile(6, TOK - n, n), o_prob[:, 0, TOK - n:TOK], o_prob[:, 1, TOK - n:TOK], rstd_o[:, TOK - n:TOK])
                x_ = q4[:, m, :] if m < 4 else kv_f[:, 0, :]
                g = V_GQN if m < 4 else V_GKN
                stt(x_, x_, vecs[:, g:g + 1], rstd_o[:, TOK - n:TOK], ALU.mult, ALU.mult).then_inc(sem("o_qn"), 1)

            def head_rope(m):
                dve.wait_ge(sem("o_rot"), m + 1)
                x_ = q4[:, m, :] if m < 4 else kv_f[:, 0, CTX:TOK]
                rope(slice(0, P), x_, bank_(5), o_rope, sum_sq[:, 0:SEQ], sem("o_rps"), 2 * m, sem("o_rp"))

            def odd_pair(i, e):
                pair = lambda per, c: i * (2 * per) + (e * per + c)
                at = dve.snap(i * 2 + e)
                for hh in range(2):
                    r = slice(hh * HD, (hh + 1) * HD)
                    dve.wait_ge(sem("o_qz_hi"), pair(2, hh + 1))
                    stt(qz[r, hh, 1, :], q4[r, bass.ds(at, 1), :].rearrange("p a c -> p (a c)"), GQA_SCALE, f(qz[r, hh, 0, :]),
                        ALU.mult, ALU.subtract).then_inc(sem("o_qz_lo"), 1)
                attention(ODD, i, e, pair)

            dve.wait_ge(vec_t, 1)
            copy(vecs[:, :], bank_(0)[:, 0:2 * P]).then_inc(vecs_ready, 1)
            for c in range(3):
                split(0, 4, c)
            dve.wait_ge(cond_hi, 1)
            tt(cond[:, :, :, 1].rearrange("p k j -> p j k"), cond_f[:, :, :],
               f(cond[:, :, :, 0]).rearrange("p k j -> p j k"), ALU.subtract).then_inc(cond_ready, 1)
            for k in range(KD):
                dve.wait_ge(tok_t, k + 1)
                copy(x[:, k, :], tile(2 * (k % 2))).then_inc(x_new, 1)
            for c in range(16):
                split_mod(0, c)
            for k in range(4):
                nc.vector.memset(y[:, 2 * k:2 * k + 2, :], 0.0).then_inc(y_done, 1)
            columns(1, 16, 1)
            pre(0, ALL)
            ffn(0, ALL)
            columns(2, 72, 2)
            post(0, ALL)
            pre(1, ALL)
            even_mixer()
            post(1, ALL)
            pre(2, ALL)
            ffn(2, ALL)
            post(2, ALL)
            pre(3, ALL)
            ffn(3, ALL)
            post(3, ALL)
            pre(4, ALL)
            odd_mixer()
            post(4, XONLY)
            pre(5, XONLY)
            ffn(5, XONLY)
            post(5, XONLY)
            for j in range(4):
                dve.wait_ge(sem("out_t"), j + 1)
                copy(tok_in[:, j, :], ps[:, (2 + 2 * (j % 2)) * 512:(4 + 2 * (j % 2)) * 512]).then_inc(sem("out_ready"), 1)


_INS = ['x', 'c', 'ctx', 'c_ctx', 'w_mod', 'b_mod', 'g_pre', 'g_post', 'ffn_w_gate', 'ffn_w_up', 'ffn_w_down',
        'ev_w_in', 'ev_conv_w', 'ev_conv_b', 'ev_ln_g', 'ev_ln_b', 'ev_g_cq', 'ev_w_uq', 'ev_g_ckv', 'ev_w_ukv',
        'ev_w_out', 'od_w_in', 'od_g_qn', 'od_g_kn', 'od_w_out']


def kernel(**inputs):
    import numpy as _np
    import concourse.bacc as _bacc
    from concourse import mybir as _mybir
    from concourse.bass_utils import run_bass_kernel_spmd as _run

    nc = _bacc.Bacc("TRN2", target_bir_lowering=False, num_devices=1)
    arrays, args = {}, []
    given = {name: _np.ascontiguousarray(inputs[name]) for name in _INS}
    given["consts"], given["dft"] = constant_array(), dft_array()
    for name, a in given.items():
        arrays[f"in_{name}_dram"] = a
        args.append(nc.dram_tensor(f"in_{name}_dram", a.shape, _mybir.dt.from_np(a.dtype), kind="ExternalInput").ap())
    args.append(nc.dram_tensor("out_dram", (1, SEQ, D), _mybir.dt.float32, kind="ExternalOutput").ap())
    trunk(nc, *args)
    r = _run(nc, [arrays], core_ids=[0])
    return r.results[0]["out_dram"]
```

```python
from contextlib import ExitStack

import numpy as np

import concourse.bass as bass
from concourse import mybir

F32 = mybir.dt.float32
F32R = mybir.dt.float32r
ACT = mybir.ActivationFunctionType
ALU = mybir.AluOpType
AX_X = mybir.AxisListType.X

P = 128
D = 1024
KD = D // P
CTX, SEQ = 256, 512
TOK = CTX + SEQ
EPS = 1e-6
D_FF = 2816
FT = D_FF // P
STEPS = FT // 2
CHUNK = 1024
RAWS, SLOTS = 2, 4
MOD_RAWS, MOD_SLOTS = 3, 2
UNITS = 18
SEG_C, SEG_X = (0, CTX, 1), (CTX, SEQ, 0)
ALL, XONLY = (SEG_C, SEG_X), (SEG_X,)

CONV_CH, CONV_K = 512, 31
KC = CONV_CH // P
HALO = CONV_K // 2
GAPPED = CTX + HALO + SEQ
PADDED = GAPPED + 2 * HALO
HEADS, NOPE, ROPE, VD = 8, 64, 32, 64
QK = NOPE + ROPE
Q_LORA, KV_LORA = 384, 256
KQ, KKV = Q_LORA // P, KV_LORA // P
MLA_SCALE = QK ** -0.5
GQA_HEADS, GQA_KV, HD = 8, 2, 64
GQA_SCALE = HD ** -0.5
GRID_W = 64
ROPE_THETA = 10000.0

FFN_CHUNKS = 3 * FT
E_IN, E_V, E_PAIR, E_OUT = 0, 14, 16, 24
E_CHUNKS = 32
O_IN, O_DFT, O_OUT = 0, 10, 14
O_CHUNKS = 22
BASE = {0: 0, 1: FFN_CHUNKS, 2: FFN_CHUNKS + E_CHUNKS, 3: 2 * FFN_CHUNKS + E_CHUNKS,
        4: 3 * FFN_CHUNKS + E_CHUNKS, 5: 3 * FFN_CHUNKS + E_CHUNKS + O_CHUNKS}

V_GPRE, V_GPOST, V_C, V_CCTX, V_CONVB, V_LNG, V_LNB, V_GCQ = 0, 48, 96, 104, 112, 116, 120, 124
V_CONVW, V_GCKV, V_GQN, V_GKN = 128, 252, 254, 255

C_ID, C_N1024, C_N384, C_N256, C_N512, C_P96, C_B64, C_P128, C_DFT = (P * i for i in range(9))
C_MROPE = C_DFT + 2 * P
C_GROPE = C_MROPE + 2 * SEQ
C_END = C_GROPE + 2 * SEQ


def rope_rows(rot_dim):
    nf = rot_dim // 4
    inv = ROPE_THETA ** (-np.arange(nf, dtype=np.float32) / np.float32(nf))
    row = np.repeat(np.arange(SEQ // GRID_W), GRID_W).astype(np.float32)
    col = np.tile(np.arange(GRID_W), SEQ // GRID_W).astype(np.float32)
    cos, sin, swap = [], [], []
    for axis, place in enumerate((row, col)):
        for half in range(2):
            for f in range(nf):
                ang = place * inv[f]
                cos.append(np.cos(ang))
                sin.append(np.sin(ang))
                d = (axis * 2 + half) * nf + f
                swap.append((d, (axis * 2 + 1 - half) * nf + f, 1.0 if half else -1.0))
    return np.array(cos, np.float32), np.array(sin, np.float32), swap


def constant_array():
    k = np.zeros((P, C_END), np.float32)
    k[:, C_ID:C_ID + P] = np.eye(P)
    for at, v in ((C_N1024, -0.5 / D), (C_N384, -0.5 / Q_LORA), (C_N256, -0.5 / KV_LORA),
                  (C_N512, -0.5 / CONV_CH)):
        k[:, at:at + P] = v
    cos, sin, swap = rope_rows(ROPE)
    for d, s, sign in swap:
        k[NOPE + s, C_P96 + NOPE + d] = sign
    k[NOPE:QK, C_MROPE:C_MROPE + SEQ] = cos
    k[NOPE:QK, C_MROPE + SEQ:C_MROPE + 2 * SEQ] = sin
    cos, sin, swap = rope_rows(HD)
    for h in range(2):
        k[h * HD:(h + 1) * HD, C_B64 + h * HD:C_B64 + (h + 1) * HD] = -0.5 / HD
        for d, s, sign in swap:
            k[h * HD + s, C_P128 + h * HD + d] = sign
        k[h * HD:(h + 1) * HD, C_GROPE:C_GROPE + SEQ] = cos
        k[h * HD:(h + 1) * HD, C_GROPE + SEQ:C_GROPE + 2 * SEQ] = sin
    a = 2 * np.pi * (np.outer(np.arange(P), np.arange(P)) % P) / P
    k[:, C_DFT:C_DFT + P] = np.cos(a) / np.sqrt(P)
    k[:, C_DFT + P:C_DFT + 2 * P] = np.sin(a) / np.sqrt(P)
    return k


def dft_array():
    a = 2 * np.pi * (np.outer(np.arange(SEQ), np.arange(SEQ)) % SEQ) / SEQ
    return np.concatenate([np.cos(a), -np.sin(a)], axis=1).astype(np.float32) / np.float32(np.sqrt(SEQ))


def trunk(nc, x_in, c_in, ctx_in, c_ctx_in, w_mod, b_mod, g_pre, g_post, w_gate, w_up, w_down,
          ev_w_in, conv_w, conv_b, ln_g, ln_b, g_cq, w_uq, g_ckv, w_ukv, ev_w_out,
          od_w_in, g_qn, g_kn, od_w_out, consts, dft, out):
    mod_scratch = nc.dram_tensor("mod_scratch", (UNITS * 8, 4, P), F32).ap()
    x_scratch = nc.dram_tensor("x_scratch", (P, KD, TOK), F32).ap()
    ctx = ExitStack()
    names = {}

    def sb(stack, name, shape, dt=F32):
        return stack.enter_context(nc.sbuf_tensor(name, shape, dt))

    def sem(name):
        if name not in names:
            names[name] = ctx.enter_context(nc.semaphore(name))
        return names[name]

    with ctx:
        h = sb(ctx, "h", [P, KD, 2, TOK], F32R)
        raw = sb(ctx, "raw", [P, RAWS, CHUNK])
        w_half = [sb(ctx, "w_hi", [P, SLOTS, CHUNK], F32R), sb(ctx, "w_lo", [P, SLOTS, CHUNK], F32R)]
        sq = sb(ctx, "sq", [P, 2, TOK])
        sum_sq = sb(ctx, "sum_sq", [P, GAPPED])
        ident = sb(ctx, "ident", [P, 2 * P])
        vecs = sb(ctx, "vecs", [P, 2 * P])
        mod = sb(ctx, "mod", [P, 6, 3, KD, 2])
        coef_pre = sb(ctx, "coef_pre", [P, 6, KD, 2])
        coef_post = sb(ctx, "coef_post", [P, 6, KD, 2])
        small = sb(ctx, "small", [P, 10])
        n1024 = ident[:, P:2 * P]
        idm = ident[:, 0:P]
        with ExitStack() as s:
            x = sb(s, "x", [P, KD, TOK])
            y = sb(s, "y", [P, KD, TOK])
            hid = sb(s, "hid", [P, 2, 2, 2, TOK], F32R)
            mod_raw = sb(s, "mod_raw", [P, MOD_RAWS, CHUNK])
            m_half = [sb(s, "m_hi", [P, MOD_SLOTS, CHUNK], F32R), sb(s, "m_lo", [P, MOD_SLOTS, CHUNK], F32R)]
            mod_row = sb(s, "mod_row", [4, CHUNK])
            cond = sb(s, "cond", [P, KD, 2, 2], F32R)
        with ExitStack() as s:
            sb(s, "x_", [P, KD, TOK])
            sb(s, "y_", [P, KD, TOK])
            t = sb(s, "t", [P, 3, TOK])
            rstd = sb(s, "rstd", [P, TOK])
            fin = sb(s, "fin", [P, 14, P])
        m_rows = fin[:, 0:8, :].rearrange("r (l s) c -> r l s c", l=2)
        m_sum = fin[:, 8:12, :].rearrange("r (l j) c -> r l j c", l=2)
        m_bias = fin[:, 12:14, :]
        with ExitStack() as s:
            sb(s, "x__", [P, KD, TOK])
            tok_in = sb(s, "tok_in", [P, TOK // P, D])
            sb(s, "t__", [P, 3, TOK])
            vec_in = sb(s, "vec_in", [P, 2, P])
            cond_f = sb(s, "cond_f", [P, 2, KD])
        with ExitStack() as s:
            u = sb(s, "u", [P, KC, PADDED])
            cn = sb(s, "cn", [P, KQ + KKV, 2, TOK], F32R)
            v_all = sb(s, "v_all", [P, TOK // P, HEADS * VD])
            e_vh = sb(s, "e_vh", [P, TOK // P, 2, 2 * VD], F32R)
            prob = sb(s, "prob", [P, 2, TOK])
            q_f = sb(s, "q_f", [P, 2, TOK])
            e_diag = sb(s, "e_diag", [P, 2, P])
            e_mats = sb(s, "e_mats", [P, C_B64 - C_N384])
            e_rope = sb(s, "e_rope", [P, 2, SEQ])
            conv_tap = sb(s, "conv_tap", [P, GAPPED])
            with ExitStack() as s2:
                q_h = sb(s2, "q_h", [P, 2, 2, TOK], F32R)
                k_h = sb(s2, "k_h", [P, 2, 2, TOK], F32R)
            with ExitStack() as s2:
                cqkv = sb(s2, "cqkv", [P, KQ + KKV, TOK])
                rstd_e = sb(s2, "rstd_e", [P, TOK])
                conv_sum = sb(s2, "conv_sum", [P, GAPPED])
        pt = h[:, 0:4, :, :].rearrange("p a b c -> p (a b c)").rearrange("p (r k g q) -> p r k g q", r=2, k=6, g=2)
        with ExitStack() as s:
            q4 = sb(s, "q4", [P, 4, SEQ])
            kv_f = sb(s, "kv_f", [P, 2, TOK])
            o_rope = sb(s, "o_rope", [P, 2, SEQ])
            o_mats = sb(s, "o_mats", [P, 4, P])
            dft_c = sb(s, "dft_c", [P, 2, 2 * P], F32R)
            k_dup = sb(s, "k_dup", [P, GQA_KV, 2, TOK], F32R)
            v_t = sb(s, "v_t", [P, TOK // P, P])
            o_vh = sb(s, "o_vh", [P, TOK // P, 2, HD], F32R)
            o_diag = sb(s, "o_diag", [P, 2, P])
            o_prob = sb(s, "o_prob", [P, 2, TOK])
            rstd_o = sb(s, "rstd_o", [P, TOK])
            qz = sb(s, "qz", [P, 2, 2, SEQ], F32R)
            with ExitStack() as s2:
                f4 = sb(s2, "f4", [P, 4, SEQ])
                f_h = sb(s2, "f_h", [P, 2, 2, SEQ], F32R)
                ab = sb(s2, "ab", [P, 4, 2, 2 * P], F32R)
            with ExitStack() as s2:
                o_pt = sb(s2, "o_pt", [P, 2, TOK // P, 2, 2 * P], F32R)

        ps = ctx.enter_context(nc.psum_tensor("ps", [P, 8 * 512], F32))

        def tile(bank, c0=0, n=TOK, r0=0, r1=P):
            return ps[r0:r1, bank * 512 + 256 + c0:bank * 512 + 256 + c0 + n]

        def bank_(b, n=512, r0=0, r1=P):
            return ps[r0:r1, b * 512:b * 512 + n]

        w_loaded = [sem(f"w_loaded{j}") for j in range(RAWS)]
        w_hi, w_lo, w_done = sem("w_hi"), sem("w_lo"), sem("w_done")
        m_loaded = [sem(f"m_loaded{j}") for j in range(MOD_RAWS)]
        m_hi, m_lo, m_done = sem("m_hi"), sem("m_lo"), sem("m_done")
        row_ready, row_stored = sem("row_ready"), sem("row_stored")
        block = ctx.enter_context(nc.Block())

        def cols(w, at, width):
            return w.rearrange("(k p) c -> p k c", p=P)[:, :, bass.ds(at, width)]

        PASSES = ((0, 0), (0, 1), (1, 0))

        def known(i):
            return isinstance(i, int)

        def down_tiles(q, segs):
            banks = (0, 1, 4, 5) if q == 0 else (4, 5, 6, 7)
            order = [(d, seg) for d in range(KD) for seg in segs]
            return [(d, seg, bank_(banks[n % 4], seg[1])) for n, (d, seg) in enumerate(order)]

        class Mixer:
            def __init__(self, m, contexts, prob_, pt_, vh, vh_at, diag, out_at):
                self.m, self.prob, self.pt, self.vh, self.vh_at, self.diag = m, prob_, pt_, vh, vh_at, diag
                self.out_at = out_at
                self.groups = [(hh, c, n) for hh in range(2) for c, n in (
                    [(CTX, 6), (CTX + 2 * P, 6)] + ([(0, 2)] if contexts else []))]
                self.tiles = [(g, c + j * P, n) for g, (_, c, n) in enumerate(self.groups) for j in range(2)]
                self.halves = [(a, k0, min(3, n - k0)) for a, (_, _, n) in enumerate(self.tiles) for k0 in range(0, n, 3)]
                self.n_t, self.n_g, self.n_h = len(self.tiles), len(self.groups), len(self.halves)

            def sem(self, name):
                return sem(self.m + name)

            def of_tile(self, a):
                return [n for n, (t_, _, _) in enumerate(self.halves) if t_ == a]

        EVEN = Mixer("e_", True, prob, pt, e_vh, VD, e_diag, 4)
        ODD = Mixer("o_", False, o_prob, o_pt, o_vh, 0, o_diag, 0)
        turned = lambda n, kn: bank_(4 + n % 3, kn * P)
        pv_place, inv_place = bank_(7, 2 * P, 0, VD), bank_(0, 2 * P, 0, VD)

        ffn_at = {0: 0, 2: 1, 3: 2, 5: 3}
        N_PRE = {0: 0, 1: 2, 2: 7, 3: 9, 4: 11, 5: 18}
        N_POST = {0: 1, 1: 6, 2: 8, 3: 10, 4: 17, 5: 19}
        N_CKV, N_CQ, N_LN, N_Q, N_K = 3, 4, 5, 12, 16
        LATENTS = (3, 4, 0, 1, 2)
        MOD_TILES = (5, 8, 11, 14)
        H_VECTOR, H_POOL = (0, 1, 2, 4, 6), (3, 5, 7)
        x_new, x_new_p, x_sq, x_sum = sem("x_new"), sem("x_new_p"), sem("x_sq"), sem("x_sum")
        h_t, h_f, h_hi, h_lo, h_lo_p, y_pre = (sem(n) for n in ("h_t", "h_f", "h_hi", "h_lo", "h_lo_p", "y_pre"))

        def wait_x(engine, version, k):
            if version == 0:
                engine.wait_ge(x_new, k + 1)
            elif k % 2 == 0:
                engine.wait_ge(x_new, 8 + 4 * (version - 1) + k // 2 + 1)
            else:
                engine.wait_ge(x_new_p, 4 * (version - 1) + k // 2 + 1)

        def wait_all_x(engine, version):
            wait_x(engine, version, KD - 2)
            wait_x(engine, version, KD - 1)

        def wait_h(engine, q, k):
            if k in H_POOL:
                engine.wait_ge(h_lo_p, len(H_POOL) * q + H_POOL.index(k) + 1)
            else:
                engine.wait_ge(h_lo, len(H_VECTOR) * q + H_VECTOR.index(k) + 1)

        def wait_all_h(engine, q):
            wait_h(engine, q, KD - 2)
            wait_h(engine, q, KD - 1)
        y_zero, y_done, y_sq, y_acc, y_sum, y_t = (sem(n) for n in ("y_zero", "y_done", "y_sq", "y_acc", "y_sum", "y_t"))
        n_ln, n_r0, n_r2, n_b, n_rstd = (sem(n) for n in ("n_ln", "n_r0", "n_r2", "n_b", "n_rstd"))
        silu_done, hid_f, hid_hi, hid_lo, down_done = (sem(n) for n in ("silu_done", "hid_f", "hid_hi", "hid_lo", "down_done"))
        consts_in, vecs_in, tok_loaded = sem("consts_in"), sem("vecs_in"), sem("tok_loaded")
        vec_t, vecs_ready, cond_f_ready, cond_hi, cond_ready = (sem(n) for n in ("vec_t", "vecs_ready", "cond_f_ready", "cond_hi", "cond_ready"))
        tok_t = sem("tok_t")
        rows_in, rows_sum, rows_full, rows_t, mod_ready, coef_ready = (
            sem(n) for n in ("rows_in", "rows_sum", "rows_full", "rows_t", "mod_ready", "coef_ready"))
        y_base = {0: 4, 1: 180, 2: 188, 3: 364, 4: 540, 5: 548}
        y_end = {0: 180, 1: 188, 2: 364, 3: 540, 4: 548, 5: 636}
        x_aside, x_back = sem("x_aside"), sem("x_back")

        @block.sync
        def _(sp):
            def load(i, per, c, src, k, n):
                if not known(i) or i * per + c >= RAWS:
                    sp.wait_ge(w_lo, i * per + (c - 1))
                dst = raw[:, c % RAWS, 0:k * n]
                if k > 1:
                    dst = dst.rearrange("p (k c) -> p k c", k=k)
                sp.dma_start(dst, src).then_inc(w_loaded[c % RAWS], 16)

            def ffn(q, l, s):
                b = BASE[q]
                gate, up, down = w_gate[l, s], w_up[l, s], w_down[l, s]

                def up_chunk(i, c, w, f):
                    at = f * P if known(i) else sp.snap(f * P)
                    load(i, 12, c, cols(w, at, P), KD, P)

                def down_chunk(i, c, f):
                    at = f * P if known(i) else sp.snap(f * P)
                    load(i, 12, c, down[bass.ds(at, P), :], 1, CHUNK)

                for j in range(4):
                    up_chunk(0, b + j, (gate, up)[j % 2], j // 2)
                with sp.Fori(0, 5) as i:
                    for half in range(2):
                        c0 = b + 4 + 6 * half
                        for j in range(6):
                            if j < 4:
                                up_chunk(i, c0 + j, (gate, up)[j % 2], i * 4 + (2 + 2 * half + j // 2))
                            else:
                                down_chunk(i, c0 + j, i * 4 + (2 * half + j - 4))
                for j in range(2):
                    down_chunk(0, b + 64 + j, FT - 2 + j)
                if q == 5:
                    down_chunk(0, b + 66, 0)

            def set_aside(version):
                wait_all_x(sp, version)
                sp.dma_start(x_scratch, x[:, :, :]).then_inc(x_aside, 16)

            def even_mixer():
                b = BASE[1]
                def in_tiles(i):
                    for c in range(4):
                        load(0, 4, b + 4 * i + c, cols(ev_w_in[0], (2 * i + c // 2) * P + (1 - c % 2) * CONV_CH, P), KD, P)
                in_tiles(0)
                set_aside(1)
                wait_all_h(sp, 1)
                sp.wait_ge(x_aside, 16)
                sp.dma_start(e_mats[:, :], consts[:, C_N384:C_B64]).then_inc(sem("e_consts"), 16)
                sp.dma_start(e_rope[:, :, :], consts[:, C_MROPE:C_MROPE + 2 * SEQ].rearrange(
                    "p (a t) -> p a t", a=2)).then_inc(sem("e_consts"), 16)
                in_tiles(1)
                for m in range(KQ + KKV):
                    load(0, 4, b + 8 + m, cols(ev_w_in[0], 2 * CONV_CH + m * P, P), KD, P)
                load(0, 4, b + 13, cols(ev_w_in[0], 2 * CONV_CH + Q_LORA + KV_LORA, ROPE), KD, ROPE)
                for k in range(KKV):
                    load(0, 4, b + E_V + k, w_ukv[0][k * P:(k + 1) * P, :], 1, CHUNK)
                with sp.Fori(0, 2) as i:
                    for e in range(2):
                        at = sp.snap(i * 4 * QK + e * 2 * QK)
                        load(i, 4, b + E_PAIR + 2 * e, cols(w_uq[0], at, 2 * QK), KQ, 2 * QK)
                        at = sp.snap(i * 4 + 2 * e)
                        keys = [w_ukv[0][k * P:(k + 1) * P, :].rearrange("p (h d) -> p h d", h=HEADS)[
                            :, bass.ds(at, 2), 0:NOPE] for k in range(KKV)]
                        c = b + E_PAIR + 2 * e + 1
                        done = sp.snap(i * 32 + 16 * (e + 1))
                        sp.wait_ge(w_lo, i * 4 + (c - 1))
                        for k in range(KKV):
                            if k == 1:
                                sp.wait_ge(sem("e_ukv"), done)
                            sp.dma_start(raw[:, c % RAWS, k * P:(k + 1) * P].rearrange("p (h d) -> p h d", h=2),
                                         keys[k]).then_inc(w_loaded[c % RAWS] if k else sem("e_ukv"), 16)
                out_chunk = lambda i, c: load(i, 4, b + E_OUT + c, cols(ev_w_out[0], i * 4 * P + c * P if known(i)
                                              else sp.snap(i * 4 * P + c * P), P), KD, P)
                for c in range(4):
                    out_chunk(0, c)
                sp.wait_ge(sem("e_ln_lo"), KC)
                sp.dma_start(x[:, :, :], x_scratch).then_inc(x_back, 16)
                for c in range(4, 8):
                    out_chunk(0, c)

            def odd_mixer():
                b = BASE[4]
                in_tiles = lambda m0, m1: [load(0, 4, b + m, cols(od_w_in[0], m * P, P), KD, P) for m in range(m0, m1)]
                in_tiles(0, 4)
                set_aside(4)
                wait_all_h(sp, 4)
                sp.wait_ge(x_aside, 32)
                for dst, at, n in ((o_mats[:, :, :], C_B64, 4 * P), (o_rope[:, :, :], C_GROPE, 2 * SEQ)):
                    sp.dma_start(dst, consts[:, at:at + n].rearrange("p (a t) -> p a t", a=dst.shape[1])).then_inc(
                        sem("o_consts"), 16)
                in_tiles(4, 10)
                for j in range(4):
                    load(0, 4, b + O_DFT + j, dft[j * P:(j + 1) * P, :], 1, CHUNK)
                out_chunk = lambda c: load(0, 4, b + O_OUT + c, cols(od_w_out[0], c * P, P), KD, P)
                for c in range(4):
                    out_chunk(c)
                sp.wait_ge(sem("o_lo"), 4 * ODD.n_g)
                sp.dma_start(x[:, :, :], x_scratch).then_inc(x_back, 16)
                for c in range(4, 8):
                    out_chunk(c)

            sp.dma_start(ident[:, :], consts[:, C_ID:C_N384]).then_inc(consts_in, 16)
            for row, src in ((V_GPRE, g_pre.rearrange("l s (k p) -> (l s k) p", p=P)),
                             (V_GPOST, g_post.rearrange("l s (k p) -> (l s k) p", p=P)),
                             (V_C, c_in.rearrange("b (k p) -> (b k) p", p=P)),
                             (V_CCTX, c_ctx_in.rearrange("(k p) -> k p", p=P)),
                             (V_CONVB, conv_b.rearrange("b (k p) -> (b k) p", p=P)),
                             (V_LNG, ln_g.rearrange("b (k p) -> (b k) p", p=P)),
                             (V_LNB, ln_b.rearrange("b (k p) -> (b k) p", p=P)),
                             (V_GCQ, g_cq.rearrange("b (k p) -> (b k) p", p=P)),
                             (127, g_cq.rearrange("b (k p) -> (b k) p", p=P)[0:1, :])):
                sp.dma_start(vec_in[row:row + src.shape[0], 0, :], src).then_inc(vecs_in, 16)
            for row, src, at, n in ((0, conv_w.rearrange("b k (c p) -> (b k c) p", p=P), 0, P),
                                    (124, g_ckv.rearrange("b (k p) -> (b k) p", p=P), 0, P),
                                    (126, g_qn, 0, HD), (126, g_qn, HD, HD), (127, g_kn, 0, HD), (127, g_kn, HD, HD)):
                sp.dma_start(vec_in[row:row + src.shape[0], 1, at:at + n], src).then_inc(vecs_in, 16)
            sp.dma_start(tok_in[:, 0:2, :], ctx_in[0].rearrange("(j p) d -> p j d", p=P)).then_inc(tok_loaded, 16)
            sp.dma_start(tok_in[:, 2:6, :], x_in[0].rearrange("(j p) d -> p j d", p=P)).then_inc(tok_loaded, 16)
            ffn(0, 0, 0)
            even_mixer()
            ffn(2, 0, 1)
            ffn(3, 1, 0)
            odd_mixer()
            ffn(5, 1, 1)
            for j in range(4):
                sp.wait_ge(sem("out_ready"), j + 1)
                sp.dma_start(out[0, j * P:(j + 1) * P, :], tok_in[:, j, :]).then_inc(sem("out_stored"), 16)
            sp.wait_ge(sem("out_stored"), 64)

        @block.gpsimd
        def _(pool):
            def load_mod(i, c, layer, unit, k):
                blocks = w_mod.rearrange("l r (u c) -> (l r u) c", c=CHUNK)
                b0 = layer * (9 * D - 9) + (unit + 9 * P * k)
                if not known(i):
                    b0 = pool.snap(b0)
                if not known(i) or i * 24 + c >= MOD_RAWS:
                    pool.wait_ge(m_lo, i * 24 + (c - 2))
                pool.dma_start(mod_raw[:, c % MOD_RAWS, :], blocks[bass.ds(b0, P, 9), :]).then_inc(
                    m_loaded[c % MOD_RAWS], 16)

            def store_row(i, u):
                at = 8 * u if known(i) else pool.snap(i * 24 + 8 * u)
                pool.wait_ge(row_ready, i * 3 + (u + 1))
                pool.dma_start(mod_scratch[bass.ds(at, 8)].rearrange("a s c -> s a c"),
                               mod_row[:, :].rearrange("s (a c) -> s a c", c=P)).then_inc(row_stored, 16)

            def zero_y(version):
                wait_all_x(pool, version)
                nc.gpsimd.memset(y[:, :, :], 0.0).then_inc(y_zero, 1)

            def post(q, segs):
                c0 = segs[0][0]
                for k in range(1, KD, 2):
                    pool.wait_ge(y_t, 8 * q + k + 1)
                    nc.gpsimd.tensor_tensor(x[:, k, c0:TOK], x[:, k, c0:TOK], t[:, k % 3, c0:TOK], ALU.add).then_inc(x_new_p, 1)

            def pre(q, segs):
                c0 = segs[0][0]
                for k in H_POOL:
                    pool.wait_ge(h_hi, 8 * q + k + 1)
                    nc.gpsimd.tensor_tensor(h[:, k, 1, c0:TOK], t[:, k % 3, c0:TOK], h[:, k, 0, c0:TOK].bitcast(F32),
                                            ALU.subtract).then_inc(h_lo_p, 1)

            for c in range(16):
                load_mod(0, c, 0, c // 8, c % 8)
                if c == 9:
                    store_row(0, 0)
            store_row(0, 1)
            pool.wait_ge(row_stored, 32)
            pool.dma_start(m_rows[0:16, 0, :, :], mod_scratch[0:16]).then_inc(rows_in, 16)
            pool.dma_start(m_bias[0:16, 0, :], b_mod[0].rearrange("(r c) -> r c", c=P)[0:16, :]).then_inc(rows_in, 16)
            for k in range(8):
                load_mod(0, 16 + k, 0, 2, k)
                if k == MOD_RAWS - 1:
                    pre(0, ALL)
            with pool.Fori(0, 5) as i:
                for m in range(24):
                    load_mod(i, 24 + m, (i + 1) // 3, i * 3 + (3 + m // 8), m % 8)
                    if m % 8 == 1:
                        store_row(i, 2 + m // 8)
            store_row(0, UNITS - 1)
            pool.wait_ge(row_stored, 16 * UNITS)
            pool.wait_ge(mod_ready, 1)
            pool.wait_ge(w_done, 64)
            for l in range(2):
                pool.dma_start(m_rows[0:72, l, :, :], mod_scratch[72 * l:72 * l + 72]).then_inc(rows_in, 16)
                pool.dma_start(m_bias[0:72, l, :], b_mod[l].rearrange("(r c) -> r c", c=P)).then_inc(rows_in, 16)
            post(0, ALL)
            pre(1, ALL)
            pool.wait_ge(x_aside, 16)
            wait_all_h(pool, 1)
            for at, n in ((0, HALO), (HALO + CTX, HALO), (HALO + GAPPED, HALO)):
                nc.gpsimd.memset(u[:, :, at:at + n], 0.0).then_inc(sem("e_zero"), 1)
            nc.gpsimd.memset(q_f[0:NOPE, 0, :], 0.0).then_inc(sem("e_zero"), 1)
            for c in range(2, KC):
                pool.wait_ge(sem("e_u"), c + 1)
                for k in range(CONV_K + 1):
                    n, m = (c - 2) * (CONV_K + 1) + k, (c - 2) * (CONV_K - 1) + k
                    src = u[:, c, k % CONV_K:k % CONV_K + GAPPED]
                    tap = vecs[:, V_CONVW + k * KC + c:V_CONVW + k * KC + c + 1]
                    if n:
                        pool.wait_ge(sem("e_conv_b"), n)
                    if k == 0:
                        ins = nc.gpsimd.tensor_scalar(sum_sq[:, :], src, tap, None, ALU.mult)
                    elif k < CONV_K:
                        nc.gpsimd.tensor_scalar(conv_tap[:, :], src, tap, None, ALU.mult).then_inc(sem("e_tap"), 1)
                        pool.wait_ge(sem("e_tap"), m)
                        ins = nc.gpsimd.tensor_tensor(sum_sq[:, :], sum_sq[:, :], conv_tap[:, :], ALU.add)
                    else:
                        ins = nc.gpsimd.tensor_scalar(u[:, c, 0:GAPPED], sum_sq[:, :],
                                                      vecs[:, V_CONVB + c:V_CONVB + c + 1], None, ALU.add)
                    ins.then_inc(sem("e_conv_b"), 1)
            post(1, ALL)
            pre(2, ALL)
            zero_y(2)
            post(2, ALL)
            pre(3, ALL)
            zero_y(3)
            post(3, ALL)
            pre(4, ALL)
            pool.wait_ge(x_aside, 32)
            wait_all_h(pool, 4)
            nc.gpsimd.memset(qz[:, :, :, :].bitcast(F32), 0.0).then_inc(sem("o_zero"), 1)
            post(4, XONLY)
            pre(5, XONLY)
            zero_y(5)
            post(5, XONLY)

        @block.tensor
        def _(pe):
            def weight(half, c, k, width, at=0, m=P):
                return w_half[half][:, c % SLOTS, k * width + at:k * width + at + m]

            def modulate(i, c):
                pe.wait_ge(m_lo, i * 24 + (c + 1))
                k = c % 8
                if k == 0 and (not known(i) or c > 0):
                    pe.wait_ge(row_ready, i * 3 + c // 8)
                for n in range(2):
                    for half in range(2):
                        mm = pe.matmul(bank_(6 + n, 512, 0, 4), cond[:, k, :, :].rearrange("p j h -> p (j h)"),
                                       m_half[half][:, c % MOD_SLOTS, n * 512:(n + 1) * 512],
                                       start=(k == 0 and half == 0), stop=(k == 7 and half == 1))
                mm.then_inc(m_done, 1)

            def project(i, per, c, place, segs, width=P, h_ready=None, mods=(), korder=range(KD), waits=None):
                pe.wait_ge(w_lo, i * per + (c + 1))
                for at, k in enumerate(korder):
                    if h_ready is not None:
                        wait_h(pe, h_ready, k)
                    if waits is not None:
                        waits(k)
                    for p_, (a, b_) in enumerate(PASSES):
                        for c0, n, _ in segs:
                            mm = pe.matmul(tile(place, c0, n, 0, width), weight(a, c, k, width, 0, width),
                                           h[:, k, b_, c0:c0 + n], start=(at == 0 and p_ == 0),
                                           stop=(at == KD - 1 and p_ == 2))
                    if at == 3 and mods:
                        modulate(i, mods[0])
                mm.then_inc(w_done, 1)
                if mods:
                    modulate(i, mods[1])

            def ffn(q, segs):
                b, fi = BASE[q], ffn_at[q]
                nt = KD * len(segs)
                tiles = down_tiles(q, segs)
                y0, d0 = y_base[q], 165 * fi

                def up(i, c, t, first, m0):
                    if q == 0 and not first:
                        pe.wait_ge(y_done, i * 2 * nt + (y0 + (t - 1) * nt - 2))
                    for j in range(4):
                        if j % 2 == 0:
                            pe.wait_ge(silu_done, i * 4 + (22 * fi + 2 * t + j // 2))
                        else:
                            pe.wait_ge(hid_f, i * 4 + (22 * fi + 2 * t + j // 2))
                        project(i, 12, c + j, 2 * (j % 2), segs, h_ready=q if first and j == 0 else None,
                                mods=(m0 + 2 * j, m0 + 2 * j + 1) if m0 is not None else ())

                def down(i, c, t, m0):
                    pe.wait_ge(w_lo, i * 12 + (c + 2))
                    pe.wait_ge(hid_lo, i * 4 + (22 * fi + 2 * t + 2))
                    if q == 0:
                        pe.wait_ge(silu_done, i * 4 + (22 * fi + min(2 * t + 4, 22)))
                    for idx, (d, (c0, n, _), place) in enumerate(tiles):
                        if idx >= 4 or known(i):
                            pe.wait_ge(y_done, i * 2 * nt + (y0 + t * nt + idx - 3))
                        for kk in range(2):
                            for p_, (a, b_) in enumerate(PASSES):
                                mm = pe.matmul(place, w_half[a][:, (c + kk) % SLOTS, d * P:(d + 1) * P],
                                               hid[:, t % 2, kk, b_, c0:c0 + n],
                                               start=(kk == 0 and p_ == 0), stop=(kk == 1 and p_ == 2))
                            if idx == nt - 1:
                                mm.then_inc(w_done, 1)
                        if idx < nt - 1:
                            mm.then_inc(down_done, 1)
                        if m0 is not None and idx in MOD_TILES:
                            modulate(i, m0 + MOD_TILES.index(idx))

                up(0, b, 0, True, 16 if q == 0 else None)
                with pe.Fori(0, 5) as i:
                    for half in range(2):
                        m0 = 24 + 12 * half if q == 0 else None
                        up(i, b + 4 + 6 * half, 1 + half, False, m0)
                        down(i, b + 8 + 6 * half, half, m0 + 8 if q == 0 else None)
                down(0, b + 64, 10, None)

            def add_squares(n, done, segs):
                pe.wait_ge(y_acc, done)
                for c0, w, _ in segs:
                    mm = pe.matmul(tile(0, c0, w), n1024, sum_sq[:, c0:c0 + w], start=True, stop=True)
                mm.then_inc(y_sum, 1)

            def square_x(q, segs, between=None):
                for k in range(KD):
                    pe.wait_ge(x_sq, 8 * q + k + 1)
                    for c0, w, _ in segs:
                        mm = pe.matmul(tile(2, c0, w), n1024, sq[:, k % 2, c0:c0 + w],
                                       start=(k == 0), stop=(k == KD - 1))
                    mm.then_inc(x_sum, 1)
                    if between:
                        between(k)

            def mod_rows(units_l, r, done):
                pe.wait_ge(rows_full, done)
                for l in range(units_l):
                    for j in range(2):
                        mm = pe.transpose(bank_(0)[:, (l * 2 + j) * 72:(l * 2 + j) * 72 + r],
                                          m_sum[0:r, l, j, :], idm[0:r, 0:r])
                mm.then_inc(rows_t, 1)

            def even_pair(i, e):
                b = BASE[1] + E_PAIR
                pair = lambda per, c: i * (2 * per) + (e * per + c)
                pe.wait_ge(w_lo, i * 4 + (b + 2 * e + 1))
                for hh in range(2):
                    for k in range(KQ):
                        for p_, (a, b_) in enumerate(PASSES):
                            for c0, n, _ in ALL:
                                mm = pe.matmul(tile(2 * hh, c0, n, 0, QK), weight(a, b + 2 * e, k, 2 * QK, hh * QK, QK),
                                               cn[:, k, b_, c0:c0 + n], start=(k == 0 and p_ == 0),
                                               stop=(k == KQ - 1 and p_ == 2))
                    mm.then_inc(sem("e_q") if hh == 0 else w_done, 1)

                def swap(hh):
                    pe.wait_ge(sem("e_qf"), pair(2, hh + 1))
                    pe.matmul(tile(2 * hh, CTX, SEQ, 0, QK), e_mats[0:QK, C_P96 - C_N384:C_P96 - C_N384 + QK],
                              q_f[0:QK, hh, CTX:TOK], start=True, stop=True).then_inc(sem("e_rot"), 1)

                swap(0)
                pe.wait_ge(w_lo, i * 4 + (b + 2 * e + 2))
                for k in range(KKV):
                    for p_, (a, b_) in enumerate(PASSES):
                        for c0, n, _ in ALL:
                            mm = pe.matmul(tile(4, c0, n), weight(a, b + 2 * e + 1, k, P), cn[:, KQ + k, b_, c0:c0 + n],
                                           start=(k == 0 and p_ == 0), stop=(k == KKV - 1 and p_ == 2))
                mm.then_inc(w_done, 1)
                swap(1)

                def product(a):
                    g, col, keys = EVEN.tiles[a]
                    hh = EVEN.groups[g][0]
                    if a in (0, EVEN.n_t // 2):
                        pe.wait_ge(sem("e_q_lo"), pair(2, hh + 1))
                        pe.wait_ge(sem("e_k_lo"), pair(2, hh + 1))
                    if a == 1:
                        pe.wait_ge(sem("e_qr"), pair(2, 2))
                    for p_, (qa, kb) in enumerate(PASSES):
                        for c0, n, _ in (ALL if keys == 6 else (SEG_C,)):
                            mm = pe.matmul(tile(2 * (a % 2), c0, n), q_h[0:QK, hh, qa, col:col + P],
                                           k_h[0:QK, hh, kb, c0:c0 + n], start=(p_ == 0), stop=(p_ == 2))
                    return mm

                attention(EVEN, pair, product, pair(1, 1))

            def attention(mx, pair, product, values_ready):
                def score(a):
                    if a >= 2:
                        pe.wait_ge(mx.sem("exp"), pair(mx.n_t, a - 1))
                    product(a).then_inc(mx.sem("s"), 1)

                def turn(a):
                    if mx is EVEN and a == 0:
                        pe.wait_ge(sem("e_k_lo"), pair(2, 2))
                    pe.wait_ge(mx.sem("exp"), pair(mx.n_t, a + 1))
                    for n in mx.of_tile(a):
                        _, k0, kn = mx.halves[n]
                        if n >= 3:
                            pe.wait_ge(mx.sem("pt_lo"), pair(mx.n_h, n - 2))
                        for k in range(kn):
                            mm = pe.transpose(turned(n, kn)[:, k * P:(k + 1) * P],
                                              mx.prob[:, a % 2, (k0 + k) * P:(k0 + k + 1) * P], idm)
                        mm.then_inc(mx.sem("tr"), 1)

                def inverse(g):
                    pe.wait_ge(mx.sem("dg"), pair(mx.n_g, g + 1))
                    pe.matmul(inv_place, n1024[:, 0:VD], mx.diag[:, :, :].rearrange("p a c -> p (a c)"),
                              start=True, stop=True).then_inc(mx.sem("inv"), 1)

                def values(g, part):
                    hh, _, keys = mx.groups[g]
                    if part == 0 and g >= 1:
                        pe.wait_ge(mx.sem("of"), pair(mx.n_g, g))
                    if part == 1:
                        pe.wait_ge(mx.sem("inv_out"), pair(mx.n_g, g + 1))
                    per = (keys + 1) // 2
                    last = mx.of_tile(2 * g + 1)[min(part, len(mx.of_tile(2 * g + 1)) - 1)]
                    pe.wait_ge(mx.sem("pt_lo"), pair(mx.n_h, last + 1))
                    at = hh * mx.vh_at
                    for kt in range(part * per, part * per + per):
                        for p_, (a, b_) in enumerate(PASSES):
                            mm = pe.matmul(pv_place, mx.vh[:, kt, a, at:at + VD], mx.pt[:, g % 2, kt, b_, :],
                                           start=(kt == 0 and p_ == 0), stop=(kt == keys - 1 and p_ == 2))
                    if part == 1:
                        mm.then_inc(mx.sem("pv"), 1)

                score(0)
                score(1)
                for a in range(mx.n_t):
                    turn(a)
                    if a >= 2 and a % 2 == 0:
                        inverse(a // 2 - 1)
                    if a + 2 < mx.n_t:
                        score(a + 2)
                    if a == 2:
                        pe.wait_ge(mx.sem("vh_lo"), values_ready)
                    if a >= 2:
                        values(a // 2 - 1, a % 2)
                inverse(mx.n_g - 1)
                values(mx.n_g - 1, 0)
                values(mx.n_g - 1, 1)

            def even_mixer():
                b = BASE[1]
                for c in range(8):
                    if c >= 2:
                        pe.wait_ge(sem("e_u" if c % 2 else "e_sig"), c // 2)
                    project(0, 4, b + c, 2 * (c % 2), ALL, h_ready=1 if c == 0 else None)
                for m in range(6):
                    if m == 0:
                        pe.wait_ge(sem("e_sig"), 4)
                    elif m == 1:
                        pe.wait_ge(sem("e_u"), 4)
                    else:
                        pe.wait_ge(sem("e_cf"), m - 1)
                    project(0, 4, b + 8 + m, 2 * (m % 2), ALL, width=P if m < 5 else ROPE)
                pe.wait_ge(sem("e_consts"), 32)
                for n_, m in enumerate(LATENTS):
                    pe.wait_ge(sem("e_csq"), n_ + 1)
                    at = (C_N384 if m < KQ else C_N256) - C_N384
                    for c0, n, _ in ALL:
                        mm = pe.matmul(tile(4 if m < KQ else 6, c0, n),
                                       e_mats[:, at:at + P], sq[:, n_ % 2, c0:c0 + n],
                                       start=(m in (0, KQ)), stop=(m in (KQ - 1, 4)))
                    mm.then_inc(sem("e_csum"), 1)
                pe.wait_ge(sem("e_cf"), 6)
                pe.wait_ge(sem("e_zero"), 4)
                pe.matmul(tile(0, CTX, SEQ, 0, QK), e_mats[0:QK, C_P96 - C_N384:C_P96 - C_N384 + QK],
                          q_f[0:QK, 0, CTX:TOK], start=True, stop=True).then_inc(sem("e_krot"), 1)
                pe.wait_ge(w_lo, b + E_V + 2)
                pe.wait_ge(sem("e_cn_lo"), KKV)
                for j in range(6):
                    if j >= 2:
                        pe.wait_ge(sem("e_v"), j - 1)
                    for k in range(KKV):
                        for p_, (a, b_) in enumerate(PASSES):
                            v_cols = w_half[b_][:, (b + E_V + k) % SLOTS, :].rearrange(
                                "p (h d) -> p h d", d=NOPE + VD)[:, :, NOPE:NOPE + VD]
                            mm = pe.matmul(bank_(2 + j % 2).rearrange("p (h d) -> p h d", d=VD),
                                           cn[:, KQ + k, a, j * P:(j + 1) * P], v_cols,
                                           start=(k == 0 and p_ == 0), stop=(k == KKV - 1 and p_ == 2))
                        if j == 5:
                            mm.then_inc(w_done, 1)
                    if j < 5:
                        mm.then_inc(sem("e_vmm"), 1)
                pe.wait_ge(sem("e_kpe_lo"), 2)
                pe.wait_ge(sem("e_v"), 6)
                pe.wait_ge(sem("e_cn_lo"), KKV + KQ)
                with pe.Fori(0, 2) as i:
                    for e in range(2):
                        even_pair(i, e)
                for n_ in range(2):
                    for c in range(KC):
                        if n_ == 0:
                            pe.wait_ge(sem("e_conv_a" if c < 2 else "e_conv_b"), (CONV_K + 1) * (c % 2 + 1))
                        else:
                            pe.wait_ge(sem("e_dsq"), c + 1)
                        for c0, n, _ in ALL:
                            at = (C_N256, C_N512)[n_] - C_N384
                            g0 = c0 + HALO if c0 else 0
                            src = u[:, c, g0:g0 + n] if n_ == 0 else sq[:, c % 2, c0:c0 + n]
                            mm = pe.matmul(tile(2 * n_, c0, n), e_mats[:, at:at + P], src,
                                           start=(c == 0), stop=(c == KC - 1))
                        mm.then_inc(sem("e_lsum"), 1)
                def attn_then_conv(k):
                    if k >= 4:
                        pe.wait_ge(sem("e_lo"), 4 * EVEN.n_g)
                    else:
                        pe.wait_ge(sem("e_ln_lo"), k + 1)
                for c in range(KD):
                    if c < 2:
                        pe.wait_ge(n_rstd, N_LN + 1)
                    else:
                        pe.wait_ge(y_done, y_base[1] + c - 1)
                    project(0, 4, b + E_OUT + c, 2 * (c % 2), ALL, korder=(4, 5, 6, 7, 0, 1, 2, 3),
                            waits=attn_then_conv if c == 0 else None)

            def odd_mixer():
                b = BASE[4]
                for m in range(10):
                    segs = ALL if m in (4, 5) else XONLY
                    if m >= 2:
                        pe.wait_ge(sem("o_pf"), m - 1)
                    project(0, 4, b + m, 2 * (m % 2), segs, h_ready=4 if m == 0 else None)
                    if m == 4:
                        pe.wait_ge(sem("o_consts"), 32)
                    if 6 <= m:
                        head_swap(m - 6)
                    if 5 <= m:
                        head_sum(m - 5)
                pe.wait_ge(sem("o_pf"), 9)
                for j in range(6):
                    mm = pe.transpose(tile(0, j * P, P), kv_f[:, 1, j * P:(j + 1) * P], idm)
                mm.then_inc(sem("o_vt"), 1)
                pe.wait_ge(sem("o_dftc"), 1)
                pe.wait_ge(w_lo, b + O_DFT + 4)
                for g in range(4):
                    pe.wait_ge(sem("o_f_lo"), g + 1)
                    for j in range(4):
                        if g * 4 + j >= 2:
                            pe.wait_ge(sem("o_ab_lo"), g * 4 + j - 1)
                        elif g == 0:
                            pe.wait_ge(sem("o_pf"), 10)
                            pe.wait_ge(sem("o_vtf"), 1)
                        for p_, (a, b_) in enumerate(PASSES):
                            mm = pe.matmul(bank_(2 * (j % 2), 2 * P), f_h[:, g % 2, a, j * P:(j + 1) * P], dft_c[:, b_, :],
                                           start=(p_ == 0), stop=(p_ == 2))
                        mm.then_inc(sem("o_ab"), 1)
                    if g == 1:
                        head_swap(4)
                    if g >= 1:
                        pe.wait_ge(sem("o_fn_lo"), g)
                    pe.wait_ge(sem("o_ab_lo"), 4 * g + 4)
                    for j in range(4):
                        for t_ in range(2):
                            for p_, (a, b_) in enumerate(PASSES):
                                mm = pe.matmul(bank_(4), ab[:, j, a, t_ * P:(t_ + 1) * P],
                                               w_half[b_][:, (b + O_DFT + j) % SLOTS, t_ * 512:(t_ + 1) * 512],
                                               start=(j == 0 and t_ == 0 and p_ == 0), stop=(j == 3 and t_ == 1 and p_ == 2))
                        if g == 3:
                            mm.then_inc(w_done, 1)
                    if g < 3:
                        mm.then_inc(sem("o_fn"), 1)
                pe.wait_ge(sem("o_kd"), 4)
                pe.wait_ge(sem("o_fn_lo"), 4)
                with pe.Fori(0, 2) as i:
                    for e in range(2):
                        odd_pair(i, e)
                for c in range(KD):
                    if c < 2:
                        pe.wait_ge(sem("o_lo"), 4 * ODD.n_g)
                    else:
                        pe.wait_ge(y_done, y_base[4] + c - 1)
                    project(0, 4, b + O_OUT + c, 2 * (c % 2), XONLY)

            def head_sum(m):
                pe.wait_ge(sem("o_qsq"), m + 1)
                if m:
                    pe.wait_ge(n_rstd, N_Q + m)
                for c0, w, _ in (XONLY if m < 4 else ALL):
                    mm = pe.matmul(tile(6, c0, w), o_mats[:, 0, :], sq[:, m % 2, c0:c0 + w], start=True, stop=True)
                mm.then_inc(sem("o_qsum"), 1)

            def head_swap(m):
                pe.wait_ge(sem("o_qn"), m + 1)
                if m:
                    pe.wait_ge(sem("o_rp"), m)
                src = q4[:, m, :] if m < 4 else kv_f[:, 0, CTX:TOK]
                pe.matmul(bank_(5), o_mats[:, 1, :], src, start=True, stop=True).then_inc(sem("o_rot"), 1)

            def odd_pair(i, e):
                pair = lambda per, c: i * (2 * per) + (e * per + c)

                def product(a):
                    g, col, _ = ODD.tiles[a]
                    hh = ODD.groups[g][0]
                    if a in (0, ODD.n_t // 2):
                        pe.wait_ge(sem("o_qz_lo"), pair(2, hh + 1))
                    for p_, (qa, kb) in enumerate(PASSES):
                        for c0, n, _ in ALL:
                            keys = k_dup[:, bass.ds(i, 1), kb, c0:c0 + n].rearrange("p a c -> p (a c)")
                            mm = pe.matmul(tile(2 * (a % 2), c0, n), qz[:, hh, qa, col - CTX:col - CTX + P], keys,
                                           start=(p_ == 0), stop=(p_ == 2))
                    return mm

                attention(ODD, pair, product, i + 1)

            pe.wait_ge(consts_in, 16)
            pe.wait_ge(vecs_in, 16 * 15)
            for j in range(2):
                mm = pe.transpose(bank_(0)[:, j * P:(j + 1) * P], vec_in[:, j, :], idm)
            mm.then_inc(vec_t, 1)
            pe.wait_ge(cond_ready, 1)
            for c in range(8):
                modulate(0, c)
            pe.wait_ge(tok_loaded, 32)
            for k in range(KD):
                if k >= 2:
                    pe.wait_ge(x_new, k - 1)
                for j in range(6):
                    mm = pe.transpose(tile(2 * (k % 2), j * P, P), tok_in[:, j, k * P:(k + 1) * P], idm)
                mm.then_inc(tok_t, 1)
            pe.wait_ge(x_new, KD)
            square_x(0, ALL, lambda k: modulate(0, 8 + k))
            mod_rows(1, 16, 1)
            pe.wait_ge(mod_ready, 1)
            ffn(0, ALL)
            mod_rows(2, 72, 2)
            pe.wait_ge(mod_ready, 2)
            add_squares(0, 8, ALL)
            square_x(1, ALL)
            even_mixer()
            add_squares(1, 16, ALL)
            square_x(2, ALL)
            ffn(2, ALL)
            add_squares(2, 24, ALL)
            square_x(3, ALL)
            ffn(3, ALL)
            add_squares(3, 32, ALL)
            square_x(4, ALL)
            odd_mixer()
            add_squares(4, 40, XONLY)
            square_x(5, XONLY)
            ffn(5, XONLY)
            add_squares(5, 48, XONLY)
            for j in range(4):
                wait_all_x(pe, 6)
                if j >= 2:
                    pe.wait_ge(sem("out_ready"), j - 1)
                for k in range(KD):
                    mm = pe.transpose(bank_(2 + 2 * (j % 2) + k // 4)[:, k % 4 * P:(k % 4 + 1) * P],
                                      x[:, k, CTX + j * P:CTX + (j + 1) * P], idm)
                mm.then_inc(sem("out_t"), 1)

        @block.scalar
        def _(act):
            copy = lambda dst, src: nc.scalar.activation(dst, src, ACT.Copy)
            norm_table = lambda: nc.scalar.preload_act_table_set("natural_log_exp_and_others")

            def split(i, per, c):
                act.wait_ge(w_loaded[c % RAWS], i * (8 * per) + 16 * (c // RAWS + 1))
                if not known(i) or i * per + c >= SLOTS:
                    act.wait_ge(w_done, i * per + (c - SLOTS + 1))
                copy(w_half[0][:, c % SLOTS, :], raw[:, c % RAWS, :]).then_inc(w_hi, 1)

            def split_mod(i, c):
                act.wait_ge(m_loaded[c % MOD_RAWS], i * (24 * 16 // MOD_RAWS) + 16 * (c // MOD_RAWS + 1))
                if not known(i) or i * 24 + c >= MOD_SLOTS:
                    act.wait_ge(m_done, i * 24 + (c - 1))
                copy(m_half[0][:, c % MOD_SLOTS, :], mod_raw[:, c % MOD_RAWS, :]).then_inc(m_hi, 1)

            def take_row(i, c):
                act.wait_ge(m_done, i * 24 + (c + 1))
                if c // 8 or not known(i):
                    act.wait_ge(row_stored, i * 48 + 16 * (c // 8))
                copy(mod_row[:, :], ps[0:4, 6 * 512:8 * 512]).then_inc(row_ready, 1)

            def norm(n, src, ra, rb, wait, count):
                act.wait_ge(wait, count)
                nc.scalar.activation(ra, src, ACT.Ln, scale=-2.0, bias=EPS).then_inc(n_ln, 1)
                act.wait_ge(n_ln, n + 1)
                nc.scalar.activation(rb, ra, ACT.Exp, scale=-0.5).then_inc(n_r0, 1)
                act.wait_ge(n_r0, n + 1)
                nc.scalar.activation(ra, rb, ACT.Square).then_inc(n_r2, 1)

            def places(segs):
                return segs[0][0], TOK - segs[0][0]

            def square_x(q, segs, between=None):
                c0, n = places(segs)
                for k in range(KD):
                    wait_x(act, q, k)
                    if k >= 2:
                        act.wait_ge(x_sum, 8 * q + k - 1)
                    nc.scalar.activation(sq[:, k % 2, c0:c0 + n], x[:, k, c0:c0 + n], ACT.Square).then_inc(x_sq, 1)
                    if between:
                        between(k)

            def pre(q, segs):
                c0, n = places(segs)
                norm(N_PRE[q], tile(2, c0, n), t[:, 0, c0:c0 + n], t[:, 1, c0:c0 + n], x_sum, 8 * q + KD)
                for k in range(KD):
                    act.wait_ge(h_t, 8 * q + k + 1)
                    for c0_, n_, j in segs:
                        t_k = t[:, k % 3, c0_:c0_ + n_]
                        ins = nc.scalar.activation(t_k if k in H_POOL else h[:, k, 0, c0_:c0_ + n_], t_k, ACT.Identity,
                                                   bias=mod[:, q, 0, k, j:j + 1])
                    if k in H_POOL:
                        ins.then_inc(h_f, 1)
                        act.wait_ge(h_f, len(H_POOL) * q + H_POOL.index(k) + 1)
                        copy(h[:, k, 0, c0:TOK], t[:, k % 3, c0:TOK]).then_inc(h_hi, 1)
                    else:
                        ins.then_inc(h_hi, 1)

            def square_y(q, k, segs, n_tiles):
                c0, n = places(segs)
                act.wait_ge(y_done, y_end[q] - n_tiles * (KD - 1 - k))
                if k >= 2:
                    act.wait_ge(y_acc, 8 * q + k - 1)
                nc.scalar.activation(sq[:, k % 2, c0:c0 + n], y[:, k, c0:c0 + n], ACT.Square).then_inc(y_sq, 1)
                if q:
                    premultiply(q, k, segs)

            def premultiply(q, k, segs):
                act.wait_ge(y_sq, 8 * q + k + 1)
                for c0, n, j in segs:
                    ins = nc.scalar.activation(y[:, k, c0:c0 + n], y[:, k, c0:c0 + n], ACT.Identity,
                                               scale=coef_post[:, q, k, j:j + 1])
                ins.then_inc(y_pre, 1)

            def post(q, segs):
                c0, n = places(segs)
                norm(N_POST[q], tile(0, c0, n), t[:, 0, c0:c0 + n], t[:, 1, c0:c0 + n], y_sum, q + 1)
                if q == 0:
                    act.wait_ge(coef_ready, 2)
                    for k in range(KD):
                        premultiply(0, k, segs)

            def ffn(q, segs):
                b, fi = BASE[q], ffn_at[q]
                c0, n = places(segs)

                def up(i, c, t_, m0):
                    for j in range(4):
                        split(i, 12, c + j + 3)
                        if m0 is not None:
                            if m0 + 2 * j > 16:
                                split_mod(i, m0 + 2 * j)
                                split_mod(i, m0 + 2 * j + 1)
                            if (m0 + 2 * j + 1) % 8 == 7:
                                take_row(i, m0 + 2 * j + 1)
                        f = 22 * fi + 2 * t_ + j // 2
                        if j % 2 == 0:
                            act.wait_ge(w_done, i * 12 + (c + j + 1))
                            act.wait_ge(hid_f, i * 4 + f)
                            nc.scalar.activation(sq[:, 0, c0:c0 + n], tile(0, c0, n), ACT.Silu).then_inc(silu_done, 1)
                        else:
                            act.wait_ge(hid_f, i * 4 + (f + 1))
                            copy(hid[:, t_ % 2, j // 2, 0, c0:c0 + n], sq[:, 1, c0:c0 + n]).then_inc(hid_hi, 1)

                def down(i, c, m0):
                    split(i, 12, c + 3)
                    if m0 is not None:
                        for e in range(4):
                            split_mod(i, m0 + e)
                            if (m0 + e) % 8 == 7:
                                take_row(i, m0 + e)
                    split(i, 12, c + 4)

                up(0, b, 0, 16 if q == 0 else None)
                with act.Fori(0, 5) as i:
                    for half in range(2):
                        m0 = 24 + 12 * half if q == 0 else None
                        up(i, b + 4 + 6 * half, 1 + half, m0)
                        down(i, b + 8 + 6 * half, m0 + 8 if q == 0 else None)
                norm_table()
                if q != 5:
                    split(0, 12, b + 64 + 3)
                for k in range(KD):
                    square_y(q, k, segs, len(segs))
                if q != 5:
                    split(0, 12, b + 64 + 4)

            def even_pair(i, e):
                b = BASE[1] + E_PAIR
                pair = lambda per, c: i * (2 * per) + (e * per + c)
                at = act.snap(i * 4 * VD + 2 * e * VD)
                copy(e_vh[:, :, 0, :], v_all[:, :, bass.ds(at, 2 * VD)]).then_inc(sem("e_vh_hi"), 1)
                for hh in range(2):
                    if hh == 0:
                        act.wait_ge(sem("e_q"), pair(1, 1))
                    else:
                        act.wait_ge(w_done, i * 4 + (b + 2 * e + 1))
                    nc.scalar.activation(q_f[0:QK, hh, :], tile(2 * hh, 0, TOK, 0, QK), ACT.Copy,
                                         scale=MLA_SCALE).then_inc(sem("e_qf"), 1)
                act.wait_ge(w_done, i * 4 + (b + 2 * e + 2))
                for hh in range(2):
                    copy(k_h[0:NOPE, hh, 0, :], tile(4, 0, TOK, hh * NOPE, (hh + 1) * NOPE)).then_inc(sem("e_k_hi"), 1)
                    act.wait_ge(sem("e_qr"), pair(2, hh + 1))
                    copy(q_h[0:QK, hh, 0, :], q_f[0:QK, hh, :]).then_inc(sem("e_q_hi"), 1)
                attention(EVEN, i, e, pair, lambda n: split(i, 4, b + 2 * e + n))

            def attention(mx, i, e, pair, ahead=None):
                at = act.snap(i * 2 + (mx.out_at + e))
                for s_ in range(mx.n_t + 5):
                    if ahead and s_ == mx.n_t + 3:
                        ahead(3)
                    if 0 <= s_ - 2 < mx.n_t:
                        a = s_ - 2
                        g = a // 2
                        for n in mx.of_tile(a):
                            _, k0, kn = mx.halves[n]
                            act.wait_ge(mx.sem("tr"), pair(mx.n_h, n + 1))
                            if g >= 2 and a % 2 == 0 and k0 == 0:
                                act.wait_ge(mx.sem("pv"), pair(mx.n_g, g - 1))
                            copy(mx.pt[:, g % 2, k0:k0 + kn, 0, a % 2 * P:(a % 2 + 1) * P],
                                 turned(n, kn).rearrange("p (k q) -> p k q", q=P)).then_inc(mx.sem("pt_hi"), 1)
                    if s_ < mx.n_t:
                        a, keys = s_, mx.tiles[s_][2] * P
                        act.wait_ge(mx.sem("nm"), pair(mx.n_t, a + 1))
                        if a >= 2:
                            act.wait_ge(mx.sem("tr"), pair(mx.n_h, mx.of_tile(a - 2)[-1] + 1))
                        if a >= 4 and a % 2 == 0:
                            act.wait_ge(mx.sem("ri"), pair(mx.n_g, a // 2 - 1))
                        nc.scalar.activation(mx.prob[:, a % 2, 0:keys], tile(2 * (a % 2), 0, keys), ACT.Exp,
                                             bias=small[:, a % 2:a % 2 + 1], scale=1.0,
                                             accum_out=small[:, 2 + a % 4:3 + a % 4]).then_inc(mx.sem("exp"), 1)
                    if s_ >= 6 and s_ % 2 == 0:
                        g = (s_ - 6) // 2
                        hh, col, _ = mx.groups[g]
                        r = slice(hh * VD, (hh + 1) * VD)
                        act.wait_ge(mx.sem("of"), pair(mx.n_g, g + 1))
                        copy(h[r, bass.ds(at, 1), 0, col:col + 2 * P].rearrange("p a c -> p (a c)"),
                             sq[r, g % 2, 0:2 * P]).then_inc(mx.sem("hi"), 1)
                if ahead:
                    ahead(4)

            def even_mixer():
                b = BASE[1]
                act.wait_ge(x_aside, 16)
                for c in range(8):
                    split(0, 4, b + c + 3)
                    if c % 2 == 0:
                        act.wait_ge(w_done, b + c + 1)
                        if c:
                            act.wait_ge(sem("e_u"), c // 2)
                        nc.scalar.activation(sq[:, 0, :], tile(0), ACT.Sigmoid).then_inc(sem("e_sig"), 1)
                norm_table()
                for m in range(6):
                    split(0, 4, b + 8 + m + 3)
                    act.wait_ge(w_done, b + 8 + m + 1)
                    if m < 5:
                        copy(cqkv[:, m, :], tile(2 * (m % 2))).then_inc(sem("e_cf"), 1)
                    else:
                        copy(q_f[NOPE:QK, 0, :], tile(2, 0, TOK, 0, ROPE)).then_inc(sem("e_cf"), 1)
                for n_, m in enumerate(LATENTS):
                    act.wait_ge(sem("e_cf"), m + 1)
                    if n_ >= 2:
                        act.wait_ge(sem("e_csum"), n_ - 1)
                    else:
                        act.wait_ge(sem("e_u"), 4)
                    nc.scalar.activation(sq[:, n_ % 2, :], cqkv[:, m, :], ACT.Square).then_inc(sem("e_csq"), 1)

                def values_out(j):
                    if j < 5:
                        act.wait_ge(sem("e_vmm"), j + 1)
                    else:
                        act.wait_ge(w_done, b + E_V + 2)
                    copy(v_all[:, j, :], bank_(2 + j % 2)).then_inc(sem("e_v"), 1)

                for number, place, ms, done in ((N_CKV, 6, LATENTS[:2], 2), (N_CQ, 4, LATENTS[2:], 5)):
                    norm(number, tile(place), prob[:, 0, :], prob[:, 1, :], sem("e_csum"), done)
                    if number == N_CQ:
                        values_out(0)
                    for n_, m in enumerate(ms):
                        act.wait_ge(sem("e_ct"), done - len(ms) + n_ + 1)
                        copy(cn[:, m, 0, :], cqkv[:, m, :]).then_inc(sem("e_cn_hi"), 1)
                        if number == N_CQ:
                            values_out(n_ + 1)
                    if number == N_CKV:
                        act.wait_ge(n_rstd, N_CKV + 1)
                for j in range(4, 6):
                    values_out(j)
                act.wait_ge(sem("e_cn_lo"), 5)
                act.wait_ge(sem("e_kr"), 1)
                for hh in range(2):
                    copy(k_h[NOPE:QK, hh, 0, :], q_f[NOPE:QK, 0, :]).then_inc(sem("e_kpe_hi"), 1)
                split(0, 4, b + E_V + 3)
                split(0, 4, b + E_V + 4)
                act.wait_ge(sem("e_v"), 6)
                act.wait_ge(sem("e_kpe_lo"), 2)
                with act.Fori(0, 2) as i:
                    for e in range(2):
                        even_pair(i, e)
                for c in range(KC):
                    act.wait_ge(sem("e_d"), c + 1)
                    if c >= 2:
                        act.wait_ge(sem("e_lsum"), KC + c - 1)
                    for c0, n, _ in ALL:
                        g0 = c0 + HALO if c0 else 0
                        ins = nc.scalar.activation(sq[:, c % 2, c0:c0 + n], u[:, c, g0:g0 + n], ACT.Square)
                    ins.then_inc(sem("e_dsq"), 1)
                norm(N_LN, tile(2), prob[:, 0, :], prob[:, 1, :], sem("e_lsum"), 2 * KC)
                for c in range(KC):
                    act.wait_ge(sem("e_lt"), c + 1)
                    nc.scalar.activation(sq[:, c % 2, :], sq[:, c % 2, :], ACT.Silu, scale=vecs[:, V_LNG + c:V_LNG + c + 1],
                                         bias=vecs[:, V_LNB + c:V_LNB + c + 1]).then_inc(sem("e_act"), 1)
                    act.wait_ge(sem("e_act"), c + 1)
                    copy(h[:, c, 0, :], sq[:, c % 2, :]).then_inc(sem("e_ln_hi"), 1)
                norm_table()
                for c in range(KD):
                    split(0, 4, b + E_OUT + c + 3)
                    if c == 0:
                        act.wait_ge(sem("e_ln_lo"), KC)
                    square_y(1, c, ALL, 1)

            def odd_mixer():
                b = BASE[4]
                act.wait_ge(x_aside, 32)
                for m in range(10):
                    split(0, 4, b + m + 3)
                    act.wait_ge(w_done, b + m + 1)
                    place = 2 * (m % 2)
                    if m < 4:
                        ins = copy(q4[:, m, :], tile(place, CTX, SEQ))
                    elif m < 6:
                        ins = copy(kv_f[:, m - 4, :], tile(place))
                    else:
                        ins = copy(f4[:, m - 6, :], tile(place, CTX, SEQ))
                    ins.then_inc(sem("o_pf"), 1)
                    if m == 4:
                        act.wait_ge(sem("o_consts"), 32)
                        copy(dft_c[:, 0, :], o_mats[:, 2:4, :].rearrange("p a c -> p (a c)")).then_inc(sem("o_dft_hi"), 1)
                        head_square(0)
                    if m >= 5:
                        norm_head(m - 5)
                        if m < 9:
                            head_square(m - 4)
                act.wait_ge(sem("o_vt"), 1)
                copy(v_t[:, :, :].rearrange("p j c -> p (j c)"), tile(0)).then_inc(sem("o_vtf"), 1)
                split(0, 4, b + O_DFT + 3)

                def group_hi(g):
                    act.wait_ge(sem("o_pf"), 7 + g)
                    if g >= 2:
                        act.wait_ge(sem("o_ab"), 4 * (g - 1))
                    copy(f_h[:, g % 2, 0, :], f4[:, g, :]).then_inc(sem("o_f_hi"), 1)

                group_hi(0)
                for g in range(4):
                    if g == 2:
                        act.wait_ge(sem("o_rp"), 5)
                        for n in range(GQA_KV):
                            r = slice(n * HD, (n + 1) * HD)
                            copy(k_dup[r, n, 0, :], kv_f[r, 0, :]).then_inc(sem("o_k_hi"), 1)
                    for j in range(4):
                        act.wait_ge(sem("o_ab"), 4 * g + j + 1)
                        if g:
                            act.wait_ge(sem("o_fn"), g)
                        copy(ab[:, j, 0, :], bank_(2 * (j % 2), 2 * P)).then_inc(sem("o_ab_hi"), 1)
                    if g < 3:
                        group_hi(g + 1)
                    if g < 3:
                        act.wait_ge(sem("o_fn"), g + 1)
                    else:
                        act.wait_ge(w_done, b + O_DFT + 4)
                    copy(h[:, 4 + g, 0, CTX:TOK], bank_(4)).then_inc(sem("o_fn_hi"), 1)
                act.wait_ge(sem("o_vtf"), 1)
                act.wait_ge(sem("o_zero"), 1)
                with act.Fori(0, 2) as i:
                    at = act.snap(i * HD)
                    copy(o_vh[:, :, 0, :], v_t[:, :, bass.ds(at, HD)]).then_inc(sem("o_vh_hi"), 1)
                    for e in range(2):
                        odd_pair(i, e)
                for c in range(1, 4):
                    split(0, 4, b + O_DFT + c + 3)
                for c in range(KD):
                    split(0, 4, b + O_OUT + c + 3)
                    square_y(4, c, XONLY, 1)

            def head_square(m):
                act.wait_ge(sem("o_pf"), m + 1)
                if m >= 2:
                    act.wait_ge(sem("o_qsum"), m - 1)
                n = SEQ if m < 4 else TOK
                src = q4[:, m, :] if m < 4 else kv_f[:, 0, :]
                nc.scalar.activation(sq[:, m % 2, TOK - n:TOK], src, ACT.Square).then_inc(sem("o_qsq"), 1)

            def norm_head(m):
                n = SEQ if m < 4 else TOK
                if m:
                    act.wait_ge(n_rstd, N_Q + m)
                norm(N_Q + m, tile(6, TOK - n, n), o_prob[:, 0, TOK - n:TOK], o_prob[:, 1, TOK - n:TOK],
                     sem("o_qsum"), m + 1)

            def odd_pair(i, e):
                pair = lambda per, c: i * (2 * per) + (e * per + c)
                at = act.snap(i * 2 + e)
                for hh in range(2):
                    r = slice(hh * HD, (hh + 1) * HD)
                    nc.scalar.activation(qz[r, hh, 0, :], q4[r, bass.ds(at, 1), :].rearrange("p a c -> p (a c)"), ACT.Copy,
                                         scale=GQA_SCALE).then_inc(sem("o_qz_hi"), 1)
                attention(ODD, i, e, pair)

            act.wait_ge(vecs_ready, 1)
            nc.scalar.activation(cond_f[:, :, :].rearrange("p j k -> p (j k)"), vecs[:, V_C:V_C + 2 * KD],
                                 ACT.Silu).then_inc(cond_f_ready, 1)
            norm_table()
            act.wait_ge(cond_f_ready, 1)
            copy(cond[:, :, :, 0].rearrange("p k j -> p j k"), cond_f[:, :, :]).then_inc(cond_hi, 1)
            for c in range(8):
                split_mod(0, c)
            take_row(0, 7)
            square_x(0, ALL, lambda k: split_mod(0, 8 + k))
            take_row(0, 15)
            for c in range(3):
                split(0, 4, c)
            for c in (16, 17):
                split_mod(0, c)
            pre(0, ALL)
            ffn(0, ALL)
            post(0, ALL)
            square_x(1, ALL)
            pre(1, ALL)
            even_mixer()
            post(1, ALL)
            square_x(2, ALL)
            pre(2, ALL)
            ffn(2, ALL)
            post(2, ALL)
            square_x(3, ALL)
            pre(3, ALL)
            ffn(3, ALL)
            post(3, ALL)
            square_x(4, ALL)
            pre(4, ALL)
            odd_mixer()
            post(4, XONLY)
            square_x(5, XONLY)
            pre(5, XONLY)
            ffn(5, XONLY)
            post(5, XONLY)

        @block.vector
        def _(dve):
            tt, stt, copy = nc.vector.tensor_tensor, nc.vector.scalar_tensor_tensor, nc.vector.tensor_copy

            def f(ap):
                return ap.bitcast(F32)

            def split(i, per, c):
                dve.wait_ge(w_hi, i * per + (c + 1))
                tt(w_half[1][:, c % SLOTS, :], raw[:, c % RAWS, :], f(w_half[0][:, c % SLOTS, :]),
                   ALU.subtract).then_inc(w_lo, 1)

            def split_mod(i, c):
                dve.wait_ge(m_hi, i * 24 + (c + 1))
                tt(m_half[1][:, c % MOD_SLOTS, :], mod_raw[:, c % MOD_RAWS, :], f(m_half[0][:, c % MOD_SLOTS, :]),
                   ALU.subtract).then_inc(m_lo, 1)

            def norm(n, src, ra, rb, out_):
                dve.wait_ge(n_r2, n + 1)
                stt(ra, src, -0.5 * EPS, ra, ALU.add, ALU.mult).then_inc(n_b, 1)
                dve.wait_ge(n_b, n + 1)
                stt(out_, ra, 1.5, rb, ALU.add, ALU.mult).then_inc(n_rstd, 1)
                dve.wait_ge(n_rstd, n + 1)

            def places(segs):
                return segs[0][0], TOK - segs[0][0]

            def pre(q, segs):
                c0, n = places(segs)
                norm(N_PRE[q], tile(2, c0, n), t[:, 0, c0:c0 + n], t[:, 1, c0:c0 + n], rstd[:, c0:c0 + n])
                for k in range(KD + 1):
                    if k < KD:
                        if k >= 3:
                            wait_h(dve, q, k - 3)
                        for c0, n, j in segs:
                            ins = stt(t[:, k % 3, c0:c0 + n], x[:, k, c0:c0 + n], coef_pre[:, q, k, j:j + 1],
                                      rstd[:, c0:c0 + n], ALU.mult, ALU.mult)
                        ins.then_inc(h_t, 1)
                    if k - 1 in H_VECTOR:
                        dve.wait_ge(h_hi, 8 * q + k)
                        for c0, n, j in segs:
                            ins = stt(h[:, k - 1, 1, c0:c0 + n], t[:, (k - 1) % 3, c0:c0 + n], mod[:, q, 0, k - 1, j:j + 1],
                                      f(h[:, k - 1, 0, c0:c0 + n]), ALU.add, ALU.subtract)
                        ins.then_inc(h_lo, 1)

            def add_square(q, k, segs):
                c0, n = places(segs)
                dve.wait_ge(y_sq, 8 * q + k + 1)
                if k == 0:
                    copy(sum_sq[:, c0:c0 + n], sq[:, 0, c0:c0 + n]).then_inc(y_acc, 1)
                else:
                    dve.wait_ge(y_acc, 8 * q + k)
                    tt(sum_sq[:, c0:c0 + n], sum_sq[:, c0:c0 + n], sq[:, k % 2, c0:c0 + n], ALU.add).then_inc(y_acc, 1)

            def post(q, segs):
                c0, n = places(segs)
                norm(N_POST[q], tile(0, c0, n), t[:, 0, c0:c0 + n], t[:, 1, c0:c0 + n], rstd[:, c0:c0 + n])
                for k in range(KD + 1):
                    if k < KD:
                        dve.wait_ge(y_pre, 8 * q + k + 1)
                        if k >= 3:
                            wait_x(dve, q + 1, k - 3)
                        tt(t[:, k % 3, c0:c0 + n], y[:, k, c0:c0 + n], rstd[:, c0:c0 + n], ALU.mult).then_inc(y_t, 1)
                    if k % 2 == 1:
                        dve.wait_ge(y_t, 8 * q + k)
                        tt(x[:, k - 1, c0:c0 + n], x[:, k - 1, c0:c0 + n], t[:, (k - 1) % 3, c0:c0 + n],
                           ALU.add).then_inc(x_new, 1)

            def columns(layers, r, done):
                dve.wait_ge(rows_in, 32 if done == 1 else 96)
                for l in range(layers):
                    tt(m_sum[0:r, l, :, :], m_rows[0:r, l, 0:4:2, :], m_rows[0:r, l, 1:4:2, :], ALU.add).then_inc(rows_sum, 1)
                dve.wait_ge(rows_sum, 1 if done == 1 else 3)
                for l in range(layers):
                    for j in range(2):
                        ins = tt(m_sum[0:r, l, j, :], m_sum[0:r, l, j, :], m_bias[0:r, l, :], ALU.add)
                ins.then_inc(rows_full, 1)
                dve.wait_ge(rows_t, done)
                flat = mod[:, :, :, :, :].rearrange("p q a k j -> p (q a k) j")
                for l in range(layers):
                    for j in range(2):
                        ins = copy(flat[:, 72 * l:72 * l + r, j], bank_(0)[:, (l * 2 + j) * 72:(l * 2 + j) * 72 + r])
                ins.then_inc(mod_ready, 1)
                dve.wait_ge(mod_ready, done)
                gain = lambda at, q0, q1: vecs[:, at:at + 6 * KD].rearrange("p (q k) -> p q k", k=KD)[:, q0:q1, :]
                nq = 1 if done == 1 else 6
                for j in range(2):
                    ins = stt(coef_pre[:, 0:nq, :, j], mod[:, 0:nq, 1, :, j], 1.0, gain(V_GPRE, 0, nq), ALU.add, ALU.mult)
                    if done == 2:
                        for q in range(6):
                            ins = stt(coef_post[:, q, :, j], mod[:, q, 2, :, j], 1.0 if q % 3 == 1 else 0.5,
                                      gain(V_GPOST, q, q + 1).rearrange("p q k -> p (q k)"), ALU.mult, ALU.mult)
                ins.then_inc(coef_ready, 1)
                dve.wait_ge(coef_ready, done)

            def ffn(q, segs):
                b, fi = BASE[q], ffn_at[q]
                c0, n = places(segs)
                nt = KD * len(segs)
                tiles = down_tiles(q, segs)

                def up(i, c, t_, m0):
                    for j in range(4):
                        split(i, 12, c + j + 3)
                        if m0 is not None and m0 + 2 * j > 16:
                            split_mod(i, m0 + 2 * j)
                            split_mod(i, m0 + 2 * j + 1)
                        if j % 2 == 1:
                            hidden = 22 * fi + 2 * t_ + j // 2
                            dve.wait_ge(w_done, i * 12 + (c + j + 1))
                            dve.wait_ge(silu_done, i * 4 + (hidden + 1))
                            dve.wait_ge(hid_lo, i * 4 + hidden)
                            tt(sq[:, 1, c0:c0 + n], sq[:, 0, c0:c0 + n], tile(2, c0, n), ALU.mult).then_inc(hid_f, 1)
                            dve.wait_ge(hid_hi, i * 4 + (hidden + 1))
                            tt(hid[:, t_ % 2, j // 2, 1, c0:c0 + n], sq[:, 1, c0:c0 + n],
                               f(hid[:, t_ % 2, j // 2, 0, c0:c0 + n]), ALU.subtract).then_inc(hid_lo, 1)

                def add_tile(i, c, t_, idx):
                    d, (s0, w, _), place = tiles[idx]
                    if idx < nt - 1:
                        dve.wait_ge(down_done, i * 2 * (nt - 1) + (165 * fi + t_ * (nt - 1) + idx + 1))
                    else:
                        dve.wait_ge(w_done, i * 12 + (c + 2))
                    tt(y[:, d, s0:s0 + w], y[:, d, s0:s0 + w], place, ALU.add).then_inc(y_done, 1)

                def down(i, c, t_, m0):
                    split(i, 12, c + 3)
                    for idx in range(nt):
                        add_tile(i, c, t_, idx)
                        if m0 is not None and idx + 4 in MOD_TILES:
                            split_mod(i, m0 + MOD_TILES.index(idx + 4))
                    split(i, 12, c + 4)

                up(0, b, 0, 16 if q == 0 else None)
                if q == 0:
                    dve.wait_ge(y_done, 4)
                else:
                    dve.wait_ge(y_zero, fi)
                with dve.Fori(0, 5) as i:
                    for half in range(2):
                        m0 = 24 + 12 * half if q == 0 else None
                        up(i, b + 4 + 6 * half, 1 + half, m0)
                        down(i, b + 8 + 6 * half, half, m0 + 8 if q == 0 else None)
                if q != 5:
                    split(0, 12, b + 64 + 3)
                for idx in range(nt):
                    add_tile(0, b + 64, 10, idx)
                    d = (idx + 1) // len(segs) - 1
                    if (idx + 1) % len(segs) == 0 and d >= 1:
                        add_square(q, d - 1, segs)
                add_square(q, KD - 1, segs)
                if q != 5:
                    split(0, 12, b + 64 + 4)

            def conv(first, last):
                for n in range(first, min(last, 2 * (CONV_K + 1))):
                    c, k = n // (CONV_K + 1), n % (CONV_K + 1)
                    src = u[:, c, k % CONV_K:k % CONV_K + GAPPED]
                    tap = vecs[:, V_CONVW + k * KC + c:V_CONVW + k * KC + c + 1]
                    if n:
                        dve.wait_ge(sem("e_conv_a"), n)
                    if k == 0:
                        ins = nc.vector.tensor_scalar(conv_sum[:, :], src, tap, None, ALU.mult)
                    elif k < CONV_K:
                        ins = stt(conv_sum[:, :], src, tap, conv_sum[:, :], ALU.mult, ALU.add)
                    else:
                        ins = nc.vector.tensor_scalar(u[:, c, 0:GAPPED], conv_sum[:, :],
                                                      vecs[:, V_CONVB + c:V_CONVB + c + 1], None, ALU.add)
                    ins.then_inc(sem("e_conv_a"), 1)

            def rope(rows, q_ap, rot, tab, tmp, step, count, done):
                tt(tmp, rot, tab[rows, 1, :], ALU.mult).then_inc(step, 1)
                tt(q_ap, q_ap, tab[rows, 0, :], ALU.mult).then_inc(step, 1)
                dve.wait_ge(step, count + 2)
                tt(q_ap, q_ap, tmp, ALU.add).then_inc(done, 1)

            def even_pair(i, e):
                b = BASE[1] + E_PAIR
                pair = lambda per, c: i * (2 * per) + (e * per + c)
                r = slice(NOPE, QK)
                at = dve.snap(i * 4 * VD + 2 * e * VD)
                dve.wait_ge(sem("e_vh_hi"), pair(1, 1))
                tt(e_vh[:, :, 1, :], v_all[:, :, bass.ds(at, 2 * VD)], f(e_vh[:, :, 0, :]), ALU.subtract).then_inc(sem("e_vh_lo"), 1)

                def lo(hh):
                    dve.wait_ge(sem("e_q_hi"), pair(2, hh + 1))
                    tt(q_h[0:QK, hh, 1, :], q_f[0:QK, hh, :], f(q_h[0:QK, hh, 0, :]), ALU.subtract).then_inc(sem("e_q_lo"), 1)

                for hh in range(2):
                    dve.wait_ge(sem("e_rot"), pair(2, hh + 1))
                    rope(r, q_f[r, hh, CTX:TOK], tile(2 * hh, CTX, SEQ, NOPE, QK), e_rope, sq[r, hh, CTX:TOK],
                         sem("e_qrs"), pair(4, 2 * hh), sem("e_qr"))
                    dve.wait_ge(sem("e_k_hi"), pair(2, hh + 1))
                    tt(k_h[0:NOPE, hh, 1, :], tile(4, 0, TOK, hh * NOPE, (hh + 1) * NOPE), f(k_h[0:NOPE, hh, 0, :]),
                       ALU.subtract).then_inc(sem("e_k_lo"), 1)
                    if hh == 0:
                        lo(0)
                attention(EVEN, i, e, pair, lambda n: split(i, 4, b + 2 * e + n), lambda: lo(1))

            def attention(mx, i, e, pair, ahead=None, late=None):
                at = dve.snap(i * 2 + (mx.out_at + e))
                for s_ in range(mx.n_t + 5):
                    if ahead and s_ == mx.n_t + 3:
                        ahead(3)
                    if s_ < mx.n_t:
                        a, keys = s_, mx.tiles[s_][2] * P
                        dve.wait_ge(mx.sem("s"), pair(mx.n_t, a + 1))
                    if s_ >= 4 and s_ % 2 == 0 and s_ // 2 - 2 < mx.n_g:
                        g = s_ // 2 - 2
                        dve.wait_ge(mx.sem("inv"), pair(mx.n_g, g + 1))
                        copy(sq[0:VD, g % 2, 2 * P:4 * P], inv_place).then_inc(mx.sem("inv_out"), 1)
                    if s_ < mx.n_t:
                        nc.vector.tensor_reduce(small[:, a % 2:a % 2 + 1], tile(2 * (a % 2), 0, keys), AX_X, ALU.max,
                                                negate=True).then_inc(mx.sem("nm"), 1)
                    if 0 <= s_ - 2 < mx.n_t:
                        a = s_ - 2
                        for n in mx.of_tile(a):
                            _, k0, kn = mx.halves[n]
                            dst = mx.pt[:, a // 2 % 2, k0:k0 + kn, :, a % 2 * P:(a % 2 + 1) * P]
                            dve.wait_ge(mx.sem("pt_hi"), pair(mx.n_h, n + 1))
                            tt(dst[:, :, 1, :], turned(n, kn).rearrange("p (k q) -> p k q", q=P), f(dst[:, :, 0, :]),
                               ALU.subtract).then_inc(mx.sem("pt_lo"), 1)
                    if 2 <= s_ <= mx.n_t and s_ % 2 == 0:
                        g = s_ // 2 - 1
                        r = slice(6 + g % 2 * 2, 8 + g % 2 * 2)
                        dve.wait_ge(mx.sem("exp"), pair(mx.n_t, s_))
                        nc.vector.reciprocal(small[:, r], small[:, 2 + g % 2 * 2:4 + g % 2 * 2]).then_inc(mx.sem("ri"), 1)
                        if g >= 1:
                            dve.wait_ge(mx.sem("inv"), pair(mx.n_g, g))
                        dve.wait_ge(mx.sem("ri"), pair(mx.n_g, g + 1))
                        for j in range(2):
                            ins = nc.vector.tensor_scalar(mx.diag[:, j, :], idm, small[:, r.start + j:r.start + j + 1],
                                                          None, ALU.mult)
                        ins.then_inc(mx.sem("dg"), 1)
                    if late and s_ == 1:
                        late()
                    if s_ >= 5 and s_ % 2 == 1:
                        g = (s_ - 5) // 2
                        r = slice(mx.groups[g][0] * VD, (mx.groups[g][0] + 1) * VD)
                        dve.wait_ge(mx.sem("pv"), pair(mx.n_g, g + 1))
                        if g >= 2:
                            dve.wait_ge(mx.sem("lo"), pair(mx.n_g, g - 1))
                        dve.wait_ge(mx.sem("inv_out"), pair(mx.n_g, g + 1))
                        stt(sq[r, g % 2, 0:2 * P], pv_place, -2.0 * D, sq[0:VD, g % 2, 2 * P:4 * P], ALU.mult, ALU.mult).then_inc(mx.sem("of"), 1)
                    if s_ >= 6 and s_ % 2 == 0:
                        g = (s_ - 6) // 2
                        hh, col, _ = mx.groups[g]
                        r = slice(hh * VD, (hh + 1) * VD)
                        dve.wait_ge(mx.sem("hi"), pair(mx.n_g, g + 1))
                        hi, lo = (h[r, bass.ds(at, 1), a, col:col + 2 * P].rearrange("p a c -> p (a c)") for a in range(2))
                        tt(lo, sq[r, g % 2, 0:2 * P], f(hi), ALU.subtract).then_inc(mx.sem("lo"), 1)
                if ahead:
                    ahead(4)

            def even_mixer():
                b = BASE[1]
                dve.wait_ge(x_aside, 16)
                dve.wait_ge(sem("e_zero"), 3)
                for c in range(8):
                    split(0, 4, b + c + 3)
                    if c % 2 == 1:
                        dve.wait_ge(w_done, b + c + 1)
                        dve.wait_ge(sem("e_sig"), c // 2 + 1)
                        for c0, n, _ in ALL:
                            g0 = c0 + HALO + (HALO if c0 else 0)
                            ins = tt(u[:, c // 2, g0:g0 + n], tile(2, c0, n), sq[:, 0, c0:c0 + n], ALU.mult)
                        ins.then_inc(sem("e_u"), 1)
                    if c >= 2:
                        if c == 2:
                            dve.wait_ge(sem("e_u"), 1)
                        conv(4 * (c - 2), 4 * (c - 1))
                dve.wait_ge(sem("e_u"), 4)
                for m in range(6):
                    split(0, 4, b + 8 + m + 3)
                    conv(24 + 7 * m, 31 + 7 * m)
                dve.wait_ge(sem("e_consts"), 32)
                dve.wait_ge(sem("e_krot"), 1)
                r = slice(NOPE, QK)
                rope(r, q_f[r, 0, CTX:TOK], tile(0, CTX, SEQ, NOPE, QK), e_rope, rstd_e[r, 0:SEQ], sem("e_krs"), 0, sem("e_kr"))
                for number, place, ms, done in ((N_CKV, 6, LATENTS[:2], 2), (N_CQ, 4, LATENTS[2:], 5)):
                    norm(number, tile(place), prob[:, 0, :], prob[:, 1, :], rstd_e[:, :])
                    for m in ms:
                        gain = vecs[:, V_GCQ + m:V_GCQ + m + 1] if m < KQ else vecs[:, V_GCKV + m - KQ:V_GCKV + m - KQ + 1]
                        stt(cqkv[:, m, :], cqkv[:, m, :], gain, rstd_e[:, :], ALU.mult, ALU.mult).then_inc(sem("e_ct"), 1)
                    for n_, m in enumerate(ms):
                        dve.wait_ge(sem("e_cn_hi"), done - len(ms) + n_ + 1)
                        tt(cn[:, m, 1, :], cqkv[:, m, :], f(cn[:, m, 0, :]), ALU.subtract).then_inc(sem("e_cn_lo"), 1)
                for hh in range(2):
                    dve.wait_ge(sem("e_kpe_hi"), hh + 1)
                    tt(k_h[r, hh, 1, :], q_f[r, 0, :], f(k_h[r, hh, 0, :]), ALU.subtract).then_inc(sem("e_kpe_lo"), 1)
                split(0, 4, b + E_V + 3)
                split(0, 4, b + E_V + 4)
                with dve.Fori(0, 2) as i:
                    for e in range(2):
                        even_pair(i, e)
                for c in range(KC):
                    if c == 0:
                        dve.wait_ge(sem("e_lsum"), KC)
                    for c0, n, _ in ALL:
                        g0 = c0 + HALO if c0 else 0
                        ins = tt(u[:, c, g0:g0 + n], u[:, c, g0:g0 + n], tile(0, c0, n), ALU.add)
                    ins.then_inc(sem("e_d"), 1)
                norm(N_LN, tile(2), prob[:, 0, :], prob[:, 1, :], rstd_e[:, :])
                for c in range(KC + 1):
                    if c < KC:
                        if c >= 2:
                            dve.wait_ge(sem("e_ln_lo"), c - 1)
                        for c0, n, _ in ALL:
                            g0 = c0 + HALO if c0 else 0
                            ins = tt(sq[:, c % 2, c0:c0 + n], u[:, c, g0:g0 + n], rstd_e[:, c0:c0 + n], ALU.mult)
                        ins.then_inc(sem("e_lt"), 1)
                    if c >= 1:
                        dve.wait_ge(sem("e_ln_hi"), c)
                        tt(h[:, c - 1, 1, :], sq[:, (c - 1) % 2, :], f(h[:, c - 1, 0, :]), ALU.subtract).then_inc(sem("e_ln_lo"), 1)
                out_tiles(1, b + E_OUT, ALL)
                dve.wait_ge(x_back, 16)

            def out_tiles(q, b, segs):
                c0, n = places(segs)
                for c in range(KD):
                    split(0, 4, b + c + 3)
                    dve.wait_ge(w_done, b + c + 1)
                    copy(y[:, c, c0:c0 + n], tile(2 * (c % 2), c0, n)).then_inc(y_done, 1)
                    if c >= 1:
                        add_square(q, c - 1, segs)
                add_square(q, KD - 1, segs)

            def odd_mixer():
                b = BASE[4]
                dve.wait_ge(x_aside, 32)
                for m in range(10):
                    split(0, 4, b + m + 3)
                    if m == 4:
                        dve.wait_ge(sem("o_dft_hi"), 1)
                        tt(dft_c[:, 1, :], o_mats[:, 2:4, :].rearrange("p a c -> p (a c)"), f(dft_c[:, 0, :]), ALU.subtract).then_inc(sem("o_dftc"), 1)
                    if m >= 5:
                        if m >= 6:
                            head_rope(m - 6)
                        head_gain(m - 5)
                split(0, 4, b + O_DFT + 3)

                def group_lo(g):
                    dve.wait_ge(sem("o_f_hi"), g + 1)
                    tt(f_h[:, g % 2, 1, :], f4[:, g, :], f(f_h[:, g % 2, 0, :]), ALU.subtract).then_inc(sem("o_f_lo"), 1)

                group_lo(0)
                for g in range(4):
                    for j in range(4):
                        dve.wait_ge(sem("o_ab_hi"), 4 * g + j + 1)
                        tt(ab[:, j, 1, :], bank_(2 * (j % 2), 2 * P), f(ab[:, j, 0, :]), ALU.subtract).then_inc(sem("o_ab_lo"), 1)
                    if g < 3:
                        group_lo(g + 1)
                    if g == 1:
                        head_rope(4)
                    if g == 3:
                        for n in range(GQA_KV):
                            r = slice(n * HD, (n + 1) * HD)
                            dve.wait_ge(sem("o_k_hi"), n + 1)
                            tt(k_dup[r, n, 1, :], kv_f[r, 0, :], f(k_dup[r, n, 0, :]), ALU.subtract).then_inc(sem("o_k_lo"), 1)
                        dve.wait_ge(sem("o_k_lo"), 2)
                        for n in range(GQA_KV):
                            r, other = slice(n * HD, (n + 1) * HD), slice((1 - n) * HD, (2 - n) * HD)
                            for a in range(2):
                                copy(k_dup[other, n, a, :], f(k_dup[r, n, a, :])).then_inc(sem("o_kd"), 1)
                    dve.wait_ge(sem("o_fn_hi"), g + 1)
                    tt(h[:, 4 + g, 1, CTX:TOK], bank_(4), f(h[:, 4 + g, 0, CTX:TOK]), ALU.subtract).then_inc(sem("o_fn_lo"), 1)
                with dve.Fori(0, 2) as i:
                    at = dve.snap(i * HD)
                    dve.wait_ge(sem("o_vh_hi"), i + 1)
                    tt(o_vh[:, :, 1, :], v_t[:, :, bass.ds(at, HD)], f(o_vh[:, :, 0, :]), ALU.subtract).then_inc(sem("o_vh_lo"), 1)
                    for e in range(2):
                        odd_pair(i, e)
                for c in range(1, 4):
                    split(0, 4, b + O_DFT + c + 3)
                out_tiles(4, b + O_OUT, XONLY)
                dve.wait_ge(x_back, 32)

            def head_gain(m):
                n = SEQ if m < 4 else TOK
                norm(N_Q + m, tile(6, TOK - n, n), o_prob[:, 0, TOK - n:TOK], o_prob[:, 1, TOK - n:TOK], rstd_o[:, TOK - n:TOK])
                x_ = q4[:, m, :] if m < 4 else kv_f[:, 0, :]
                g = V_GQN if m < 4 else V_GKN
                stt(x_, x_, vecs[:, g:g + 1], rstd_o[:, TOK - n:TOK], ALU.mult, ALU.mult).then_inc(sem("o_qn"), 1)

            def head_rope(m):
                dve.wait_ge(sem("o_rot"), m + 1)
                x_ = q4[:, m, :] if m < 4 else kv_f[:, 0, CTX:TOK]
                rope(slice(0, P), x_, bank_(5), o_rope, sum_sq[:, 0:SEQ], sem("o_rps"), 2 * m, sem("o_rp"))

            def odd_pair(i, e):
                pair = lambda per, c: i * (2 * per) + (e * per + c)
                at = dve.snap(i * 2 + e)
                for hh in range(2):
                    r = slice(hh * HD, (hh + 1) * HD)
                    dve.wait_ge(sem("o_qz_hi"), pair(2, hh + 1))
                    stt(qz[r, hh, 1, :], q4[r, bass.ds(at, 1), :].rearrange("p a c -> p (a c)"), GQA_SCALE, f(qz[r, hh, 0, :]),
                        ALU.mult, ALU.subtract).then_inc(sem("o_qz_lo"), 1)
                attention(ODD, i, e, pair)

            dve.wait_ge(vec_t, 1)
            copy(vecs[:, :], bank_(0)[:, 0:2 * P]).then_inc(vecs_ready, 1)
            dve.wait_ge(cond_hi, 1)
            tt(cond[:, :, :, 1].rearrange("p k j -> p j k"), cond_f[:, :, :],
               f(cond[:, :, :, 0]).rearrange("p k j -> p j k"), ALU.subtract).then_inc(cond_ready, 1)
            for c in range(8):
                split_mod(0, c)
            for k in range(KD):
                dve.wait_ge(tok_t, k + 1)
                copy(x[:, k, :], tile(2 * (k % 2))).then_inc(x_new, 1)
            for c in range(8, 16):
                if c % 2 == 0:
                    k = c // 2 - 4
                    nc.vector.memset(y[:, 2 * k:2 * k + 2, :], 0.0).then_inc(y_done, 1)
                split_mod(0, c)
            for c in range(3):
                split(0, 4, c)
            for c in (16, 17):
                split_mod(0, c)
            columns(1, 16, 1)
            pre(0, ALL)
            ffn(0, ALL)
            columns(2, 72, 2)
            post(0, ALL)
            pre(1, ALL)
            even_mixer()
            post(1, ALL)
            pre(2, ALL)
            ffn(2, ALL)
            post(2, ALL)
            pre(3, ALL)
            ffn(3, ALL)
            post(3, ALL)
            pre(4, ALL)
            odd_mixer()
            post(4, XONLY)
            pre(5, XONLY)
            ffn(5, XONLY)
            post(5, XONLY)
            for j in range(4):
                dve.wait_ge(sem("out_t"), j + 1)
                copy(tok_in[:, j, :], ps[:, (2 + 2 * (j % 2)) * 512:(4 + 2 * (j % 2)) * 512]).then_inc(sem("out_ready"), 1)


_INS = ['x', 'c', 'ctx', 'c_ctx', 'w_mod', 'b_mod', 'g_pre', 'g_post', 'ffn_w_gate', 'ffn_w_up', 'ffn_w_down',
        'ev_w_in', 'ev_conv_w', 'ev_conv_b', 'ev_ln_g', 'ev_ln_b', 'ev_g_cq', 'ev_w_uq', 'ev_g_ckv', 'ev_w_ukv',
        'ev_w_out', 'od_w_in', 'od_g_qn', 'od_g_kn', 'od_w_out']


def kernel(**inputs):
    import numpy as _np
    import concourse.bacc as _bacc
    from concourse import mybir as _mybir
    from concourse.bass_utils import run_bass_kernel_spmd as _run

    nc = _bacc.Bacc("TRN2", target_bir_lowering=False, num_devices=1)
    arrays, args = {}, []
    given = {name: _np.ascontiguousarray(inputs[name]) for name in _INS}
    given["consts"], given["dft"] = constant_array(), dft_array()
    for name, a in given.items():
        arrays[f"in_{name}_dram"] = a
        args.append(nc.dram_tensor(f"in_{name}_dram", a.shape, _mybir.dt.from_np(a.dtype), kind="ExternalInput").ap())
    args.append(nc.dram_tensor("out_dram", (1, SEQ, D), _mybir.dt.float32, kind="ExternalOutput").ap())
    trunk(nc, *args)
    r = _run(nc, [arrays], core_ids=[0])
    return r.results[0]["out_dram"]
```
